# Optimizing a Trainium2 kernel written in Bass

```python
import math
import jax, jax.numpy as jnp
from jax import lax
import numpy as np

D_MODEL = 1024
BATCH = 1
SEQ = 512
DEPTH = 2

CHUNK = 64
Q_BLOCK = 128
RMS_EPS = 1e-6
ROPE_THETA = 500000.0
MLA_ROPE_THETA = 10000.0
MACARON_WEIGHT = 0.5
N_MOD = 9
D_FF = 2816

FOX_HEADS = 8
FOX_HD = 64
FOX_GATE_BIAS = 3.0
DSA_HEADS = 8
DSA_HD = 64
DSA_ROT = DSA_HD // 4
IDX_HEADS = 4
IDX_HD = 64
IDX_ROT = IDX_HD // 4
DSA_TOPK_MAX = 256
MLA_HEADS = 8
MLA_NOPE = 128
MLA_ROPE = 64
MLA_V = 128
MLA_Q_LORA = 384
MLA_KV_LORA = 256
MLA_DOWN = MLA_Q_LORA + MLA_KV_LORA + MLA_ROPE

HYB_SIZES = (FOX_HEADS * FOX_HD, FOX_HEADS * FOX_HD, FOX_HEADS * FOX_HD, FOX_HEADS,
             DSA_HEADS * DSA_HD, DSA_HEADS * DSA_HD, DSA_HEADS * DSA_HD,
             IDX_HEADS * IDX_HD, IDX_HEADS, IDX_HD)
HYB_IN = sum(HYB_SIZES)
HYB_OUT = FOX_HEADS * FOX_HD + DSA_HEADS * DSA_HD
N_EVEN = (DEPTH + 1) // 2
N_ODD = DEPTH // 2


def _rmsnorm(x, g):
    x32 = x.astype(jnp.float32)
    y = x32 * lax.rsqrt(jnp.mean(x32 * x32, axis=-1, keepdims=True) + RMS_EPS)
    return (y * g.astype(jnp.float32)).astype(x.dtype)

def _rope(x, pos, rot_dim, theta):
    half = rot_dim // 2
    inv_freq = jnp.exp(-math.log(theta) * 2.0 * jnp.arange(half, dtype=jnp.float32) / rot_dim)
    ang = pos.astype(jnp.float32)[:, :, None, None] * inv_freq
    cos, sin = jnp.cos(ang), jnp.sin(ang)
    xr = x[..., :rot_dim].astype(jnp.float32)
    x1, x2 = xr[..., :half], xr[..., half:]
    rot = jnp.concatenate([x1 * cos - x2 * sin, x2 * cos + x1 * sin], axis=-1).astype(x.dtype)
    return jnp.concatenate([rot, x[..., rot_dim:]], axis=-1)

def _sweep_query_blocks(fn, *q_args):
    b, s = q_args[0].shape[:2]
    nblk = s // Q_BLOCK
    blocked = tuple(jnp.moveaxis(a.reshape(b, nblk, Q_BLOCK, *a.shape[2:]), 1, 0) for a in q_args)
    out = lax.map(lambda xs: fn(xs[0] * Q_BLOCK + jnp.arange(Q_BLOCK, dtype=jnp.int32), *xs[1:]),
                  (jnp.arange(nblk, dtype=jnp.int32),) + blocked)
    out = jnp.moveaxis(out, 0, 1)
    return out.reshape(b, s, *out.shape[3:])

def _fox_attention(q, k, v, log_f):
    s = k.shape[1]
    cum = jnp.moveaxis(jnp.cumsum(log_f, axis=1), 1, 2)
    s_idx = jnp.arange(s, dtype=jnp.int32)
    scale = q.shape[-1] ** -0.5

    def block(t_idx, qb, cum_q):
        logits = jnp.einsum('bqhd,bshd->bhqs', qb, k, preferred_element_type=jnp.float32) * scale
        logits = logits + (jnp.moveaxis(cum_q, 1, 2)[..., :, None] - cum[..., None, :])
        mask = s_idx[None, :] <= t_idx[:, None]
        logits = jnp.where(mask, logits, -jnp.inf)
        p = jax.nn.softmax(logits, axis=-1).astype(v.dtype)
        return jnp.einsum('bhqs,bshd->bqhd', p, v)

    return _sweep_query_blocks(block, q, jnp.moveaxis(cum, 1, 2))

def _dsa_attention(q, k, v, iq, iw, ik):
    s = k.shape[1]
    top_k = min(DSA_TOPK_MAX, s // 4)
    s_chunk = jnp.arange(s, dtype=jnp.int32) // CHUNK
    scale = q.shape[-1] ** -0.5
    idx_scale = iq.shape[-1] ** -0.5
    gather = jax.vmap(lambda table, ix: table[ix])

    def block(t_idx, qb, iqb, iwb):
        dots = jnp.einsum('bqhd,bsd->bqhs', iqb, ik, preferred_element_type=jnp.float32) * idx_scale
        score = jnp.einsum('bqhs,bqh->bqs', jax.nn.relu(dots), iwb.astype(jnp.float32))
        admissible = s_chunk[None, :] <= (t_idx // CHUNK)[:, None]
        score = jnp.where(admissible[None], score, -jnp.inf)
        sel_score, sel = lax.top_k(score, top_k)
        kg = gather(k, sel)
        vg = gather(v, sel)
        logits = jnp.einsum('bqhd,bqkhd->bhqk', qb, kg, preferred_element_type=jnp.float32) * scale
        valid = jnp.isfinite(sel_score)[:, None]
        logits = jnp.where(valid, logits, -jnp.inf)
        p = jax.nn.softmax(logits, axis=-1).astype(v.dtype)
        return jnp.einsum('bhqk,bqkhd->bqhd', p, vg)

    return _sweep_query_blocks(block, q, iq, iw)

def _mla_attention(q_nope, q_rope, k_nope, k_rope, v):
    s = k_nope.shape[1]
    s_chunk = jnp.arange(s, dtype=jnp.int32) // CHUNK
    scale = (q_nope.shape[-1] + q_rope.shape[-1]) ** -0.5

    def block(t_idx, qn, qr):
        logits = (jnp.einsum('bqhd,bshd->bhqs', qn, k_nope, preferred_element_type=jnp.float32)
                  + jnp.einsum('bqhr,bsr->bhqs', qr, k_rope, preferred_element_type=jnp.float32)) * scale
        mask = s_chunk[None, :] <= (t_idx // CHUNK)[:, None]
        logits = jnp.where(mask, logits, -jnp.inf)
        p = jax.nn.softmax(logits, axis=-1).astype(v.dtype)
        return jnp.einsum('bhqs,bshd->bqhd', p, v)

    return _sweep_query_blocks(block, q_nope, q_rope)

def _hybrid_mixer(u, positions, w_in, b_f, w_out):
    b, s, _ = u.shape
    offsets = np.cumsum(HYB_SIZES)[:-1].tolist()
    fq, fk, fv, ff, dq, dk, dv, iq, iw, ik = jnp.split(u @ w_in, offsets, axis=-1)
    log_f = jax.nn.log_sigmoid((ff + b_f).astype(jnp.float32))
    out_a = _fox_attention(fq.reshape(b, s, FOX_HEADS, FOX_HD), fk.reshape(b, s, FOX_HEADS, FOX_HD),
                           fv.reshape(b, s, FOX_HEADS, FOX_HD), log_f)
    dq = _rope(dq.reshape(b, s, DSA_HEADS, DSA_HD), positions, DSA_ROT, ROPE_THETA)
    dk = _rope(dk.reshape(b, s, DSA_HEADS, DSA_HD), positions, DSA_ROT, ROPE_THETA)
    iq = _rope(iq.reshape(b, s, IDX_HEADS, IDX_HD), positions, IDX_ROT, ROPE_THETA)
    ik = _rope(ik[:, :, None, :], positions, IDX_ROT, ROPE_THETA)[:, :, 0, :]
    iw = iw * IDX_HEADS ** -0.5
    out_b = _dsa_attention(dq, dk, dv.reshape(b, s, DSA_HEADS, DSA_HD), iq, iw, ik)
    mixed = jnp.concatenate([out_a.reshape(b, s, -1), out_b.reshape(b, s, -1)], axis=-1)
    return mixed @ w_out

def _mla_mixer(u, positions, w_down, q_norm, kv_norm, w_uq, w_ukv, w_out):
    b, s, _ = u.shape
    cq, ckv, k_rope = jnp.split(u @ w_down, [MLA_Q_LORA, MLA_Q_LORA + MLA_KV_LORA], axis=-1)
    q = (_rmsnorm(cq, q_norm) @ w_uq).reshape(b, s, MLA_HEADS, MLA_NOPE + MLA_ROPE)
    kv = (_rmsnorm(ckv, kv_norm) @ w_ukv).reshape(b, s, MLA_HEADS, MLA_NOPE + MLA_V)
    q_nope = q[..., :MLA_NOPE]
    q_rope = _rope(q[..., MLA_NOPE:], positions, MLA_ROPE, MLA_ROPE_THETA)
    k_nope, v = kv[..., :MLA_NOPE], kv[..., MLA_NOPE:]
    k_rope = _rope(k_rope[:, :, None, :], positions, MLA_ROPE, MLA_ROPE_THETA)[:, :, 0, :]
    out = _mla_attention(q_nope, q_rope, k_nope, k_rope, v)
    return out.reshape(b, s, -1) @ w_out

def _swiglu(u, w_gate, w_up, w_down):
    return (jax.nn.silu(u @ w_gate) * (u @ w_up)) @ w_down

def first_inputs(seed: int = 0) -> dict:
    key = jax.random.key(seed)
    ks = jax.random.split(key, 20)
    f32 = jnp.float32

    def nrm(k, shape, fan_in):
        return jax.random.normal(k, shape, f32) * fan_in ** -0.5

    x = jax.random.normal(ks[0], (BATCH, SEQ, D_MODEL), f32)
    c = jax.random.normal(ks[1], (BATCH, D_MODEL), f32)
    start = jax.random.randint(ks[2], (BATCH, 1), 0, 4096, dtype=jnp.int32)
    positions = start + jnp.arange(SEQ, dtype=jnp.int32)[None, :]
    ada_w = 0.5 * nrm(ks[3], (DEPTH, D_MODEL, N_MOD * D_MODEL), D_MODEL)
    ada_b = 0.02 * jax.random.normal(ks[4], (DEPTH, N_MOD * D_MODEL), f32)
    norm_g = 1.0 + 0.02 * jax.random.normal(ks[5], (DEPTH, 3, D_MODEL), f32)
    ffn_w_gate = nrm(ks[6], (DEPTH, 2, D_MODEL, D_FF), D_MODEL)
    ffn_w_up = nrm(ks[7], (DEPTH, 2, D_MODEL, D_FF), D_MODEL)
    ffn_w_down = nrm(ks[8], (DEPTH, 2, D_FF, D_MODEL), D_FF)
    hyb_w_in = nrm(ks[9], (N_EVEN, D_MODEL, HYB_IN), D_MODEL)
    fox_b_f = FOX_GATE_BIAS + 0.5 * jax.random.normal(ks[10], (N_EVEN, FOX_HEADS), f32)
    hyb_w_out = nrm(ks[11], (N_EVEN, HYB_OUT, D_MODEL), HYB_OUT)
    mla_w_down = nrm(ks[12], (N_ODD, D_MODEL, MLA_DOWN), D_MODEL)
    mla_q_norm = 1.0 + 0.02 * jax.random.normal(ks[13], (N_ODD, MLA_Q_LORA), f32)
    mla_kv_norm = 1.0 + 0.02 * jax.random.normal(ks[14], (N_ODD, MLA_KV_LORA), f32)
    mla_w_uq = nrm(ks[15], (N_ODD, MLA_Q_LORA, MLA_HEADS * (MLA_NOPE + MLA_ROPE)), MLA_Q_LORA)
    mla_w_ukv = nrm(ks[16], (N_ODD, MLA_KV_LORA, MLA_HEADS * (MLA_NOPE + MLA_V)), MLA_KV_LORA)
    mla_w_out = nrm(ks[17], (N_ODD, MLA_HEADS * MLA_V, D_MODEL), MLA_HEADS * MLA_V)
    final_g = 1.0 + 0.02 * jax.random.normal(ks[18], (D_MODEL,), f32)
    return {'x': x, 'c': c, 'positions': positions, 'ada_w': ada_w, 'ada_b': ada_b,
            'norm_g': norm_g, 'ffn_w_gate': ffn_w_gate, 'ffn_w_up': ffn_w_up,
            'ffn_w_down': ffn_w_down, 'hyb_w_in': hyb_w_in, 'fox_b_f': fox_b_f,
            'hyb_w_out': hyb_w_out, 'mla_w_down': mla_w_down, 'mla_q_norm': mla_q_norm,
            'mla_kv_norm': mla_kv_norm, 'mla_w_uq': mla_w_uq, 'mla_w_ukv': mla_w_ukv,
            'mla_w_out': mla_w_out, 'final_g': final_g}

def first_block(x, c, positions, ada_w, ada_b, norm_g, ffn_w_gate, ffn_w_up, ffn_w_down,
              hyb_w_in, fox_b_f, hyb_w_out, mla_w_down, mla_q_norm, mla_kv_norm,
              mla_w_uq, mla_w_ukv, mla_w_out, final_g):
    h = x
    cond = jax.nn.silu(c)
    for i in range(DEPTH):
        mod = (cond @ ada_w[i] + ada_b[i]).reshape(c.shape[0], N_MOD, D_MODEL)[:, :, None, :]
        sh1, sc1, g1, sh2, sc2, g2, sh3, sc3, g3 = [mod[:, j] for j in range(N_MOD)]
        u = _rmsnorm(h, norm_g[i, 0]) * (1 + sc1) + sh1
        h = h + MACARON_WEIGHT * g1 * _swiglu(u, ffn_w_gate[i, 0], ffn_w_up[i, 0], ffn_w_down[i, 0])
        u = _rmsnorm(h, norm_g[i, 1]) * (1 + sc2) + sh2
        j = i // 2
        if i % 2 == 0:
            mix = _hybrid_mixer(u, positions, hyb_w_in[j], fox_b_f[j], hyb_w_out[j])
        else:
            mix = _mla_mixer(u, positions, mla_w_down[j], mla_q_norm[j], mla_kv_norm[j],
                             mla_w_uq[j], mla_w_ukv[j], mla_w_out[j])
        h = h + g2 * mix
        u = _rmsnorm(h, norm_g[i, 2]) * (1 + sc3) + sh3
        h = h + MACARON_WEIGHT * g3 * _swiglu(u, ffn_w_gate[i, 1], ffn_w_up[i, 1], ffn_w_down[i, 1])
    return _rmsnorm(h, final_g)


DEPTH_2 = 1

ATTN_GROUPS = ((128, 1), (512, 4), (2048, 16))
N_ATTN_GROUPS = len(ATTN_GROUPS)
HEADS_PER_GROUP = 6
ATTN_HEADS = N_ATTN_GROUPS * HEADS_PER_GROUP
HEAD_DIM = 64
ATTN_WIDTH = ATTN_HEADS * HEAD_DIM
ATTN_OUT_WIDTH = HEADS_PER_GROUP * HEAD_DIM
REL_BUCKETS = 32
REL_MAX_DISTANCE = 2048
POOL_WINDOWS = (2, 4, 8, 16)
POOL_WIDTH = D_MODEL
POOL_GROUP = POOL_WIDTH // len(POOL_WINDOWS)
SSD_INNER = D_MODEL
SSD_HEAD_DIM = 64
SSD_HEADS = SSD_INNER // SSD_HEAD_DIM
SSD_GROUPS = 2
SSD_STATE = 128
SSD_CONV = 4
SSD_CHUNK = 128
SSD_XBC = SSD_INNER + 2 * SSD_GROUPS * SSD_STATE
FFN_CONV = 3
N_BRANCH = 3
NORM_EPS = 1e-6
IN_SPLIT_SIZES = (ATTN_WIDTH, ATTN_WIDTH, ATTN_WIDTH, POOL_WIDTH, SSD_INNER, SSD_XBC, SSD_HEADS, N_BRANCH * D_MODEL)
IN_WIDTH = sum(IN_SPLIT_SIZES)


def rmsnorm(x, g):
    xf = x.astype(jnp.float32)
    y = xf * lax.rsqrt(jnp.mean(xf * xf, axis=-1, keepdims=True) + NORM_EPS)
    return (y * g.astype(jnp.float32)).astype(x.dtype)

def causal_dwconv(x, w, b):
    K = w.shape[0]
    s = x.shape[1]
    xp = jnp.pad(x, ((0, 0), (K - 1, 0), (0, 0)))
    y = xp[:, 0:s] * w[0]
    for k in range(1, K):
        y = y + xp[:, k:k + s] * w[k]
    return y + b

def t5_bucket(dist):
    max_exact = REL_BUCKETS // 2
    is_small = dist < max_exact
    nf = jnp.maximum(dist, 1).astype(jnp.float32)
    large = max_exact + (jnp.log(nf / max_exact) / math.log(REL_MAX_DISTANCE / max_exact)
                         * (REL_BUCKETS - max_exact)).astype(jnp.int32)
    large = jnp.minimum(large, REL_BUCKETS - 1)
    return jnp.where(is_small, dist, large)

def dilated_group_attention(q, k, v, bias_table, dilation, steps):
    b, s, h, dh = q.shape
    L = s // dilation
    W = steps
    nb = -(-L // W)
    Lp = nb * W
    bd = b * dilation

    def to_res(t):
        return t.reshape(b, L, dilation, h, dh).transpose(0, 2, 3, 1, 4).reshape(bd, h, L, dh)

    qb = jnp.pad(to_res(q), ((0, 0), (0, 0), (0, Lp - L), (0, 0))).reshape(bd, h, nb, W, dh)
    kr = jnp.pad(to_res(k), ((0, 0), (0, 0), (W, Lp - L), (0, 0))).reshape(bd, h, nb + 1, W, dh)
    vr = jnp.pad(to_res(v), ((0, 0), (0, 0), (W, Lp - L), (0, 0))).reshape(bd, h, nb + 1, W, dh)
    kb = jnp.concatenate([kr[:, :, :-1], kr[:, :, 1:]], axis=3)
    vb = jnp.concatenate([vr[:, :, :-1], vr[:, :, 1:]], axis=3)

    qi = jnp.arange(W)[:, None]
    kk = jnp.arange(2 * W)[None, :]
    rel = qi + W - kk
    band = (rel >= 0) & (rel <= W)
    kabs = jnp.arange(nb)[:, None, None] * W + kk[None] - W
    valid = band[None] & (kabs >= 0)
    bucket = t5_bucket(jnp.clip(rel, 0, None) * dilation)
    bias = bias_table[bucket].transpose(2, 0, 1).astype(jnp.float32)

    scale = 1.0 / math.sqrt(dh)
    scores = jnp.einsum("bhnqd,bhnkd->bhnqk", qb, kb).astype(jnp.float32) * scale + bias[:, None]
    scores = jnp.where(valid[None, None], scores, -jnp.inf)
    m = jnp.max(scores, axis=-1, keepdims=True)
    p = jnp.exp(scores - m)
    l = jnp.sum(p, axis=-1)
    o = jnp.einsum("bhnqk,bhnkd->bhnqd", p, vb.astype(jnp.float32)) / l[..., None]
    lse = m[..., 0] + jnp.log(l)

    o = o.reshape(bd, h, Lp, dh)[:, :, :L].reshape(b, dilation, h, L, dh)
    o = o.transpose(0, 3, 1, 2, 4).reshape(b, s, h, dh)
    lse = lse.reshape(bd, h, Lp)[:, :, :L].reshape(b, dilation, h, L)
    lse = lse.transpose(0, 3, 1, 2).reshape(b, s, h)
    return o, lse

def dilated_attention_mixer(q, k, v, rel_bias):
    b, s = q.shape[:2]
    outs, lses = [], []
    for gi, (window, dilation) in enumerate(ATTN_GROUPS):
        hs = slice(gi * HEADS_PER_GROUP, (gi + 1) * HEADS_PER_GROUP)
        o, lse = dilated_group_attention(q[:, :, hs], k[:, :, hs], v[:, :, hs],
                                         rel_bias[:, hs], dilation, window // dilation)
        outs.append(o)
        lses.append(lse)
    o = jnp.stack(outs, axis=0)
    alpha = jax.nn.softmax(jnp.stack(lses, axis=0), axis=0)
    o = jnp.sum(alpha[..., None] * o, axis=0)
    return o.reshape(b, s, ATTN_OUT_WIDTH).astype(q.dtype)

def pool_mixer(u, w_grp, scale):
    b, s, _ = u.shape
    uf = u.astype(jnp.float32)
    cs = jnp.cumsum(uf, axis=1)
    pos = (jnp.arange(s) + 1)[None, :, None]
    outs = []
    for gi, w in enumerate(POOL_WINDOWS):
        sl = slice(gi * POOL_GROUP, (gi + 1) * POOL_GROUP)
        c = cs[..., sl]
        shifted = jnp.pad(c, ((0, 0), (w, 0), (0, 0)))[:, :s]
        cnt = jnp.minimum(pos, w).astype(jnp.float32)
        outs.append((c - shifted) / cnt - uf[..., sl])
    d = jnp.stack(outs, axis=2).astype(u.dtype)
    y = jnp.einsum("bsgc,gcd->bsgd", d, w_grp).reshape(b, s, POOL_WIDTH)
    return y * scale

def ssd_scan(x, dt, A, Bm, Cm):
    b, s, h, p = x.shape
    g, n = Bm.shape[2:]
    e = h // g
    l = SSD_CHUNK
    c = s // l
    xc = (x * dt[..., None]).reshape(b, c, l, g, e, p)
    a = (dt * A).reshape(b, c, l, h).transpose(0, 3, 1, 2)
    a_cs = jnp.cumsum(a, axis=-1)
    Bc = Bm.reshape(b, c, l, g, n)
    Cc = Cm.reshape(b, c, l, g, n)
    causal = jnp.tril(jnp.ones((l, l), dtype=bool))
    seg = a_cs[..., :, None] - a_cs[..., None, :]
    Lmat = jnp.exp(jnp.where(causal, seg, -jnp.inf)).reshape(b, g, e, c, l, l)
    cb = jnp.einsum("bclgn,bcsgn->bcgls", Cc, Bc)
    y_diag = jnp.einsum("bcgls,bgecls,bcsgep->bclgep", cb, Lmat, xc)
    decay = jnp.exp(a_cs[..., -1:] - a_cs).reshape(b, g, e, c, l)
    states = jnp.einsum("bclgn,bgecl,bclgep->bcgepn", Bc, decay, xc)
    chunk_decay = jnp.exp(a_cs[..., -1]).reshape(b, g, e, c)

    def step(carry, inp):
        st, dec = inp
        return carry * dec[..., None, None] + st, carry

    init = jnp.zeros((b, g, e, p, n), dtype=x.dtype)
    _, prev = lax.scan(step, init, (states.transpose(1, 0, 2, 3, 4, 5), chunk_decay.transpose(3, 0, 1, 2)))
    prev = prev.transpose(1, 0, 2, 3, 4, 5)
    out_decay = jnp.exp(a_cs).reshape(b, g, e, c, l)
    y_off = jnp.einsum("bclgn,bcgepn,bgecl->bclgep", Cc, prev, out_decay)
    return (y_diag + y_off).reshape(b, s, h, p)

def ssd_mixer(z, xbc, dt_raw, conv_w, conv_b, dt_bias, a_log, d_skip, norm_w):
    b, s, _ = z.shape
    xbc = jax.nn.silu(causal_dwconv(xbc, conv_w, conv_b))
    xs = xbc[..., :SSD_INNER].reshape(b, s, SSD_HEADS, SSD_HEAD_DIM).astype(jnp.float32)
    Bm = xbc[..., SSD_INNER:SSD_INNER + SSD_GROUPS * SSD_STATE].reshape(b, s, SSD_GROUPS, SSD_STATE).astype(jnp.float32)
    Cm = xbc[..., SSD_INNER + SSD_GROUPS * SSD_STATE:].reshape(b, s, SSD_GROUPS, SSD_STATE).astype(jnp.float32)
    dt = jax.nn.softplus(dt_raw.astype(jnp.float32) + dt_bias.astype(jnp.float32))
    A = -jnp.exp(a_log.astype(jnp.float32))
    y = ssd_scan(xs, dt, A, Bm, Cm) + d_skip.astype(jnp.float32)[:, None] * xs
    y = y.reshape(b, s, SSD_INNER) * jax.nn.silu(z.astype(jnp.float32))
    yg = y.reshape(b, s, SSD_GROUPS, SSD_INNER // SSD_GROUPS)
    yg = yg * lax.rsqrt(jnp.mean(yg * yg, axis=-1, keepdims=True) + NORM_EPS)
    y = yg.reshape(b, s, SSD_INNER) * norm_w.astype(jnp.float32)
    return y.astype(z.dtype)

def conv_ffn(u, w_up, conv_w, conv_b, w_down):
    h = causal_dwconv(u @ w_up, conv_w, conv_b)
    a, v = h[..., :D_FF], h[..., D_FF:]
    return (jax.nn.silu(a) * v) @ w_down

def second_inputs(seed: int = 0) -> dict:
    key = jax.random.key(seed)
    ks = jax.random.split(key, 24)
    f32 = jnp.float32

    def nrm(k, shape, scale):
        return jax.random.normal(k, shape, dtype=f32) * scale

    dt0 = jnp.exp(jax.random.uniform(ks[10], (DEPTH_2, SSD_HEADS), dtype=f32)
                  * (math.log(0.1) - math.log(0.001)) + math.log(0.001))
    return {
        "x": nrm(ks[0], (BATCH, SEQ, D_MODEL), 1.0),
        "rel_bias": nrm(ks[1], (REL_BUCKETS, ATTN_HEADS), 0.1),
        "ln1_g": 1.0 + nrm(ks[2], (DEPTH_2, D_MODEL), 0.02),
        "w_in": nrm(ks[3], (DEPTH_2, D_MODEL, IN_WIDTH), D_MODEL ** -0.5),
        "b_gate": nrm(ks[4], (DEPTH_2, N_BRANCH * D_MODEL), 0.02),
        "w_a": nrm(ks[5], (DEPTH_2, ATTN_OUT_WIDTH, D_MODEL), ATTN_OUT_WIDTH ** -0.5),
        "pool_w": nrm(ks[6], (DEPTH_2, len(POOL_WINDOWS), POOL_GROUP, POOL_GROUP), POOL_GROUP ** -0.5),
        "pool_scale": 1.0 + nrm(ks[7], (DEPTH_2, POOL_WIDTH), 0.1),
        "w_b": nrm(ks[8], (DEPTH_2, POOL_WIDTH, D_MODEL), POOL_WIDTH ** -0.5),
        "ssd_conv_w": nrm(ks[9], (DEPTH_2, SSD_CONV, SSD_XBC), SSD_CONV ** -0.5),
        "ssd_conv_b": nrm(ks[11], (DEPTH_2, SSD_XBC), 0.02),
        "ssd_dt_bias": dt0 + jnp.log(-jnp.expm1(-dt0)),
        "ssd_a_log": jnp.log(jax.random.uniform(ks[12], (DEPTH_2, SSD_HEADS), dtype=f32, minval=1.0, maxval=16.0)),
        "ssd_d": 1.0 + nrm(ks[13], (DEPTH_2, SSD_HEADS), 0.1),
        "ssd_norm_w": 1.0 + nrm(ks[14], (DEPTH_2, SSD_INNER), 0.02),
        "w_c": nrm(ks[15], (DEPTH_2, SSD_INNER, D_MODEL), SSD_INNER ** -0.5),
        "w_o": nrm(ks[16], (DEPTH_2, D_MODEL, D_MODEL), D_MODEL ** -0.5),
        "ln2_g": 1.0 + nrm(ks[17], (DEPTH_2, D_MODEL), 0.02),
        "ffn_w_up": nrm(ks[18], (DEPTH_2, D_MODEL, 2 * D_FF), D_MODEL ** -0.5),
        "ffn_conv_w": nrm(ks[19], (DEPTH_2, FFN_CONV, 2 * D_FF), FFN_CONV ** -0.5),
        "ffn_conv_b": nrm(ks[20], (DEPTH_2, 2 * D_FF), 0.02),
        "ffn_w_down": nrm(ks[21], (DEPTH_2, D_FF, D_MODEL), D_FF ** -0.5),
        "final_g": 1.0 + nrm(ks[22], (D_MODEL,), 0.02),
    }

def second_block(x, rel_bias, ln1_g, w_in, b_gate, w_a, pool_w, pool_scale, w_b,
              ssd_conv_w, ssd_conv_b, ssd_dt_bias, ssd_a_log, ssd_d, ssd_norm_w, w_c,
              w_o, ln2_g, ffn_w_up, ffn_conv_w, ffn_conv_b, ffn_w_down, final_g):
    b, s, _ = x.shape
    split_idx = []
    acc = 0
    for sz in IN_SPLIT_SIZES[:-1]:
        acc += sz
        split_idx.append(acc)
    for i in range(DEPTH_2):
        u = rmsnorm(x, ln1_g[i])
        proj = u @ w_in[i]
        q, k, v, pool_in, z, xbc, dt_raw, gate_pre = jnp.split(proj, split_idx, axis=-1)
        q = q.reshape(b, s, ATTN_HEADS, HEAD_DIM)
        k = k.reshape(b, s, ATTN_HEADS, HEAD_DIM)
        v = v.reshape(b, s, ATTN_HEADS, HEAD_DIM)
        y_a = dilated_attention_mixer(q, k, v, rel_bias) @ w_a[i]
        y_b = pool_mixer(pool_in, pool_w[i], pool_scale[i]) @ w_b[i]
        y_c = ssd_mixer(z, xbc, dt_raw, ssd_conv_w[i], ssd_conv_b[i], ssd_dt_bias[i],
                        ssd_a_log[i], ssd_d[i], ssd_norm_w[i]) @ w_c[i]
        gates = jax.nn.sigmoid(gate_pre + b_gate[i]).reshape(b, s, N_BRANCH, D_MODEL)
        merged = gates[:, :, 0] * y_a + gates[:, :, 1] * y_b + gates[:, :, 2] * y_c
        x = x + merged @ w_o[i]
        x = x + conv_ffn(rmsnorm(x, ln2_g[i]), ffn_w_up[i], ffn_conv_w[i], ffn_conv_b[i], ffn_w_down[i])
    return rmsnorm(x, final_g)


def setup_inputs(seed=0):
    out = dict(first_inputs(seed))
    for name, value in second_inputs(seed + 1).items():
        if name != "x":
            out[name + "_2"] = value
    return out


def reference(
    x, c, positions, ada_w, ada_b, norm_g, ffn_w_gate, ffn_w_up, ffn_w_down, hyb_w_in, fox_b_f,
    hyb_w_out, mla_w_down, mla_q_norm, mla_kv_norm, mla_w_uq, mla_w_ukv, mla_w_out, final_g,
    rel_bias_2, ln1_g_2, w_in_2, b_gate_2, w_a_2, pool_w_2, pool_scale_2, w_b_2, ssd_conv_w_2,
    ssd_conv_b_2, ssd_dt_bias_2, ssd_a_log_2, ssd_d_2, ssd_norm_w_2, w_c_2, w_o_2, ln2_g_2,
    ffn_w_up_2, ffn_conv_w_2, ffn_conv_b_2, ffn_w_down_2, final_g_2,
):
    x = first_block(
        x, c, positions, ada_w, ada_b, norm_g, ffn_w_gate, ffn_w_up, ffn_w_down, hyb_w_in,
        fox_b_f, hyb_w_out, mla_w_down, mla_q_norm, mla_kv_norm, mla_w_uq, mla_w_ukv, mla_w_out,
        final_g,
    )
    return second_block(
        x, rel_bias_2, ln1_g_2, w_in_2, b_gate_2, w_a_2, pool_w_2, pool_scale_2, w_b_2,
        ssd_conv_w_2, ssd_conv_b_2, ssd_dt_bias_2, ssd_a_log_2, ssd_d_2, ssd_norm_w_2, w_c_2,
        w_o_2, ln2_g_2, ffn_w_up_2, ffn_conv_w_2, ffn_conv_b_2, ffn_w_down_2, final_g_2,
    )


_drawn_inputs = setup_inputs


def setup_inputs(seed=0):
    import zlib

    import numpy as np

    out = dict(_drawn_inputs(seed))
    spreads = {}
    factors = {'norm_g': 5.323,
     'fox_b_f': 3.7,
     'mla_q_norm': 8.0,
     'mla_kv_norm': 8.0,
     'rel_bias_2': 8.0,
     'ln1_g_2': 3.216,
     'b_gate_2': 8.0,
     'ssd_conv_b_2': 4.394,
     'ssd_norm_w_2': 6.08,
     'ln2_g_2': 4.465,
     'ffn_conv_b_2': 4.56,
     'final_g_2': 25.507,
     'ssd_d_2': 37.02}
    for name, (base, spread) in spreads.items():
        noise = np.random.default_rng([zlib.crc32(name.encode()), seed]).standard_normal(out[name].shape)
        drawn = base * np.exp(spread * noise) if base else spread * noise
        out[name] = __import__('jax').numpy.asarray(drawn.astype(out[name].dtype))
    for name, factor in factors.items():
        out[name] = (out[name] * factor).astype(out[name].dtype)
    return out
```

```python
from collections import defaultdict
from contextlib import ExitStack
import math

import numpy as np

import concourse.bass as bass
from concourse import mybir

ALU = mybir.AluOpType
ACT = mybir.ActivationFunctionType
F32 = mybir.dt.float32
I32 = mybir.dt.int32
ds = bass.ds

P = 128
T = 512
D = 1024
KT = D // P
QT = T // P
FF = 2816
FT = FF // P
SLAB = 3 * D
SLOTS = 4
HD = 64
TOPK = 128
NEG = -1.0e30
IDX_SCALE = 0.125
GONE = -3.0e38
EPS = 1e-6
SSD_HEADS = 16
DIL_HEADS = 6
RES = 4
GW = 256
GN = 9
BIAS_W = GN * GW

CONST = {}


def _const_columns():
    at = 0
    for name, width in (("ident", P), ("ones", P), ("triu", P), ("causal", T), ("chunked", T), ("below", P),
                        ("rot16", P), ("rot64", P), ("poolfix", 64),
                        ("sel", SSD_HEADS * P), ("selpair", SSD_HEADS // 2 * P), ("foxrow", 16), ("foxone", 16),
                        ("foxkey", 2)):
        CONST[name] = (at, width)
        at += width
    return at


CONST_W = _const_columns()

VEC = {}


def _vec_columns():
    at = 0
    for name, width in (("c", 8), ("ada_b", 144), ("norm_g", 48), ("final_g", 8), ("ln1", 8), ("ln2", 8),
                        ("final2", 8), ("q_norm", 3), ("kv_norm", 2), ("b_gate", 24), ("pool_scale", 8),
                        ("conv_w", 48), ("conv_b", 12), ("ssd_norm", 8), ("ssd_d", 8), ("ffn_cw", 132),
                        ("ffn_cb", 44), ("dt_bias", 16), ("a_log", 16), ("b_f", 16), ("rel", 18),
                        ("invf16", 1), ("invf64", 1)):
        VEC[name] = (at, width)
        at += width
    return at


VEC_W = _vec_columns()


class Counts:

    def __init__(self):
        self.n = defaultdict(int)
        self.marks = {}
        self.step = {}
        self.it = None

    def value(self, what, n):
        step = self.step.get(what, 0) if self.it is not None else 0
        return self.it * step + n if step else n

    def __getitem__(self, what):
        return self.value(what, self.n[what])

    def add(self, what, times=1):
        self.n[what] += times

    def mark(self, name, sem, what):
        self.marks[name] = (sem, what, self.n[what])

    def wait_mark(self, eng, name):
        if name in self.marks:
            sem, what, n = self.marks[name]
            after(eng, sem, self.value(what, n))

    def loop(self, eng, first, end, body):
        before = dict(self.n)
        body(first)
        step = {k: v - before.get(k, 0) for k, v in self.n.items()}
        assert step.get("job", 0) % 2 == 0
        if end - first == 1:
            return
        mid, old = dict(self.n), dict(self.marks)
        with eng.Fori(first + 1, end) as i:
            self.it, self.step = i - (first + 1), step
            body(i)
            self.it = None
        assert all(self.n[k] - mid.get(k, 0) == step.get(k, 0) for k in self.n)
        for k in self.n:
            self.n[k] = before.get(k, 0) + step.get(k, 0) * (end - first)
        for name, (sem, what, n) in self.marks.items():
            if old.get(name) != (sem, what, n):
                self.marks[name] = (sem, what, n + step.get(what, 0) * (end - first - 2))


def after(eng, sem, count):
    if isinstance(count, int) and count <= 0:
        return
    eng.wait_ge(sem, count)


def build_program(nc, a, out, stop=None):
    ctx = ExitStack()
    with ctx:
        def sb(name, shape, dt=F32):
            return ctx.enter_context(nc.sbuf_tensor(name, shape, dt))

        def sem(name):
            return ctx.enter_context(nc.semaphore(name))

        hT = sb("residual_T", [P, KT, T])
        uT = sb("normed_T", [P, KT, T])
        A = sb("arena", [P, 36, T])
        W = sb("work", [P, 10, T])
        ring = sb("weight_ring", [P, SLOTS, SLAB])
        cst = sb("constants", [P, CONST_W])
        vec = sb("vectors", [P, VEC_W])
        mod = sb("modulation", [P, 2, 72])
        gs = sb("norm_scales", [P, 6, KT])
        gate = sb("residual_gates", [P, 6, KT])
        cond = sb("cond", [P, KT])
        stat = sb("row_stats", [P, 4, 8])
        diag = sb("diag_inverse_sums", [P, 2, P])
        carrier = sb("wait_carrier", [P, 3])
        top8 = sb("top8", [P, 3, 8])
        small = sb("small", [P, 12, 64])
        table = sb("bias_table", [P, 18])

        lin = [ctx.enter_context(nc.psum_tensor(f"lin{i}", [P, T], F32)) for i in range(2)]
        score = [ctx.enter_context(nc.psum_tensor(f"score{i}", [P, T], F32)) for i in range(2)]
        turn = [ctx.enter_context(nc.psum_tensor(f"turn{i}", [P, T], F32)) for i in range(2)]
        outp = [ctx.enter_context(nc.psum_tensor(f"out{i}", [P, T], F32)) for i in range(2)]

        skew = nc.dram_tensor("skew_scratch", [DIL_HEADS, P * BIAS_W], F32, kind="Internal").ap()

        slot_full = [sem(f"slot_full{s}") for s in range(SLOTS)]
        ada_full = [sem(f"ada_full{s}") for s in range(SLOTS)]
        ada_folded = sem("ada_folded")
        lin_full = [sem(f"lin_full{b}") for b in range(2)]
        lin_taken = [sem(f"lin_taken{b}") for b in range(2)]
        const_loaded = sem("const_loaded")
        vec_loaded = sem("vec_loaded")
        x_loaded = sem("x_loaded")
        dve_step = sem("dve_step")
        act_step = sem("act_step")
        cond_ready = sem("cond_ready")
        angle_ready = sem("angle_ready")
        rope_table = sem("rope_table")
        squares = sem("squares_added")
        sumsq_summed = sem("sumsq_summed")
        inverse_ready = sem("inverse_ready")
        root_ready = sem("root_ready")
        scaled = sem("scaled")
        u_ready = sem("u_ready")
        tap_done = sem("tap_done")
        silu_done = sem("silu_done")
        gated = sem("gated")
        roped = sem("roped")
        score_ready = sem("score_ready")
        logits_ready = sem("logits_ready")
        negmax_ready = sem("negmax_ready")
        probs_ready = sem("probs_ready")
        diag_ready = sem("diag_ready")
        turned = sem("turned")
        pT_ready = sem("pT_ready")
        pv_done = sem("pv_done")
        head_taken = sem("head_taken")
        relu_ready = sem("relu_ready")
        relu_used = sem("relu_used")
        forget_ready = sem("forget_ready")
        foxrow_ready = sem("foxrow_ready")
        softplus_ready = sem("softplus_ready")
        zeros_ready = sem("zeros_ready")
        merged_ready = sem("merged_ready")
        table_ready = sem("table_ready")
        bias_stored = [sem(f"bias_stored{i}") for i in range(2)]
        bias_loaded = [sem(f"bias_loaded{i}") for i in range(2)]
        perm_ready = sem("perm_ready")
        dt_ready = sem("dt_ready")
        ssd_ready = sem("ssd_ready")
        ssd_exp = sem("ssd_exp")
        ssd_pe = sem("ssd_pe")
        ssd_dve = sem("ssd_dve")
        result_ready = sem("result_ready")
        result_stored = sem("result_stored")

        def C(name, rows=P, lo=0, width=None):
            at, w = CONST[name]
            return cst[0:rows, at + lo:at + lo + (width or w)]

        def V(name, lo=0, width=None):
            at, w = VEC[name]
            return vec[:, at + lo:at + lo + (w if width is None else width)]

        def Vr(name, i):
            return vec[:, ds(i + VEC[name][0], 1)]

        def job_done(c, slot=None, note=None):
            b = c.n["job"] % 2
            c.add(f"bank{b}")
            c.add("job")
            if slot is not None:
                c.mark(f"slot{slot}", lin_full[b], f"bank{b}")
            if note:
                c.mark(note, lin_taken[b], f"bank{b}")

        def load(sp, c, s, src, width, full=slot_full):
            c.wait_mark(sp, f"slot{s}")
            sp.dma_start(ring[:, s, 0:width], src).then_inc(full[s], 16)

        def load_ada(sp, c, s, layer, sub, m):
            load(sp, c, s, a["ada"][layer, sub, ds(m, 1)].squeeze(0), SLAB, ada_full)
            c.add("folded")
            c.mark(f"slot{s}", ada_folded, "folded")

        def slab_there(pe, c, s):
            c.add(f"load{s}")
            pe.wait_ge(slot_full[s], c[f"load{s}"] * 16)

        def bank_open(pe, c):
            b = c.n["job"] % 2
            after(pe, lin_taken[b], c[f"bank{b}"])
            return lin[b]

        def bank_close(c, ins, **kw):
            ins.then_inc(lin_full[c.n["job"] % 2], 1)
            job_done(c, **kw)

        def bank_wait(eng, c):
            b = c.n["job"] % 2
            eng.wait_ge(lin_full[b], c[f"bank{b}"] + 1)
            return lin[b]

        def bank_take(c, ins, **kw):
            ins.then_inc(lin_taken[c.n["job"] % 2], 1)
            job_done(c, **kw)

        def skip_jobs(c, n=1):
            for _ in range(n):
                job_done(c)

        def all_taken(eng, c):
            for b in range(2):
                after(eng, lin_taken[b], c[f"bank{b}"])

        def vlink(v, c, ins):
            ins.then_inc(dve_step, 1)
            c.add("dve")
            v.wait_ge(dve_step, c["dve"])

        def carry_waits(v, place):
            v.memset(carrier[:, place:place + 1], 0.0)

        def alink(s, c, ins):
            ins.then_inc(act_step, 1)
            c.add("act")
            s.wait_ge(act_step, c["act"])

        def mm(pe, o, l, r, k, last):
            return pe.matmul(o, l, r, start=(k == 0), stop=(k == last))

        def copy_job(s, c, dst, w=T, rows=P, **kw):
            o = bank_wait(s, c)
            bank_take(c, s.activation(dst, o[0:rows, 0:w], ACT.Copy), **kw)

        sumsq, square, rinv = (W[:, n, :] for n in range(3))
        folded = [W[:, 5 + n, :] for n in range(2)]

        def add_squares(v, c, tile):
            vlink(v, c, v.tensor_tensor(W[:, 1:2, :], tile, tile, ALU.mult))
            v.tensor_tensor(W[:, 0:1, :], W[:, 0:1, :], W[:, 1:2, :], ALU.add).then_inc(squares, 1)
            c.add("sq")
            v.wait_ge(squares, c["sq"])

        def norm_pe(pe, c, tiles=KT):
            c.add("sq", tiles)
            pe.wait_ge(squares, c["sq"])
            pe.matmul(score[0][:, :], C("ones"), sumsq, start=True, stop=True).then_inc(sumsq_summed, 1)

        def norm_root(v, c, n):
            c.add("summed")
            v.wait_ge(sumsq_summed, c["summed"])
            vlink(v, c, v.tensor_scalar(rinv, score[0][:, :], 1.0 / n, EPS, ALU.mult, ALU.add))
            v.reciprocal(rinv, rinv).then_inc(inverse_ready, 1)
            v.wait_ge(root_ready, c["summed"])

        def norm_act(s, c):
            c.add("root")
            s.wait_ge(inverse_ready, c["root"])
            s.activation(rinv, rinv, ACT.Sqrt).then_inc(root_ready, 1)

        def ada_norm_dve(v, c, inst):
            norm_root(v, c, D)
            for k in range(KT):
                v.scalar_tensor_tensor(out=uT[:, k, :], in0=hT[:, k, :], scalar=gs[:, inst, k:k + 1], in1=rinv,
                                       op0=ALU.mult, op1=ALU.mult).then_inc(scaled, 1)

        def ada_norm_act(s, c, inst):
            layer, sub = inst // 3, inst % 3
            norm_act(s, c)
            for k in range(KT):
                c.add("scaled")
                s.wait_ge(scaled, c["scaled"])
                s.activation(uT[:, k, :], uT[:, k, :], ACT.Identity,
                             bias=mod[:, layer, 24 * sub + k:24 * sub + k + 1]).then_inc(u_ready, 1)

        def plain_norm_dve(v, c, g):
            norm_root(v, c, D)
            for k in range(KT):
                v.scalar_tensor_tensor(out=uT[:, k, :], in0=hT[:, k, :], scalar=V(g, k, 1), in1=rinv,
                                       op0=ALU.mult, op1=ALU.mult).then_inc(u_ready, 1)

        def u_done(pe, c):
            c.add("u", KT)
            pe.wait_ge(u_ready, c["u"])

        def clear_sumsq(v, c):
            vlink(v, c, v.memset(sumsq, 0.0))

        def fold_dve(v, c, s, n):
            c.add(f"ada{s}")
            v.wait_ge(ada_full[s], c[f"ada{s}"] * 16)
            w = ring[:, s, :].rearrange("p (k n) -> p k n", k=KT)
            acc = folded[n][:, 0:SLAB // KT]
            vlink(v, c, v.tensor_scalar(acc, w[:, 0, :], cond[:, 0:1], None, ALU.mult))
            for k in range(1, KT):
                ins = v.scalar_tensor_tensor(out=acc, in0=w[:, k, :], scalar=cond[:, k:k + 1], in1=acc,
                                             op0=ALU.mult, op1=ALU.add)
                if k < KT - 1:
                    vlink(v, c, ins)
            ins.then_inc(ada_folded, 1)

        def ada_pe(pe, c, n):
            c.add("folded")
            pe.wait_ge(ada_folded, c["folded"])
            o = bank_open(pe, c)
            for m in range(3):
                last = pe.matmul(o[:, m:m + 1], folded[n][:, m * P:(m + 1) * P], C("ones", width=1), start=True,
                                 stop=True)
            bank_close(c, last)

        def ada_dve(v, c, layer, sub, group):
            o = bank_wait(v, c)
            at = VEC["ada_b"][0] + 72 * layer + 24 * sub
            bank_take(c, v.tensor_tensor(mod[:, layer, ds(group * 3 + 24 * sub, 3)], o[:, 0:3],
                                         vec[:, ds(group * 3 + at, 3)], ALU.add))

        def mod_dve(v, c, layer, sub):
            i = 3 * layer + sub
            all_taken(v, c)
            vlink(v, c, v.scalar_tensor_tensor(out=gs[:, i, :], in0=mod[:, layer, 24 * sub + 8:24 * sub + 16],
                                               scalar=1.0, in1=V("norm_g", 8 * i, 8), op0=ALU.add, op1=ALU.mult))
            vlink(v, c, v.tensor_scalar(gate[:, i, :], mod[:, layer, 24 * sub + 16:24 * sub + 24],
                                        1.0 if sub == 1 else 0.5, None, ALU.mult))

        onehot = A[:, 0:5, :].rearrange("p a b -> p (a b)")[:, 0:BIAS_W]
        relx = A[:, 5:10, :].rearrange("p a b -> p (a b)")[:, 0:18 * P].rearrange("p (h n) -> p h n", h=18)
        biasrow = [A[:, 26 + 5 * i:31 + 5 * i, :].rearrange("p a b -> p (a b)")[:, 0:BIAS_W] for i in range(2)]
        CHUNKS = [(0, 512, 0), (512, 512, 0), (1024, 512, 0), (1536, 256, 0), (1792, 256, 1), (2048, 256, 2)]
        cos16, sin16, cos64, sin64 = (A[:, 22 + i, :] for i in range(4))
        positions = A[:, 10, :]

        def prologue_sp(sp, c):
            sp.dma_start(positions.bitcast(I32), a["positions"].to_broadcast([P, T])).then_inc(vec_loaded, 16)
            sp.dma_start(vec[:, :], a["vectors"]).then_inc(vec_loaded, 16)
            sp.dma_start(cst[:, :], a["constants"]).then_inc(const_loaded, 16)
            sp.dma_start(onehot[0:33, :], a["onehot"]).then_inc(const_loaded, 16)
            for j in range(4):
                load_ada(sp, c, j, 0, 0, j)
            sp.dma_start(hT[:, :, :], a["xT"]).then_inc(x_loaded, 16)
            for j in range(KT):
                if j < DIL_HEADS:
                    for _ in CHUNKS:
                        job_done(c, note="row")
                    c.wait_mark(sp, "row")
                    sp.dma_start(skew[j].rearrange("(p w) -> p w", p=P), biasrow[j % 2])\
                      .then_inc(bias_stored[j % 2], 16)
                if j + 4 < KT:
                    load_ada(sp, c, j, 0, 0, j + 4)
                job_done(c)

        def prologue_pe(pe, c):
            pe.wait_ge(const_loaded, 32)
            pe.wait_ge(table_ready, 1)
            for j in range(KT):
                if j < DIL_HEADS:
                    for lo, w, g in CHUNKS:
                        o = bank_open(pe, c)
                        bank_close(c, pe.matmul(o[:, 0:w], relx[0:33, g * DIL_HEADS + j, :],
                                                onehot[0:33, lo:lo + w], start=True, stop=True))
                ada_pe(pe, c, j % 2)

        def prologue_act(s, c):
            s.wait_ge(vec_loaded, 32)
            s.activation(cond[:, :], V("c"), ACT.Silu).then_inc(cond_ready, 1)
            for j in range(KT):
                if j < DIL_HEADS:
                    after(s, bias_stored[j % 2], 16 * (j // 2))
                    for lo, w, _ in CHUNKS:
                        copy_job(s, c, biasrow[j % 2][:, lo:lo + w], w)
                skip_jobs(c)
            for i in range(2):
                s.wait_ge(angle_ready, 2 * i + 2)
                s.activation(A[:, 23 + 2 * i, :], A[:, 13 + 2 * i, :], ACT.Sin).then_inc(rope_table, 1)
                s.activation(A[:, 22 + 2 * i, :], A[:, 14 + 2 * i, :], ACT.Sin).then_inc(rope_table, 1)

        def prologue_dve(v, c):
            vlink(v, c, v.memset(stat[:, :, :], 0.0))
            vlink(v, c, v.memset(table[:, :], NEG))
            v.wait_ge(vec_loaded, 32)
            vlink(v, c, v.tensor_scalar(table[0:32, :], V("rel")[0:32, :], 8.0, None, ALU.mult))
            v.tensor_copy(relx[0:33, :, :], table[0:33, :].unsqueeze(2).to_broadcast([33, 18, P]))\
             .then_inc(table_ready, 1)
            two_pi = 2 * math.pi
            c1 = 6.28125
            c2 = float(np.float32(math.floor((two_pi - c1) * 2 ** 21) / 2 ** 21))
            c3 = float(np.float32(two_pi - c1 - c2))
            magic = 1.5 * 2 ** 23
            vlink(v, c, v.tensor_copy(positions, positions.bitcast(I32)))
            for i, inv in enumerate(("invf16", "invf64")):
                ang, k, r, q = (A[:, n, :] for n in (11, 12, 13 + 2 * i, 14 + 2 * i))
                vlink(v, c, v.tensor_scalar(ang, positions, V(inv), None, ALU.mult))
                vlink(v, c, v.tensor_scalar(k, ang, 1.0 / two_pi, magic, ALU.mult, ALU.add))
                vlink(v, c, v.tensor_scalar(k, k, -magic, None, ALU.add))
                for part in (c1, c2, c3):
                    vlink(v, c, v.scalar_tensor_tensor(out=ang, in0=k, scalar=-part, in1=ang, op0=ALU.mult,
                                                       op1=ALU.add))
                v.tensor_scalar(r, ang, 3.1415925, -3.1415925, ALU.min, ALU.max).then_inc(angle_ready, 1)
                v.wait_ge(angle_ready, 2 * i + 1)
                vlink(v, c, v.tensor_scalar(q, r, -1.0, None, ALU.mult))
                vlink(v, c, v.tensor_tensor(q, q, r, ALU.min))
                v.tensor_scalar(q, q, math.pi / 2, None, ALU.add).then_inc(angle_ready, 1)
            v.wait_ge(cond_ready, 1)
            clear_sumsq(v, c)
            for j in range(KT):
                fold_dve(v, c, j % 4, j % 2)
                if j >= 4:
                    if j == 4:
                        v.wait_ge(x_loaded, 16)
                    for k in (2 * j - 8, 2 * j - 7):
                        add_squares(v, c, hT[:, k:k + 1, :])
                if j < DIL_HEADS:
                    skip_jobs(c, len(CHUNKS))
                ada_dve(v, c, 0, 0, j)
            mod_dve(v, c, 0, 0)

        def down_sp(sp, c, src, width, adas=()):
            def body(i):
                for j in range(2):
                    load(sp, c, 2 + j, src[ds(i * 2 + j, 1)].squeeze(0), width)
                    job_done(c, slot=2 + j)
                    for n, (l, s) in enumerate(adas):
                        load_ada(sp, c, n, l, s, i * 2 + j)
                        job_done(c)
            c.loop(sp, 0, KT // 2, body)

        def down_pe(pe, c, rhs, adas=()):
            n_k = len(rhs)

            def body(i):
                for j in range(2):
                    slab_there(pe, c, 2 + j)
                    o = bank_open(pe, c)
                    for k in range(n_k):
                        last = mm(pe, o[:, :], ring[:, 2 + j, k * P:(k + 1) * P], rhs[k], k, n_k - 1)
                    bank_close(c, last)
                    for n in range(len(adas)):
                        ada_pe(pe, c, n)
            c.loop(pe, 0, KT // 2, body)

        def down_act(s, c, adas=()):
            skip_jobs(c, KT * (1 + len(adas)))

        def down_dve(v, c, inst, adas=()):
            clear_sumsq(v, c)

            def body(i):
                for j in range(2):
                    m = i * 2 + j
                    for n in range(len(adas)):
                        fold_dve(v, c, n, n)
                    o = bank_wait(v, c)
                    tile = hT[:, ds(m, 1), :]
                    if inst is None:
                        ins = v.tensor_tensor(tile, o[:, :].unsqueeze(1), tile, ALU.add)
                    else:
                        ins = v.scalar_tensor_tensor(out=tile, in0=o[:, :].unsqueeze(1),
                                                     scalar=gate[:, inst, ds(m, 1)], in1=tile,
                                                     op0=ALU.mult, op1=ALU.add)
                    bank_take(c, ins, note="updated")
                    c.wait_mark(v, "updated")
                    add_squares(v, c, tile)
                    for l, s in adas:
                        ada_dve(v, c, l, s, m)
            c.loop(v, 0, KT // 2, body)
            for l, s in adas:
                mod_dve(v, c, l, s)

        def up_sp(sp, c, src):
            def body(i):
                for j in range(2):
                    load(sp, c, j, src[ds(i * 2 + j, 1)].squeeze(0), 2 * D)
                    job_done(c)
                    job_done(c, slot=j)
            c.loop(sp, 0, FT // 2, body)

        def up_pe(pe, c):
            u0 = c.n["u"]

            def body(i):
                for j in range(2):
                    slab_there(pe, c, j)
                    w = ring[:, j, 0:2 * D].rearrange("p (g k n) -> p g k n", g=2, k=KT)
                    for g in range(2):
                        o = bank_open(pe, c)
                        for k in range(KT):
                            if isinstance(i, int) and j == 0 and g == 0:
                                pe.wait_ge(u_ready, u0 + k + 1)
                            last = mm(pe, o[:, :], w[:, g, k, :], uT[:, k, :], k, KT - 1)
                        bank_close(c, last)
            c.loop(pe, 0, FT // 2, body)
            c.add("u", KT)

        hidden = [A[:, k, :] for k in range(FT)]

        def swiglu_act(s, c):
            def body(i):
                for j in range(2):
                    o = bank_wait(s, c)
                    c.wait_mark(s, f"silu{j}")
                    bank_take(c, s.activation(W[:, 3 + j, :], o[:, :], ACT.Silu))
                    job_done(c, note=f"silu{j}")
            c.marks.pop("silu0", None)
            c.marks.pop("silu1", None)
            c.loop(s, 0, FT // 2, body)

        def swiglu_dve(v, c):
            def body(i):
                for j in range(2):
                    job_done(c, note="gate")
                    c.wait_mark(v, "gate")
                    o = bank_wait(v, c)
                    bank_take(c, v.tensor_tensor(A[:, ds(i * 2 + j, 1), :], o[:, :].unsqueeze(1),
                                                 W[:, 3 + j:4 + j, :], ALU.mult))
            c.loop(v, 0, FT // 2, body)

        def ffn(inst, index, adas):
            def sp(e, c):
                up_sp(e, c, a["up"][index])
                down_sp(e, c, a["down"][index], FF, adas)

            def pe(e, c):
                norm_pe(e, c)
                up_pe(e, c)
                all_taken(e, c)
                down_pe(e, c, hidden, adas)

            def act(e, c):
                ada_norm_act(e, c, inst)
                swiglu_act(e, c)
                down_act(e, c, adas)

            def dve(e, c):
                ada_norm_dve(e, c, inst)
                swiglu_dve(e, c)
                down_dve(e, c, inst, adas)
            return sp, pe, act, dve

        logits = [W[:, 2 + n, :] for n in range(4)]
        probsT = [W[:, 6 + n, :] for n in range(2)]

        def attend_pe(pe, c, units):
            part0, unit0 = c.n["part"], c.n["unit"]
            first_part = [sum(len(u["parts"]) for u in units[:n]) for n in range(len(units) + 1)]
            for t in range(len(units) + 3):
                if t < len(units):
                    for q, part in enumerate(units[t]["parts"]):
                        n = first_part[t] + q
                        after(pe, logits_ready, c.value("part", part0 + n - 1))
                        k = len(part["products"])
                        for m, (l, r, lo, hi) in enumerate(part["products"]):
                            opens = m == 0 or part["products"][m - 1][2] != lo
                            closes = m == k - 1 or part["products"][m + 1][2] != lo
                            last = pe.matmul(score[(part0 + n) % 2][:, lo:hi], l, r, start=opens, stop=closes)
                        last.then_inc(score_ready, 1)
                if 0 <= t - 2 < len(units):
                    u = t - 2
                    pe.wait_ge(diag_ready, c.value("unit", unit0 + u + 1))
                    for q, part in enumerate(units[u]["parts"]):
                        n = first_part[u] + q
                        pe.wait_ge(probs_ready, c.value("part", part0 + n + 1))
                        after(pe, pT_ready, c.value("part", part0 + n - 1))
                        for b in range(part["n"] // P):
                            last = pe.matmul(turn[(part0 + n) % 2][:, b * P:(b + 1) * P],
                                             logits[(part0 + n) % 4][:, b * P:(b + 1) * P],
                                             diag[:, (unit0 + u) % 2, :], start=True, stop=True)
                        last.then_inc(turned, 1)
                if t - 3 >= 0:
                    u = t - 3
                    blocks = sum(len(part["values"]) for part in units[u]["parts"])
                    at = 0
                    for q, part in enumerate(units[u]["parts"]):
                        n = first_part[u] + q
                        pe.wait_ge(pT_ready, c.value("part", part0 + n + 1))
                        if u == 0 and q == 0:
                            after(pe, head_taken, c["head"])
                        for b, val in enumerate(part["values"]):
                            last = mm(pe, units[u]["out"], val, probsT[(part0 + n) % 2][:, b * P:(b + 1) * P],
                                      at, blocks - 1)
                            at += 1
                        last.then_inc(pv_done, 1)
            count_units(c, units)

        def count_units(c, units):
            c.add("part", sum(len(u["parts"]) for u in units))
            c.add("unit", len(units))

        def attend_dve(v, c, units, scale, between=lambda t: None):
            part0, unit0 = c.n["part"], c.n["unit"]
            p = 0
            for t in range(len(units) + 1):
                if t < len(units):
                    st = stat[:, (unit0 + t) % 4, :]
                    parts = units[t]["parts"]
                    for q, part in enumerate(parts):
                        n = part0 + p
                        p += 1
                        v.wait_ge(score_ready, c.value("part", n + 1))
                        after(v, turned, c.value("part", n - 3))
                        carry_waits(v, q)
                        v.tensor_tensor_reduce(logits[n % 4][:, 0:part["n"]], score[n % 2][:, 0:part["n"]],
                                               part["bias"], scale, NEG, ALU.add, ALU.max,
                                               st[:, q:q + 1]).then_inc(logits_ready, 1)
                    v.wait_ge(logits_ready, c.value("part", part0 + p))
                    if len(parts) == 2:
                        vlink(v, c, v.tensor_tensor(st[:, 0:1], st[:, 0:1], st[:, 1:2], ALU.max))
                    v.tensor_scalar(st[:, 2:3], st[:, 0:1], -1.0, None, ALU.mult).then_inc(negmax_ready, 1)
                    between(t)
                if t > 0:
                    u = t - 1
                    st = stat[:, (unit0 + u) % 4, :]
                    two = len(units[u]["parts"]) == 2
                    done = sum(len(x["parts"]) for x in units[:u + 1])
                    v.wait_ge(probs_ready, c.value("part", part0 + done))
                    if two:
                        vlink(v, c, v.tensor_tensor(st[:, 3:4], st[:, 3:4], st[:, 4:5], ALU.add))
                    vlink(v, c, v.reciprocal(st[:, 5:6], st[:, 3:4]))
                    after(v, turned, c.value("part", part0 + sum(len(x["parts"]) for x in units[:max(u - 1, 0)])))
                    v.tensor_scalar(diag[:, (unit0 + u) % 2, :], C("ident"), st[:, 5:6], None,
                                    ALU.mult).then_inc(diag_ready, 1)
            count_units(c, units)

        def attend_act(s, c, units, outs):
            part0, unit0 = c.n["part"], c.n["unit"]
            first_part = [sum(len(u["parts"]) for u in units[:n]) for n in range(len(units) + 1)]
            for t in range(len(units) + 3):
                if t < len(units):
                    st = stat[:, (unit0 + t) % 4, :]
                    s.wait_ge(negmax_ready, c.value("unit", unit0 + t + 1))
                    for q, part in enumerate(units[t]["parts"]):
                        n = part0 + first_part[t] + q
                        lg = logits[n % 4][:, 0:part["n"]]
                        s.activation(lg, lg, ACT.Exp, bias=st[:, 2:3], accum_out=st[:, 3 + q:4 + q])\
                         .then_inc(probs_ready, 1)
                if 0 <= t - 2 < len(units):
                    for q, part in enumerate(units[t - 2]["parts"]):
                        n = part0 + first_part[t - 2] + q
                        s.wait_ge(turned, c.value("part", n + 1))
                        after(s, pv_done, c.value("part", n - 1))
                        s.activation(probsT[n % 2][:, 0:part["n"]], turn[n % 2][:, 0:part["n"]], ACT.Copy)\
                         .then_inc(pT_ready, 1)
                if t - 3 >= 0:
                    for src, dst in outs.get(t - 3, ()):
                        s.wait_ge(pv_done, c.value("part", part0 + first_part[t - 2]))
                        s.activation(dst, src, ACT.Copy).then_inc(head_taken, 1)
                        c.add("head")
            count_units(c, units)

        def rope_raw_act(s, c, raw, name):
            o = bank_wait(s, c)
            c.wait_mark(s, name)
            bank_take(c, s.activation(raw, o[:, :], ACT.Copy))

        def rope_note(c, name):
            c.add("rope")
            c.mark(name, roped, "rope")

        def rotate_pe(pe, c, raw, rot, note):
            c.wait_mark(pe, note)
            o = bank_open(pe, c)
            bank_close(c, pe.matmul(o[:, :], C(rot), raw, start=True, stop=True))

        def rope_dve(v, c, raw, cos, sin, dst, note):
            c.wait_mark(v, note)
            after(v, roped, c["rope"])
            v.tensor_tensor(W[:, 8, :], raw, cos, ALU.mult)
            o = bank_wait(v, c)
            bank_take(c, v.tensor_tensor(W[:, 9, :], o[:, :], sin, ALU.mult), note="rope_terms")
            c.wait_mark(v, "rope_terms")
            v.tensor_tensor(dst, W[:, 8, :], W[:, 9, :], ALU.add).then_inc(roped, 1)
            c.add("rope")

        def project(pe, c, w, rhs, row=0, **kw):
            o = bank_open(pe, c)
            m = w(0).shape[-1]
            for k in range(len(rhs)):
                last = mm(pe, o[row:row + m, :], w(k), rhs[k], k, len(rhs) - 1)
            bank_close(c, last, **kw)

        def project_rows(pe, c, w, lhs, tiles, width, **kw):
            o = bank_open(pe, c)
            for n, tt in enumerate(tiles):
                for k in range(len(lhs)):
                    last = mm(pe, o[:, n * width:(n + 1) * width], lhs[k][:, tt * P:(tt + 1) * P], w(k), k,
                              len(lhs) - 1)
            bank_close(c, last, **kw)

        u_tiles = [uT[:, k, :] for k in range(KT)]

        def part(products, n, bias, values):
            return dict(products=products, n=n, bias=bias, values=values)

        qT, kT, vN = A[:, 16, :], A[:, 17, :], A[:, 18, :].rearrange("p (t n) -> p t n", t=QT)
        foxK, foxC = A[0:16, 19, :], A[0:16, 20, :]
        foxQ = [A[0:16, 21, :], A[0:16, 26, :]]
        iq, ik = [A[:, 0, :], A[:, 1, :]], A[:, 2, :]
        sel_mask = [None] + [A[:, 4 + n, :] for n in range(1, QT)]
        raw = [W[:, 0, :], W[:, 1, :]]
        mixed = [A[:, 8 + n, :] for n in range(8)]

        def pair_units(kind):
            units = []
            for hh in range(2):
                r = slice(64 * hh, 64 * hh + 64)
                for qt in range(QT):
                    n = (qt + 1) * P
                    q = slice(qt * P, n)
                    products = [(qT[r, q], kT[r, 0:n], 0, n)]
                    if kind == "fox":
                        products.append((foxQ[hh][:, q], foxK[:, 0:n], 0, n))
                        bias = C("causal", lo=T - n, width=n)
                    else:
                        bias = sel_mask[qt][:, 0:n] if qt else C("chunked", lo=T - n, width=n)
                    values = [vN[:, b, r] for b in range(qt + 1)]
                    units.append(dict(parts=[part(products, n, bias, values)], out=outp[0][r, q]))
            return units

        def softplus_act(s, c):
            c.add("softplus_in")
            s.wait_ge(forget_ready, c["softplus_in"])
            alink(s, c, s.activation(small[:, 2, :], small[:, 1, :], ACT.Exp))
            s.activation(small[:, 2, :], small[:, 2, :], ACT.Ln, bias=1.0).then_inc(softplus_ready, 1)

        def softplus_dve_in(v, c):
            vlink(v, c, v.tensor_scalar(small[:, 1, :], small[:, 0, :], -1.0, None, ALU.mult))
            v.tensor_tensor(small[:, 1, :], small[:, 1, :], small[:, 0, :], ALU.min).then_inc(forget_ready, 1)
            c.add("softplus")
            v.wait_ge(softplus_ready, c["softplus"])

        def hybrid():
            def sp(e, c):
                for n in range(2):
                    e.wait_ge(bias_stored[n], 16 * (DIL_HEADS // 2))
                load(e, c, 0, a["idx"], SLAB)
                load(e, c, 1, a["idx_small"], KT * 20)
                job_done(c), job_done(c), job_done(c)
                job_done(c, slot=0)
                job_done(c), job_done(c)
                job_done(c, slot=1)
                skip_jobs(c, 1 + 12)

                def fox(i):
                    load(e, c, 2, a["fox"][ds(i, 1)].squeeze(0), SLAB)
                    skip_jobs(c, 3)
                    job_done(c, slot=2)
                    c.add("part", 2 * QT)
                c.loop(e, 0, 4, fox)

                def dsa(i):
                    load(e, c, 3, a["dsa"][ds(i, 1)].squeeze(0), SLAB)
                    skip_jobs(c, 4)
                    skip_jobs(c, 1)
                    job_done(c, slot=3)
                    c.add("part", 2 * QT)
                c.loop(e, 0, 4, dsa)
                down_sp(e, c, a["hyb_out"], D)

            def pe(e, c):
                norm_pe(e, c)
                u_done(e, c)
                slab_there(e, c, 0)
                w = ring[:, 0, :].rearrange("p (k n) -> p k n", k=KT)
                project(e, c, lambda k: w[:, k, 0:128], u_tiles, note="iq0")
                project(e, c, lambda k: w[:, k, 128:256], u_tiles, note="iq1")
                rotate_pe(e, c, raw[0], "rot16", "iq0")
                project(e, c, lambda k: w[:, k, 256:384], u_tiles, note="ik")
                rotate_pe(e, c, raw[1], "rot16", "iq1")
                rotate_pe(e, c, raw[0], "rot16", "ik")
                slab_there(e, c, 1)
                ws = ring[:, 1, 0:KT * 20].rearrange("p (k n) -> p k n", k=KT)
                project_rows(e, c, lambda k: ws[:, k, :], u_tiles, range(QT), 20)
                c.add("forget", 2)
                e.wait_ge(forget_ready, c["forget"])
                o = bank_open(e, c)
                for b in range(QT):
                    for b2 in range(b + 1):
                        last = mm(e, o[0:16, b * P:(b + 1) * P], small[:, 3, b2 * 16:b2 * 16 + 16],
                                  C("triu") if b2 == b else C("ones"), b2, b)
                bank_close(c, last)
                c.add("rope", 3)
                e.wait_ge(roped, c["rope"])
                for qt in range(1, QT):
                    n = (qt + 1) * P
                    for hh in range(4):
                        r = slice(64 * (hh % 2), 64 * (hh % 2) + 64)
                        o = bank_open(e, c)
                        bank_close(c, e.matmul(o[:, 0:n], iq[hh // 2][r, qt * P:n], ik[r, 0:n], start=True, stop=True))

                def fox(i):
                    slab_there(e, c, 2)
                    w = ring[:, 2, :].rearrange("p (g k n) -> p g k n", g=3, k=KT)
                    project(e, c, lambda k: w[:, 0, k, :], u_tiles)
                    project(e, c, lambda k: w[:, 1, k, :], u_tiles)
                    for v2 in range(2):
                        project_rows(e, c, lambda k: w[:, 2, k, :], u_tiles, (2 * v2, 2 * v2 + 1), P)
                    all_taken(e, c)
                    c.add("foxrow")
                    e.wait_ge(foxrow_ready, c["foxrow"])
                    attend_pe(e, c, pair_units("fox"))
                    c.add("head")
                c.loop(e, 0, 4, fox)

                def dsa(i):
                    slab_there(e, c, 3)
                    w = ring[:, 3, :].rearrange("p (g k n) -> p g k n", g=3, k=KT)
                    project(e, c, lambda k: w[:, 0, k, :], u_tiles, note="q")
                    project(e, c, lambda k: w[:, 1, k, :], u_tiles, note="k")
                    rotate_pe(e, c, raw[0], "rot16", "q")
                    rotate_pe(e, c, raw[1], "rot16", "k")
                    for v2 in range(2):
                        project_rows(e, c, lambda k: w[:, 2, k, :], u_tiles, (2 * v2, 2 * v2 + 1), P)
                    all_taken(e, c)
                    c.add("rope", 2)
                    e.wait_ge(roped, c["rope"])
                    attend_pe(e, c, pair_units("dsa"))
                    c.add("head")
                c.loop(e, 0, 4, dsa)
                e.wait_ge(head_taken, c["head"])
                down_pe(e, c, mixed)

            def act(e, c):
                ada_norm_act(e, c, 1)
                rope_raw_act(e, c, raw[0], "raw0")
                rope_note(c, "raw0")
                rope_raw_act(e, c, raw[1], "raw1")
                rope_note(c, "raw1")
                skip_jobs(c)
                rope_raw_act(e, c, raw[0], "raw0")
                rope_note(c, "raw0")
                skip_jobs(c, 3)
                softplus_act(e, c)
                c.add("softplus_in")
                skip_jobs(c)
                for n in range(12):
                    o = bank_wait(e, c)
                    width = (n // 4 + 2) * P
                    after(e, relu_used, n - 1)
                    bank_take(c, e.activation(W[:, 2 + n % 2, 0:width], o[:, 0:width], ACT.Relu, scale=IDX_SCALE))
                c.add("relu", 12)

                def fox(i):
                    copy_job(e, c, qT)
                    copy_job(e, c, kT)
                    for v2 in range(2):
                        copy_job(e, c, vN[:, 2 * v2:2 * v2 + 2, :].rearrange("p t n -> p (t n)"), 2 * P)
                    attend_act(e, c, pair_units("fox"),
                               {7: [(outp[0][:, :].unsqueeze(1), A[:, ds(i + 8, 1), :])]})
                c.loop(e, 0, 4, fox)

                def dsa(i):
                    rope_raw_act(e, c, raw[0], "raw0")
                    rope_note(c, "raw0")
                    rope_raw_act(e, c, raw[1], "raw1")
                    rope_note(c, "raw1")
                    skip_jobs(c, 2)
                    for v2 in range(2):
                        copy_job(e, c, vN[:, 2 * v2:2 * v2 + 2, :].rearrange("p t n -> p (t n)"), 2 * P)
                    attend_act(e, c, pair_units("dsa"),
                               {7: [(outp[0][:, :].unsqueeze(1), A[:, ds(i + 12, 1), :])]})
                c.loop(e, 0, 4, dsa)
                down_act(e, c)

            def dve(e, c):
                ada_norm_dve(e, c, 1)
                job_done(c, note="iq0")
                job_done(c, note="iq1")
                rope_dve(e, c, raw[0], cos16, sin16, iq[0], "iq0")
                job_done(c, note="ik")
                rope_dve(e, c, raw[1], cos16, sin16, iq[1], "iq1")
                rope_dve(e, c, raw[0], cos16, sin16, ik, "ik")
                o = bank_wait(e, c)
                rows = o[:, 0:80].rearrange("p (t n) -> p t n", t=QT)
                x = small[:, 0, :].rearrange("p (t n) -> p t n", t=QT)
                vlink(e, c, e.tensor_tensor(x, rows[:, :, 0:16], V("b_f").unsqueeze(1).to_broadcast([P, QT, 16]),
                                            ALU.add))
                iw = small[:, 4, 0:16]
                bank_take(c, e.tensor_scalar(iw.rearrange("p (t n) -> p t n", t=QT), rows[:, :, 16:20], 0.5, None,
                                             ALU.mult), note="iw")
                c.wait_mark(e, "iw")
                softplus_dve_in(e, c)
                e.scalar_tensor_tensor(out=small[:, 3, :], in0=small[:, 0, :], scalar=0.0, in1=small[:, 2, :],
                                       op0=ALU.min, op1=ALU.subtract).then_inc(forget_ready, 1)
                o = bank_wait(e, c)
                vlink(e, c, e.tensor_copy(foxC, o[0:16, :]))
                bank_take(c, e.tensor_scalar(foxK, o[0:16, :], C("foxkey", 16, 0, 1), C("foxkey", 16, 1, 1), ALU.mult,
                                             ALU.add))
                for n in range(12):
                    qt, hh = n // 4 + 1, n % 4
                    width = (qt + 1) * P
                    job_done(c, note="relu")
                    c.wait_mark(e, "relu")
                    acc, r, w = sel_mask[qt][:, 0:width], W[:, 2 + n % 2, 0:width], iw[:, 4 * qt + hh:4 * qt + hh + 1]
                    if hh == 0:
                        e.tensor_scalar(acc, r, w, None, ALU.mult).then_inc(relu_used, 1)
                    else:
                        e.scalar_tensor_tensor(out=acc, in0=r, scalar=w, in1=acc, op0=ALU.mult, op1=ALU.add)\
                         .then_inc(relu_used, 1)
                    e.wait_ge(relu_used, n + 1)
                    if hh == 3:
                        last = acc[:, width - P:width]
                        vlink(e, c, e.tensor_tensor(last, last, C("chunked", lo=T - P, width=P), ALU.add))

                def search(qt):
                    tile = sel_mask[qt][:, 0:(qt + 1) * P]
                    carry_waits(e, 2)
                    vlink(e, c, e.max(top8[:, qt - 1, :], tile))
                    carry_waits(e, 2)
                    vlink(e, c, e.match_replace(tile, top8[:, qt - 1, :], tile, GONE))

                def fox(i):
                    for hh in range(2):
                        if hh == 0:
                            b = c.n["job"] % 2
                            e.wait_ge(lin_full[b], c[f"bank{b}"] + 1)
                        ins = e.tensor_scalar(foxQ[hh], foxC, cst[0:16, ds(i * 2 + (CONST["foxrow"][0] + hh), 1)],
                                              cst[0:16, ds(i * 2 + (CONST["foxone"][0] + hh), 1)], ALU.mult, ALU.add)
                        if hh == 0:
                            vlink(e, c, ins)
                        else:
                            ins.then_inc(foxrow_ready, 1)
                    skip_jobs(c, 4)
                    todo = [qt for _ in range(TOPK // 8 // 4) for qt in range(1, QT)]

                    def between(t):
                        for _ in range(2 if t % 2 == 0 else 1):
                            search(todo.pop())
                    attend_dve(e, c, pair_units("fox"), 0.125, between)
                    assert not todo
                c.loop(e, 0, 4, fox)
                for qt in range(1, QT):
                    tile = sel_mask[qt][:, 0:(qt + 1) * P]
                    vlink(e, c, e.tensor_scalar(tile, tile, -2.0e38, NEG, ALU.is_gt, ALU.mult))

                def dsa(i):
                    job_done(c, note="q")
                    job_done(c, note="k")
                    rope_dve(e, c, raw[0], cos16, sin16, qT, "q")
                    rope_dve(e, c, raw[1], cos16, sin16, kT, "k")
                    skip_jobs(c, 2)
                    attend_dve(e, c, pair_units("dsa"), 0.125)
                c.loop(e, 0, 4, dsa)
                down_dve(e, c, 1)
            return sp, pe, act, dve

        latent = [A[:, n, :] for n in range(5)]
        kr = A[:, 5, :]
        qn, kn, qr = [A[:, 16, :], A[:, 17, :]], [A[:, 19, :], A[:, 20, :]], A[:, 18, :]
        vM = A[:, 26:28, :].rearrange("p a b -> p (a b)").rearrange("p (t n) -> p t n", t=QT)
        kr_raw = W[:, 3, :]

        def mla_units():
            units = []
            for hh in range(2):
                r = slice(64 * hh, 64 * hh + 64)
                for qt in range(QT):
                    n = (qt + 1) * P
                    q = slice(qt * P, n)
                    products = [(qn[hh][:, q], kn[hh][:, 0:n], 0, n), (qr[r, q], kr[r, 0:n], 0, n)]
                    values = [vM[:, b, hh * P:(hh + 1) * P] for b in range(qt + 1)]
                    units.append(dict(parts=[part(products, n, C("chunked", lo=T - n, width=n), values)],
                                      out=outp[hh][:, q]))
            return units

        def mla():
            def sp(e, c):
                for n in range(2):
                    load(e, c, n, a["mla_down"][n], SLAB)
                    skip_jobs(c, 2)
                    job_done(c, slot=n)
                skip_jobs(c)

                def pair(i):
                    load(e, c, 2, a["mla_up"][ds(i, 1)].squeeze(0), 2176)
                    skip_jobs(c, 7)
                    job_done(c, slot=2)
                    c.add("part", 2 * QT)
                c.loop(e, 0, 4, pair)
                down_sp(e, c, a["mla_out"], D)

            def pe(e, c):
                norm_pe(e, c)
                u_done(e, c)
                for n in range(2):
                    slab_there(e, c, n)
                    w = ring[:, n, :].rearrange("p (k n) -> p k n", k=KT)
                    for m in range(3):
                        project(e, c, lambda k: w[:, k, m * P:(m + 1) * P], u_tiles,
                                note="kr" if (n, m) == (1, 2) else None)
                rotate_pe(e, c, kr_raw, "rot64", "kr")
                for tiles in (3, 2):
                    norm_pe(e, c, tiles)
                c.add("u", 5)
                e.wait_ge(u_ready, c["u"])

                def pair(i):
                    slab_there(e, c, 2)
                    wq = ring[:, 2, 0:1152].rearrange("p (k n) -> p k n", k=3)
                    wk = ring[:, 2, 1152:2176].rearrange("p (k n) -> p k n", k=2)
                    project(e, c, lambda k: wq[:, k, 256:384], latent[0:3], note="q")
                    project(e, c, lambda k: wq[:, k, 0:128], latent[0:3])
                    rotate_pe(e, c, raw[0], "rot64", "q")
                    project(e, c, lambda k: wq[:, k, 128:256], latent[0:3])
                    project(e, c, lambda k: wk[:, k, 0:128], latent[3:5])
                    project(e, c, lambda k: wk[:, k, 128:256], latent[3:5])
                    for v2 in range(2):
                        project_rows(e, c, lambda k: wk[:, k, 256:512], latent[3:5], (2 * v2, 2 * v2 + 1), 2 * P)
                    all_taken(e, c)
                    c.add("rope")
                    e.wait_ge(roped, c["rope"])
                    attend_pe(e, c, mla_units())
                    c.add("head", 2)
                c.add("rope")
                c.loop(e, 0, 4, pair)
                e.wait_ge(head_taken, c["head"])
                down_pe(e, c, mixed)

            def act(e, c):
                ada_norm_act(e, c, 4)
                for n in range(5):
                    copy_job(e, c, latent[n])
                copy_job(e, c, kr_raw)
                norm_act(e, c)
                norm_act(e, c)
                skip_jobs(c)
                c.add("rope")

                def pair(i):
                    rope_raw_act(e, c, raw[0], "raw0")
                    rope_note(c, "raw0")
                    copy_job(e, c, qn[0])
                    skip_jobs(c)
                    copy_job(e, c, qn[1])
                    copy_job(e, c, kn[0])
                    copy_job(e, c, kn[1])
                    for v2 in range(2):
                        copy_job(e, c, vM[:, 2 * v2:2 * v2 + 2, :].rearrange("p t n -> p (t n)"))
                    attend_act(e, c, mla_units(),
                               {3: [(outp[0][:, :].unsqueeze(1), A[:, ds(i * 2 + 8, 1), :])],
                                7: [(outp[1][:, :].unsqueeze(1), A[:, ds(i * 2 + 9, 1), :])]})
                c.loop(e, 0, 4, pair)
                down_act(e, c)

            def dve(e, c):
                ada_norm_dve(e, c, 4)
                for name, tiles, n in (("q_norm", latent[0:3], 384), ("kv_norm", latent[3:5], 256)):
                    clear_sumsq(e, c)
                    for t in tiles:
                        job_done(c, note="latent")
                        c.wait_mark(e, "latent")
                        add_squares(e, c, t.unsqueeze(1))
                    norm_root(e, c, n)
                    for k, t in enumerate(tiles):
                        e.scalar_tensor_tensor(out=t, in0=t, scalar=V(name, k, 1), in1=rinv, op0=ALU.mult,
                                               op1=ALU.mult).then_inc(u_ready, 1)
                job_done(c, note="kr")
                rope_dve(e, c, kr_raw, cos64, sin64, kr, "kr")

                def pair(i):
                    job_done(c, note="q")
                    skip_jobs(c)
                    rope_dve(e, c, raw[0], cos64, sin64, qr, "q")
                    skip_jobs(c, 5)
                    attend_dve(e, c, mla_units(), (128 + 64) ** -0.5)
                c.loop(e, 0, 4, pair)
                down_dve(e, c, 4)
            return sp, pe, act, dve

        def renorm():
            def pe(e, c):
                norm_pe(e, c)
                norm_pe(e, c)

            def dve(e, c):
                norm_root(e, c, D)
                clear_sumsq(e, c)
                for k in range(KT):
                    vlink(e, c, e.scalar_tensor_tensor(out=hT[:, k, :], in0=hT[:, k, :], scalar=V("final_g", k, 1),
                                                       in1=rinv, op0=ALU.mult, op1=ALU.mult))
                    add_squares(e, c, hT[:, k:k + 1, :])
                plain_norm_dve(e, c, "ln1")
            def act(e, c):
                norm_act(e, c)
                norm_act(e, c)
            return (lambda e, c: None), pe, act, dve

        uP = [A[:, n, :] for n in range(KT)]
        dq, dk = [A[:, 8, :], A[64:128, 9, :]], [A[:, 10, :], A[64:128, 11, :]]
        dv = A[:, 12:14, :].rearrange("p a b -> p (a b)")[:, 0:768].rearrange("p (t n) -> p t n", t=RES)
        dbias = [A[:, 14 + 3 * n:17 + 3 * n, :].rearrange("p a b -> p (a b)")[:, 0:GN * P] for n in range(2)]
        dil_out = [A[:, 20 + n, :] for n in range(3)]
        merged = [A[:, 28 + n, :] for n in range(KT)]

        def by_residue(ap):
            return ap.rearrange("p (n r) -> p r n", r=RES)

        def dil_units(jj):
            units = []
            o = slice(64 * jj, 64 * jj + 64)
            for r in range(RES):
                q = slice(r * P, (r + 1) * P)
                first = part([(dq[0][0:64, q], dk[0][0:64, :], 0, T)], T, dbias[jj][:, (3 - r) * P:(7 - r) * P],
                             [dv[:, b, 0:64] for b in range(RES)])
                second = part([(dq[0][64:128, q], dk[0][64:128, q], 0, P), (dq[1][:, q], dk[1][:, q], P, 2 * P)],
                              2 * P, dbias[jj][:, 7 * P:9 * P], [dv[:, r, 64:128], dv[:, r, 128:192]])
                units.append(dict(parts=[first, second], out=outp[jj][o, q]))
            return units

        def dilated():
            def sp(e, c):
                before_pairs = [c.n[f"bank{b}"] for b in range(2)]

                def pair(i):
                    for jj in range(2):
                        load(e, c, 2 * jj, a["dil_qk"][ds(i * 2 + jj, 1)].squeeze(0), SLAB)
                        load(e, c, 2 * jj + 1, a["dil_v"][ds(i * 2 + jj, 1)].squeeze(0), 192 * KT)
                        if isinstance(i, int) and jj == 0:
                            for b in range(2):
                                e.wait_ge(lin_full[b], before_pairs[b])
                        src = skew[ds(i * 2 + jj, 1), 127:127 + P * (BIAS_W - 1)].squeeze(0)\
                            .rearrange("(p w) -> p w", w=BIAS_W - 1)
                        c.wait_mark(e, f"bias{jj}")
                        e.dma_start(dbias[jj][:, 0:8 * P].rearrange("p (t n) -> p t n", n=P),
                                    src[:, 0:8 * GW].rearrange("p (t w) -> p t w", w=GW)[:, :, 0:P])\
                         .then_inc(bias_loaded[jj], 16)
                        e.dma_start(dbias[jj][:, 8 * P:9 * P], src[:, 8 * GW:8 * GW + P]).then_inc(bias_loaded[jj], 16)
                        skip_jobs(c, 3)
                        job_done(c, slot=2 * jj)
                        job_done(c)
                        job_done(c, slot=2 * jj + 1)
                        c.add("part", 2 * RES)
                        c.mark(f"bias{jj}", logits_ready, "part")
                c.loop(e, 0, DIL_HEADS // 2, pair)

            def pe(e, c):
                u_done(e, c)

                def pair(i):
                    for jj in range(2):
                        slab_there(e, c, 2 * jj)
                        w = ring[:, 2 * jj, :].rearrange("p (k n) -> p k n", k=KT)
                        for at in (0, 192):
                            project(e, c, lambda k: w[:, k, at:at + 128], u_tiles)
                            project(e, c, lambda k: w[:, k, at + 128:at + 192], u_tiles, row=64)
                        slab_there(e, c, 2 * jj + 1)
                        wv = ring[:, 2 * jj + 1, 0:192 * KT].rearrange("p (k n) -> p k n", k=KT)
                        if isinstance(i, int) and jj == 0:
                            e.wait_ge(perm_ready, KT)
                        for v2 in range(2):
                            project_rows(e, c, lambda k: wv[:, k, :], uP, (2 * v2, 2 * v2 + 1), 192)
                        all_taken(e, c)
                        attend_pe(e, c, dil_units(jj))
                        c.add("head")
                c.loop(e, 0, DIL_HEADS // 2, pair)
                e.wait_ge(head_taken, c["head"])
                branch_pe(e, c, dil_out)

            def act(e, c):
                def pair(i):
                    for jj in range(2):
                        for tiles in (dq, dk):
                            for n, rows in enumerate((slice(0, P), slice(64, P))):
                                o = bank_wait(e, c)
                                bank_take(c, e.activation(tiles[n].rearrange("p (r n) -> p r n", r=RES),
                                                          by_residue(o[rows, :]), ACT.Copy))
                        for v2 in range(2):
                            copy_job(e, c, dv[:, 2 * v2:2 * v2 + 2, :].rearrange("p t n -> p (t n)"), 384)
                        o = slice(64 * jj, 64 * jj + 64)
                        attend_act(e, c, dil_units(jj),
                                   {3: [(outp[jj][o, :].rearrange("p (a r n) -> p a r n", a=1, r=RES),
                                         A[o, ds(i + 20, 1), :].rearrange("p a (n r) -> p a r n", r=RES))]})
                c.loop(e, 0, DIL_HEADS // 2, pair)
                branch_act(e, c, 0)

            def dve(e, c):
                def pair(i):
                    for jj in range(2):
                        c.add(f"bias{jj}", 32)
                        e.wait_ge(bias_loaded[jj], c[f"bias{jj}"])
                        skip_jobs(c, 6)
                        attend_dve(e, c, dil_units(jj), 0.125)
                c.loop(e, 0, DIL_HEADS // 2, pair)
                branch_dve(e, c, 0)

            def sp2(e, c):
                sp(e, c)
                branch_sp(e, c, a["branch_a"], D + 384)
            return sp2, pe, act, dve

        def permute_pool(e):
            for k in range(KT):
                e.wait_ge(u_ready, u_before_dilated + k + 1)
                e.tensor_copy(uP[k].rearrange("p (r n) -> p r n", r=RES), by_residue(uT[:, k, :])).then_inc(perm_ready, 1)

        def branch_sp(e, c, src, width):
            def body(i):
                for j in range(2):
                    load(e, c, j, src[ds(i * 2 + j, 1)].squeeze(0), width)
                    job_done(c)
                    job_done(c, slot=j)
            c.loop(e, 0, KT // 2, body)

        def branch_pe(e, c, rhs):
            def body(i):
                for j in range(2):
                    slab_there(e, c, j)
                    project(e, c, lambda k: ring[:, j, k * P:(k + 1) * P], u_tiles)
                    project(e, c, lambda k: ring[:, j, D + k * P:D + (k + 1) * P], rhs)
            c.loop(e, 0, KT // 2, body)

        def branch_act(e, c, n):
            def body(i):
                for j in range(2):
                    o = bank_wait(e, c)
                    c.wait_mark(e, f"gate{j}")
                    bank_take(c, e.activation(W[:, 3 + j, :], o[:, :], ACT.Sigmoid, bias=Vr("b_gate", i * 2 + (j + 8 * n))))
                    job_done(c, note=f"gate{j}")
            c.marks.pop("gate0", None)
            c.marks.pop("gate1", None)
            c.loop(e, 0, KT // 2, body)

        def branch_dve(e, c, n):
            def body(i):
                for j in range(2):
                    job_done(c, note="gate")
                    c.wait_mark(e, "gate")
                    o = bank_wait(e, c)
                    dst = A[:, ds(i * 2 + (28 + j), 1), :]
                    if n == 0:
                        bank_take(c, e.tensor_tensor(dst, o[:, :].unsqueeze(1), W[:, 3 + j:4 + j, :], ALU.mult))
                    else:
                        bank_take(c, e.tensor_tensor(W[:, 5 + j, :], o[:, :], W[:, 3 + j, :], ALU.mult), note="y")
                        c.wait_mark(e, "y")
                        e.tensor_tensor(dst, dst, W[:, 5 + j:6 + j, :], ALU.add).then_inc(merged_ready, 1)
            c.loop(e, 0, KT // 2, body)

        flatW = W[:, :, :].rearrange("p a b -> p (a b)")
        padded = [flatW[:, 1024 * n:1024 * n + 16 + T] for n in range(4)]
        pooled = [A[:, n, :] for n in range(KT)]
        pool_y = [A[:, 8 + n, :] for n in range(KT)]

        def pooling():
            def sp(e, c):
                for n in range(3):
                    load(e, c, n, a["pool_in"][n], SLAB)
                load(e, c, 3, a["pool_w"], 2048)
                for n in range(8):
                    job_done(c, slot=n // 3)
                for n in range(8):
                    job_done(c, slot=3)
                branch_sp(e, c, a["branch_b"], 2 * D)

            def pe(e, c):
                for n in range(8):
                    if n % 3 == 0:
                        slab_there(e, c, n // 3)
                    w = ring[:, n // 3, :].rearrange("p (k n) -> p k n", k=KT)
                    project(e, c, lambda k: w[:, k, (n % 3) * P:(n % 3 + 1) * P], u_tiles)
                slab_there(e, c, 3)
                w = ring[:, 3, 0:2048].rearrange("p (g k n) -> p g k n", g=4, k=2)
                for n in range(8):
                    if n % 2 == 0:
                        e.wait_ge(gated, c["gated"] + n + 2)
                    g = n // 2
                    project(e, c, lambda k: w[:, g, k, (n % 2) * P:(n % 2 + 1) * P], pooled[2 * g:2 * g + 2])
                c.add("gated", 8)
                all_taken(e, c)
                branch_pe(e, c, pool_y)

            def act(e, c):
                for n in range(8):
                    o = bank_wait(e, c)
                    if n < 2:
                        e.wait_ge(zeros_ready, 1)
                    after(e, gated, c["gated"] + n - 1 if n >= 2 else 0)
                    bank_take(c, e.activation(padded[n % 2][:, 16:16 + T], o[:, :], ACT.Copy))
                c.add("gated", 8)
                for n in range(8):
                    o = bank_wait(e, c)
                    bank_take(c, e.activation(pool_y[n], o[:, :], ACT.Copy, scale=V("pool_scale", n, 1)))
                branch_act(e, c, 1)

            def dve(e, c):
                for n in range(3):
                    vlink(e, c, e.memset(padded[n][:, 0:16], 0.0))
                e.memset(padded[3][:, 0:16], 0.0).then_inc(zeros_ready, 1)
                e.wait_ge(zeros_ready, 1)
                for n in range(8):
                    job_done(c, note="x")
                    c.wait_mark(e, "x")
                    x = cur = padded[n % 2]
                    step = 1
                    for k in range(n // 2 + 1):
                        nxt = padded[2 + k % 2]
                        vlink(e, c, e.tensor_tensor(nxt[:, 16:16 + T], cur[:, 16:16 + T],
                                                    cur[:, 16 - step:16 - step + T], ALU.add))
                        cur, step = nxt, 2 * step
                    vlink(e, c, e.scalar_tensor_tensor(out=pooled[n], in0=cur[:, 16:16 + T], scalar=1.0 / step,
                                                       in1=x[:, 16:16 + T], op0=ALU.mult, op1=ALU.subtract))
                    vlink(e, c, e.tensor_tensor(stat16, cur[:, 16:32], C("poolfix", P, 16 * (n // 2), 16), ALU.mult))
                    e.tensor_tensor(pooled[n][:, 0:16], stat16, x[:, 16:32], ALU.subtract).then_inc(gated, 1)
                    c.add("gated")
                skip_jobs(c, 8)
                branch_dve(e, c, 1)
            return sp, pe, act, dve

        stat16 = small[:, 11, 0:16]

        xs = [A[:, n, :] for n in range(KT)]
        bT, cT = [A[:, 8, :], A[:, 9, :]], [A[:, 10, :], A[:, 11, :]]
        bN = [A[:, 12 + g, :] for g in range(2)]
        xdt = [A[:, 14 + 2 * n:16 + 2 * n, :].rearrange("p a b -> p (a b)") for n in range(QT)]
        state = [[A[:, 22 + 2 * n + g, :] for g in range(2)] for n in range(3)]
        acsT = W[0:16, 0, :]
        cb = [W[:, 1 + g, :] for g in range(2)]
        xdec = [W[:, 3 + 2 * n:5 + 2 * n, :].rearrange("p a b -> p (a b)") for n in range(2)]
        m_dt, m_nacs, m_dec, m_tot = small[:, 5, :], small[:, 6, :], small[:, 7, :], small[:, 8, :]
        m_a, m_expA = small[:, 9, :], small[:, 10, 0:16]

        def by_chunk(ap):
            return ap.rearrange("p (t n) -> p t n", t=QT)

        def head_wide(col, first, n):
            return col[:, first:first + n].unsqueeze(2).to_broadcast([P, n, 64])

        def ssd():
            def sp(e, c):
                for n in range(4):
                    load(e, c, n, a["xbc"][n], SLAB)
                for n in range(12):
                    job_done(c, slot=n // 3)
                load(e, c, 0, a["dt"], KT * 16)
                job_done(c, slot=0)
                skip_jobs(c, 2 + 8 + 2 + 2 + 6)
                for n in range(3):
                    load(e, c, 1 + n, a["z"][n], SLAB)
                for j in range(8):
                    skip_jobs(c, 3)
                    job_done(c, slot=1 + j // 3)
                branch_sp(e, c, a["branch_c"], 2 * D)

            def y_pe(e, c, j):
                g = j // 4
                c.add("ssdM", 2)
                e.wait_ge(ssd_dve, c["ssdM"])
                after(e, ssd_ready, j)
                for hh in range(2):
                    h = 2 * j + hh
                    M = W[:, 3 + 2 * (j % 2) + hh, :]
                    for k in range(QT):
                        e.matmul(outp[0][64 * hh:64 * hh + 64, k * P:(k + 1) * P], xdt[k][:, h * 64:(h + 1) * 64],
                                 M[:, k * P:(k + 1) * P], start=True, stop=True)
                for k in range(1, QT):
                    last = e.matmul(outp[1][:, k * P:(k + 1) * P], state[k - 1][g][:, (j % 4) * P:(j % 4 + 1) * P],
                                    cT[g][:, k * P:(k + 1) * P], start=True, stop=True)
                last.then_inc(ssd_pe, 1)

            def pe(e, c):
                for n in range(12):
                    if n % 3 == 0:
                        slab_there(e, c, n // 3)
                    w = ring[:, n // 3, :].rearrange("p (k n) -> p k n", k=KT)
                    project(e, c, lambda k: w[:, k, (n % 3) * P:(n % 3 + 1) * P], u_tiles)
                slab_there(e, c, 0)
                w = ring[:, 0, 0:KT * 16].rearrange("p (k n) -> p k n", k=KT)
                project_rows(e, c, lambda k: w[:, k, :], u_tiles, range(QT), 16)
                e.wait_ge(dt_ready, 1)
                o = bank_open(e, c)
                e.matmul(o[:, 0:64], C("triu"), m_a, start=True, stop=True)
                bank_close(c, e.matmul(o[:, 64:128], C("ones"), m_a, start=True, stop=True))
                o = bank_open(e, c)
                for k in range(QT):
                    last = e.matmul(o[0:16, k * P:(k + 1) * P], by_chunk(m_a)[:, k, :], C("triu"), start=True, stop=True)
                bank_close(c, last)
                c.add("silu", 12)
                e.wait_ge(silu_done, c["silu"])
                for k in range(QT):
                    for half in range(2):
                        o = bank_open(e, c)
                        for n in range(4):
                            last = e.matmul(o[:, n * P:(n + 1) * P], xs[4 * half + n][:, k * P:(k + 1) * P], C("ident"),
                                            start=True, stop=True)
                        bank_close(c, last)
                for g in range(2):
                    o = bank_open(e, c)
                    for k in range(QT):
                        last = e.matmul(o[:, k * P:(k + 1) * P], bT[g][:, k * P:(k + 1) * P], C("ident"),
                                        start=True, stop=True)
                    bank_close(c, last)
                for g in range(2):
                    o = bank_open(e, c)
                    for k in range(QT):
                        last = e.matmul(o[:, k * P:(k + 1) * P], bT[g][:, k * P:(k + 1) * P],
                                        cT[g][:, k * P:(k + 1) * P], start=True, stop=True)
                    bank_close(c, last)
                for k in range(3):
                    e.wait_ge(ssd_dve, k + 1)
                    for g in range(2):
                        o = bank_open(e, c)
                        bank_close(c, e.matmul(o[:, :], bN[g][:, k * P:(k + 1) * P], xdec[k % 2][:, g * T:(g + 1) * T],
                                               start=True, stop=True))
                c.add("ssdM", 3)
                for j in range(8):
                    for hh in range(2):
                        o = bank_open(e, c)
                        bank_close(c, e.matmul(o[:, :], C("sel", 16, (2 * j + hh) * P, P), acsT, start=True, stop=True))
                    o = bank_open(e, c)
                    bank_close(c, e.matmul(o[:, :], C("selpair", 16, j * P, P), acsT, start=True, stop=True))
                    if j % 3 == 0:
                        slab_there(e, c, 1 + j // 3)
                    w = ring[:, 1 + j // 3, :].rearrange("p (k n) -> p k n", k=KT)
                    project(e, c, lambda k: w[:, k, (j % 3) * P:(j % 3 + 1) * P], u_tiles)
                    if j > 0:
                        y_pe(e, c, j - 1)
                y_pe(e, c, 7)
                for g in range(2):
                    norm_pe(e, c, 4)
                c.add("u", 8)
                e.wait_ge(u_ready, c["u"])
                branch_pe(e, c, xs)

            def act(e, c):
                for n in range(12):
                    o = bank_wait(e, c)
                    e.activation(W[:, 3 + n % 2, :], o[:, :], ACT.Identity, bias=V("conv_b", n, 1),
                                 scale=V("conv_w", 36 + n, 1)).then_inc(tap_done, 1)
                    job_done(c, note="conv")
                    c.wait_mark(e, "conv")
                    e.activation(A[:, n, :], W[:, 3 + n % 2, :], ACT.Silu).then_inc(silu_done, 1)
                c.add("tap", 12)
                c.add("silu", 12)
                job_done(c)
                softplus_act(e, c)
                e.activation(m_expA, V("a_log"), ACT.Exp).then_inc(ssd_exp, 1)
                skip_jobs(c)
                copy_job(e, c, acsT, T, 16)
                e.wait_ge(forget_ready, 4)
                e.activation(m_dec, m_dec, ACT.Exp).then_inc(ssd_exp, 1)
                e.activation(m_tot, m_tot, ACT.Exp).then_inc(ssd_exp, 1)
                skip_jobs(c, 8)
                for g in range(2):
                    copy_job(e, c, bN[g])
                for g in range(2):
                    copy_job(e, c, cb[g])
                skip_jobs(c, 6)
                for j in range(8):
                    for hh in range(2):
                        h = 2 * j + hh
                        R = W[:, 3 + 2 * (j % 2) + hh, :]
                        job_done(c, note="decay")
                        c.wait_mark(e, "decay")
                        for k in range(QT):
                            ins = e.activation(R[:, k * P:(k + 1) * P], R[:, k * P:(k + 1) * P], ACT.Exp,
                                               bias=by_chunk(m_nacs)[:, k, h:h + 1])
                        ins.then_inc(ssd_exp, 1)
                    o = bank_wait(e, c)
                    after(e, ssd_ready, j - 1)
                    bank_take(c, e.activation(W[:, 7 + j % 2, :], o[:, :], ACT.Exp))
                    o = bank_wait(e, c)
                    after(e, ssd_ready, j)
                    bank_take(c, e.activation(W[:, 9, :], o[:, :], ACT.Silu))
                norm_act(e, c)
                norm_act(e, c)
                branch_act(e, c, 2)

            def dve(e, c):
                for n in range(12):
                    o = bank_wait(e, c)
                    e.wait_ge(tap_done, n + 1)
                    buf = W[:, 3 + n % 2, :]
                    for d in (1, 2, 3):
                        ins = e.scalar_tensor_tensor(out=buf[:, d:T], in0=o[:, 0:T - d],
                                                     scalar=V("conv_w", 12 * (3 - d) + n, 1), in1=buf[:, d:T],
                                                     op0=ALU.mult, op1=ALU.add)
                        if d < 3:
                            vlink(e, c, ins)
                    bank_take(c, ins)
                o = bank_wait(e, c)
                bank_take(c, e.tensor_tensor(by_chunk(small[:, 0, :]), by_chunk(o[:, 0:64]),
                                             V("dt_bias").unsqueeze(1).to_broadcast([P, QT, 16]), ALU.add), note="dt")
                c.wait_mark(e, "dt")
                softplus_dve_in(e, c)
                vlink(e, c, e.scalar_tensor_tensor(out=m_dt, in0=small[:, 0, :], scalar=0.0, in1=small[:, 2, :],
                                                   op0=ALU.max, op1=ALU.add))
                e.wait_ge(ssd_exp, 1)
                e.scalar_tensor_tensor(out=by_chunk(m_a), in0=by_chunk(m_dt), scalar=-1.0,
                                       in1=m_expA.unsqueeze(1).to_broadcast([P, QT, 16]), op0=ALU.mult,
                                       op1=ALU.mult).then_inc(dt_ready, 1)
                o = bank_wait(e, c)
                vlink(e, c, e.tensor_scalar(m_nacs, o[:, 0:64], -1.0, None, ALU.mult))
                vlink(e, c, e.tensor_copy(m_tot, o[:, 64:128]))
                bank_take(c, e.tensor_tensor(m_dec, m_nacs, o[:, 64:128], ALU.add), note="dec")
                c.wait_mark(e, "dec")
                e.tensor_copy(small[:, 11, 16:17], m_dec[:, 0:1]).then_inc(forget_ready, 1)
                skip_jobs(c)
                for k in range(QT):
                    for half in range(2):
                        o = bank_wait(e, c)
                        bank_take(c, e.tensor_tensor(
                            xdt[k][:, half * T:(half + 1) * T].rearrange("p (h d) -> p h d", d=64),
                            o[:, :].rearrange("p (h d) -> p h d", d=64),
                            head_wide(by_chunk(m_dt)[:, k, :], 8 * half, 8), ALU.mult))
                all_x = {b: c.n[f"bank{b}"] for b in range(2)}
                skip_jobs(c, 4)
                e.wait_ge(ssd_exp, 3)
                for b in range(2):
                    e.wait_ge(lin_taken[b], all_x[b])

                def decayed(k):
                    e.tensor_tensor(xdec[k % 2].rearrange("p (h d) -> p h d", d=64),
                                    xdt[k].rearrange("p (h d) -> p h d", d=64),
                                    head_wide(by_chunk(m_dec)[:, k, :], 0, 16), ALU.mult).then_inc(ssd_dve, 1)
                decayed(0)
                decayed(1)
                for k in range(3):
                    for g in range(2):
                        dst = state[k][g]
                        if k:
                            vlink(e, c, e.tensor_tensor(dst.rearrange("p (h d) -> p h d", d=64),
                                                        state[k - 1][g].rearrange("p (h d) -> p h d", d=64),
                                                        head_wide(by_chunk(m_tot)[:, k, :], 8 * g, 8), ALU.mult))
                        o = bank_wait(e, c)
                        if k:
                            bank_take(c, e.tensor_tensor(dst, dst, o[:, :], ALU.add), note="state")
                        else:
                            bank_take(c, e.tensor_copy(dst, o[:, :]), note="state")
                        c.wait_mark(e, "state")
                    if k == 0:
                        decayed(2)
                for j in range(8):
                    g = j // 4
                    for hh in range(2):
                        o = bank_wait(e, c)
                        R = W[:, 3 + 2 * (j % 2) + hh, :]
                        after(e, ssd_pe, j - 1)
                        bank_take(c, e.tensor_tensor(by_chunk(R), by_chunk(o[:, :]),
                                                     C("below").unsqueeze(1).to_broadcast([P, QT, P]), ALU.add))
                    skip_jobs(c, 2)
                    for hh in range(2):
                        R = W[:, 3 + 2 * (j % 2) + hh, :]
                        e.wait_ge(ssd_exp, 3 + 2 * j + hh + 1)
                        e.tensor_tensor(R, R, cb[g], ALU.mult).then_inc(ssd_dve, 1)
                    if j > 0:
                        y_dve(e, c, j - 1)
                y_dve(e, c, 7)
                for g in range(2):
                    clear_sumsq(e, c)
                    for n in range(4):
                        add_squares(e, c, A[:, 4 * g + n:4 * g + n + 1, :])
                    norm_root(e, c, 512)
                    for n in range(4 * g, 4 * g + 4):
                        e.scalar_tensor_tensor(out=xs[n], in0=xs[n], scalar=V("ssd_norm", n, 1), in1=rinv,
                                               op0=ALU.mult, op1=ALU.mult).then_inc(u_ready, 1)
                branch_dve(e, c, 2)

            def y_dve(e, c, j):
                e.wait_ge(ssd_pe, j + 1)
                E = W[:, 7 + j % 2, :]
                vlink(e, c, e.scalar_tensor_tensor(out=xs[j], in0=xs[j], scalar=V("ssd_d", j, 1), in1=outp[0][:, :],
                                                   op0=ALU.mult, op1=ALU.add))
                for b in range(2):
                    e.wait_ge(lin_taken[b], c.n[f"bank{b}"] - (2 if j < 7 else 0))
                vlink(e, c, e.tensor_tensor(E[:, P:T], outp[1][:, P:T], E[:, P:T], ALU.mult))
                vlink(e, c, e.tensor_tensor(xs[j][:, P:T], xs[j][:, P:T], E[:, P:T], ALU.add))
                e.tensor_tensor(xs[j], xs[j], W[:, 9, :], ALU.mult).then_inc(ssd_ready, 1)
                e.wait_ge(ssd_ready, j + 1)
            return sp, pe, act, dve

        def output_projection():
            def pe(e, c):
                e.wait_ge(merged_ready, 2 * KT)
                down_pe(e, c, merged)
            return (lambda e, c: down_sp(e, c, a["w_o"], D), pe, lambda e, c: down_act(e, c),
                    lambda e, c: down_dve(e, c, None))

        def conv_ffn():
            def sp(e, c):
                up_sp(e, c, a["up2"])
                down_sp(e, c, a["down2"], FF)

            def pe(e, c):
                norm_pe(e, c)
                up_pe(e, c)
                c.add("gated", FT)
                e.wait_ge(gated, c["gated"])
                down_pe(e, c, hidden)

            def act(e, c):
                def body(i):
                    for j in range(2):
                        for g in range(2):
                            o = bank_wait(e, c)
                            after(e, gated, c["gated"] - 1)
                            e.activation(W[:, 3 + 2 * j + g, :], o[:, :], ACT.Identity,
                                         bias=Vr("ffn_cb", i * 2 + (j + FT * g)),
                                         scale=Vr("ffn_cw", i * 2 + (j + FT * g + 4 * FT))).then_inc(tap_done, 1)
                            job_done(c, note=f"conv{g}")
                        c.wait_mark(e, "conv0")
                        e.activation(W[:, 7 + j, :], W[:, 3 + 2 * j, :], ACT.Silu).then_inc(silu_done, 1)
                        c.add("gated")
                norm_act(e, c)
                c.loop(e, 0, FT // 2, body)
                down_act(e, c)

            def dve(e, c):
                plain_norm_dve(e, c, "ln2")
                c.add("tap", 12)
                c.add("silu", 12)

                def body(i):
                    for j in range(2):
                        for g in range(2):
                            o = bank_wait(e, c)
                            c.add("tap")
                            e.wait_ge(tap_done, c["tap"])
                            buf = W[:, 3 + 2 * j + g, :]
                            for d in (1, 2):
                                ins = e.scalar_tensor_tensor(out=buf[:, d:T], in0=o[:, 0:T - d],
                                                             scalar=Vr("ffn_cw", i * 2 + (j + FT * g + 2 * FT * (2 - d))),
                                                             in1=buf[:, d:T], op0=ALU.mult, op1=ALU.add)
                                if d == 1:
                                    vlink(e, c, ins)
                            bank_take(c, ins, note="conv")
                        c.wait_mark(e, "conv")
                        c.add("silu")
                        e.wait_ge(silu_done, c["silu"])
                        e.tensor_tensor(A[:, ds(i * 2 + j, 1), :], W[:, 4 + 2 * j:5 + 2 * j, :], W[:, 7 + j:8 + j, :],
                                        ALU.mult).then_inc(gated, 1)
                        c.add("gated")
                c.loop(e, 0, FT // 2, body)
                down_dve(e, c, None)
            return sp, pe, act, dve

        def last_norm():
            def sp(e, c):
                for k in range(KT):
                    e.wait_ge(result_ready, k + 1)
                    e.dma_start(out[k], A[:, k, :]).then_inc(result_stored, 16)
                e.wait_ge(result_stored, 16 * KT)

            def dve(e, c):
                norm_root(e, c, D)
                for k in range(KT):
                    e.scalar_tensor_tensor(out=A[:, k, :], in0=hT[:, k, :], scalar=V("final2", k, 1), in1=rinv,
                                           op0=ALU.mult, op1=ALU.mult).then_inc(result_ready, 1)
            return sp, norm_pe, norm_act, dve

        def raw_dump():
            def sp(e, c):
                e.wait_ge(result_ready, 1)
                e.dma_start(out.rearrange("k p t -> p k t"), A[:, 28:36, :] if stop in (9, 10, 11) else hT[:, :, :]).then_inc(result_stored, 16)
                e.wait_ge(result_stored, 16)

            def dve(e, c):
                e.tensor_copy(W[:, 1, :], W[:, 0, :]).then_inc(result_ready, 1)
            return sp, (lambda e, c: None), (lambda e, c: None), dve

        stages = [
            (prologue_sp, prologue_pe, prologue_act, prologue_dve),
            ffn(0, 0, ((0, 1), (0, 2))), hybrid(), ffn(2, 1, ((1, 0),)),
            ffn(3, 2, ((1, 1), (1, 2))), mla(), ffn(5, 3, ()),
            renorm(), dilated(), pooling(), ssd(), output_projection(), conv_ffn(), last_norm(),
        ]
        u_before_dilated = 6 * KT + 5
        if stop is not None:
            stages = stages[:stop] + [raw_dump()]

        block = ctx.enter_context(nc.Block())

        @block.sync
        def _(sp):
            c = Counts()
            for run, _, _, _ in stages:
                run(sp, c)

        @block.tensor
        def _(pe):
            c = Counts()
            for _, run, _, _ in stages:
                run(pe, c)

        @block.scalar
        def _(act):
            c = Counts()
            for _, _, run, _ in stages:
                run(act, c)

        @block.vector
        def _(dve):
            c = Counts()
            for _, _, _, run in stages:
                run(dve, c)

        @block.gpsimd
        def _(pool):
            if stop is None or stop > 8:
                permute_pool(pool)


def _bucket(dist):
    dist = np.asarray(dist)
    f = np.float32
    nf = np.maximum(dist, 1).astype(f)
    large = 16 + (np.log(nf / f(16)) / f(math.log(2048 / 16)) * f(16)).astype(np.int32)
    return np.where(dist < 16, dist, np.minimum(large, 31))


def _inv_freq(rot, theta):
    x = np.float32(-math.log(theta) * 2.0) * np.arange(rot // 2, dtype=np.float32) / np.float32(rot)
    return np.exp(x.astype(np.float64)).astype(np.float32)


def _rotation(rot, period=64):
    m = np.zeros((P, P), np.float32)
    for base in range(0, P, period):
        for j in range(rot // 2):
            m[base + j + rot // 2, base + j] = -1.0
            m[base + j, base + j + rot // 2] = 1.0
    return m


def _inv_freq_column(rot, theta):
    col = np.zeros((P, 1), np.float32)
    for base in (0, 64):
        col[base:base + rot // 2, 0] = _inv_freq(rot, theta)
        col[base + rot // 2:base + rot, 0] = _inv_freq(rot, theta)
    return col


def shape_constants():
    c = np.zeros((P, CONST_W), np.float32)

    def put(name, value):
        at, w = CONST[name]
        value = np.asarray(value, np.float32)
        c[:value.shape[0], at:at + w] = value
    i, j = np.arange(P)[:, None], np.arange(P)[None, :]
    put("ident", np.eye(P))
    put("ones", np.ones((P, P)))
    put("triu", i <= j)
    put("causal", np.concatenate([np.zeros((P, T - P)), np.where(j > i, NEG, 0)], 1))
    put("chunked", np.concatenate([np.zeros((P, T - P)), np.where(j // 64 > i // 64, NEG, 0)], 1))
    put("below", np.where(j < i, NEG, 0))
    put("rot16", _rotation(16))
    put("rot64", _rotation(64))
    fix = np.concatenate([1.0 / np.minimum(np.arange(16) + 1, w) for w in (2, 4, 8, 16)])
    put("poolfix", np.tile(fix, (P, 1)))
    sel = np.zeros((16, SSD_HEADS, P))
    pair = np.zeros((16, SSD_HEADS // 2, P))
    for h in range(SSD_HEADS):
        sel[h, h] = 1
        pair[h, h // 2, 64 * (h % 2):64 * (h % 2) + 64] = 1
    put("sel", sel.reshape(16, -1))
    put("selpair", pair.reshape(16, -1))
    put("foxrow", np.concatenate([8 * np.eye(8), np.zeros((8, 8))], 0).repeat(1, 1) @ np.eye(8, 16))
    put("foxone", np.concatenate([np.zeros((8, 8)), -np.eye(8)], 0) @ np.eye(8, 16))
    key = np.zeros((16, 2))
    key[8:, 0] = 8
    key[:8, 1] = 1
    put("foxkey", key)
    return c


def distance_onehots():
    m = np.arange(GW) - (P - 1)
    out = np.zeros((33, GN, GW), np.float32)
    for t in range(GN):
        if t < 7:
            dist = -RES * m + (3 - t)
            ok = (dist >= 0) & (dist <= 128)
        else:
            dist = -RES * m
            ok = (dist >= 0) & ((m % 4 == 0) | (t == 7))
        b = np.where(ok, _bucket(np.maximum(dist, 0)), 32)
        out[b, t, np.arange(GW)] = 1
    return out.reshape(33, BIAS_W)


def tiles(w):
    k, m = w.shape
    return w.reshape(k // P, P, m // P, P).transpose(2, 1, 0, 3).reshape(m // P, P, k)


def slab(w):
    k, m = w.shape
    return w.reshape(k // P, P, m).transpose(1, 0, 2).reshape(P, k // P * m)


def slabs3(w):
    out = []
    for at in range(0, w.shape[1], 384):
        piece = w[:, at:at + 384]
        if piece.shape[1] < 384:
            piece = np.concatenate([piece, w[:, :384 - piece.shape[1]]], 1)
        out.append(slab(piece))
    return np.stack(out)


def columns(v):
    return v.reshape(-1, P).T


def layout(x):
    w_in, w2 = x["hyb_w_in"][0], x["w_in_2"][0]
    fq, fk, fv, ff, dq, dk, dv, iq, iw, ik = np.split(w_in, np.cumsum([512, 512, 512, 8, 512, 512, 512, 256, 4]), 1)
    q2, k2, v2, pool_in, z, xbc, dt, gates = np.split(w2, np.cumsum([1152, 1152, 1152, 1024, 1024, 1536, 16]), 1)

    def pairs(q, k, v):
        return np.concatenate([tiles(q), tiles(k), tiles(v)], 2)

    def up_gate(g, u):
        return np.concatenate([tiles(g), tiles(u)], 2)

    uq = x["mla_w_uq"][0].reshape(384, 8, 192)
    ukv = x["mla_w_ukv"][0].reshape(256, 8, 256)
    mla_up = []
    for i in range(4):
        h = (2 * i, 2 * i + 1)
        wq = np.concatenate([uq[:, h[0], :128], uq[:, h[1], :128], uq[:, h[0], 128:], uq[:, h[1], 128:]], 1)
        wk = np.concatenate([ukv[:, h[0], :128], ukv[:, h[1], :128], ukv[:, h[0], 128:], ukv[:, h[1], 128:]], 1)
        mla_up.append(np.concatenate([slab(wq), slab(wk)], 1))
    md = x["mla_w_down"][0]
    q3, k3, v3 = (w.reshape(D, 3, DIL_HEADS, HD) for w in (q2, k2, v2))
    g3 = [gates[:, n * D:(n + 1) * D] for n in range(3)]
    rel = np.zeros((P, 18), np.float32)
    rel[:32] = x["rel_bias_2"]
    vec = [columns(x["c"]), columns(x["ada_b"]), columns(x["norm_g"]), columns(x["final_g"]), columns(x["ln1_g_2"]),
           columns(x["ln2_g_2"]), columns(x["final_g_2"]), columns(x["mla_q_norm"]), columns(x["mla_kv_norm"]),
           columns(x["b_gate_2"]), columns(x["pool_scale_2"]), columns(x["ssd_conv_w_2"]),
           columns(x["ssd_conv_b_2"]), columns(x["ssd_norm_w_2"]), columns(np.repeat(x["ssd_d_2"][0], HD)),
           columns(x["ffn_conv_w_2"]), columns(x["ffn_conv_b_2"]), np.tile(x["ssd_dt_bias_2"], (P, 1)),
           np.tile(x["ssd_a_log_2"], (P, 1)), np.tile(x["fox_b_f"], (P, 2)), rel, _inv_freq_column(16, 500000.0),
           _inv_freq_column(64, 10000.0)]
    gate_w, up_w, down_w = (x[f"ffn_w_{n}"].reshape(4, *x[f"ffn_w_{n}"].shape[2:]) for n in ("gate", "up", "down"))
    return {
        "constants": shape_constants(),
        "onehot": distance_onehots(),
        "vectors": np.concatenate(vec, 1),
        "positions": x["positions"],
        "xT": x["x"][0].T.reshape(KT, P, T).transpose(1, 0, 2),
        "ada": x["ada_w"].reshape(2, KT, P, 3, 8, 384).transpose(0, 3, 4, 2, 1, 5).reshape(2, 3, 8, P, SLAB),
        "up": np.stack([up_gate(gate_w[n], up_w[n]) for n in range(4)]),
        "down": np.stack([tiles(down_w[n]) for n in range(4)]),
        "idx": slab(np.concatenate([iq, ik, ik], 1)),
        "idx_small": slab(np.concatenate([ff, ff, iw], 1)),
        "fox": pairs(fq, fk, fv),
        "dsa": pairs(dq, dk, dv),
        "hyb_out": tiles(x["hyb_w_out"][0]),
        "mla_down": np.stack([slab(md[:, :384]), slab(np.concatenate([md[:, 384:704], md[:, 640:704]], 1))]),
        "mla_up": np.stack(mla_up),
        "mla_out": tiles(x["mla_w_out"][0]),
        "dil_qk": np.stack([slab(np.concatenate([q3[:, :, j].reshape(D, 192), k3[:, :, j].reshape(D, 192)], 1))
                            for j in range(DIL_HEADS)]),
        "dil_v": np.stack([slab(v3[:, :, j].reshape(D, 192)) for j in range(DIL_HEADS)]),
        "branch_a": up_gate(g3[0], x["w_a_2"][0]),
        "branch_b": up_gate(g3[1], x["w_b_2"][0]),
        "branch_c": up_gate(g3[2], x["w_c_2"][0]),
        "pool_in": slabs3(pool_in),
        "pool_w": np.concatenate([slab(x["pool_w_2"][0, g]) for g in range(4)], 1),
        "xbc": slabs3(xbc),
        "dt": slab(dt),
        "z": slabs3(z),
        "w_o": tiles(x["w_o_2"][0]),
        "up2": up_gate(x["ffn_w_up_2"][0][:, :FF], x["ffn_w_up_2"][0][:, FF:]),
        "down2": tiles(x["ffn_w_down_2"][0]),
    }


def kernel(**inputs):
    import concourse.bacc as _bacc
    from concourse.bass_utils import run_bass_kernel_spmd as _run

    nc = _bacc.Bacc("TRN2", target_bir_lowering=False, num_devices=1)
    arrays, aps = {}, {}
    for name, value in layout({k: np.asarray(v) for k, v in inputs.items()}).items():
        value = np.ascontiguousarray(value)
        arrays[f"in_{name}"] = value
        aps[name] = nc.dram_tensor(f"in_{name}", value.shape, mybir.dt.from_np(value.dtype), kind="ExternalInput").ap()
    out = nc.dram_tensor("out_T", [KT, P, T], F32, kind="ExternalOutput").ap()
    build_program(nc, aps, out)
    r = _run(nc, [arrays], core_ids=[0])
    return np.ascontiguousarray(r.results[0]["out_T"].reshape(D, T).T).reshape(1, T, D)
```

```python
from collections import defaultdict
from contextlib import ExitStack
import math

import numpy as np

import concourse.bass as bass
from concourse import mybir

ALU = mybir.AluOpType
ACT = mybir.ActivationFunctionType
F32 = mybir.dt.float32
I32 = mybir.dt.int32
ds = bass.ds

P = 128
T = 512
D = 1024
KT = D // P
QT = T // P
FF = 2816
FT = FF // P
SLAB = 3 * D
SLOTS = 4
HD = 64
TOPK = 128
NEG = -1.0e30
IDX_SCALE = 0.125
GONE = -3.0e38
EPS = 1e-6
SSD_HEADS = 16
DIL_HEADS = 6
RES = 4
GW = 256
GN = 9
BIAS_W = GN * GW

CONST = {}


def _const_columns():
    at = 0
    for name, width in (("ident", P), ("ones", P), ("triu", P), ("causal", T), ("chunked", T), ("below", P),
                        ("rot16", P), ("rot64", P), ("poolfix", 64),
                        ("foxrow", 16), ("foxone", 16), ("foxkey", 2), ("sel", SSD_HEADS * P),
                        ("selpair", SSD_HEADS // 2 * P)):
        CONST[name] = (at, width)
        at += width
    return at


CONST_W = _const_columns()

VEC = {}


def _vec_columns():
    at = 0
    for name, width in (("c", 8), ("ada_b", 144), ("norm_g", 48), ("final_g", 8), ("ln1", 8), ("ln2", 8),
                        ("final2", 8), ("q_norm", 3), ("kv_norm", 2), ("b_gate", 24), ("pool_scale", 8),
                        ("conv_w", 48), ("conv_b", 12), ("ssd_norm", 8), ("ssd_d", 8), ("ffn_cw", 132),
                        ("ffn_cb", 44), ("dt_bias", 16), ("a_log", 16), ("b_f", 16), ("rel", 18),
                        ("invf16", 1), ("invf64", 1), ("eps", 1)):
        VEC[name] = (at, width)
        at += width
    return at


VEC_W = _vec_columns()


class Counts:

    def __init__(self):
        self.n = defaultdict(int)
        self.marks = {}
        self.step = {}
        self.it = None

    def value(self, what, n):
        step = self.step.get(what, 0) if self.it is not None else 0
        return self.it * step + n if step else n

    def __getitem__(self, what):
        return self.value(what, self.n[what])

    def add(self, what, times=1):
        self.n[what] += times

    def mark(self, name, sem, what):
        self.marks[name] = (sem, what, self.n[what])

    def wait_mark(self, eng, name):
        if name in self.marks:
            sem, what, n = self.marks[name]
            after(eng, sem, self.value(what, n))

    def loop(self, eng, first, end, body):
        before = dict(self.n)
        body(first)
        step = {k: v - before.get(k, 0) for k, v in self.n.items()}
        assert step.get("job", 0) % 2 == 0
        if end - first == 1:
            return
        mid, old = dict(self.n), dict(self.marks)
        with eng.Fori(first + 1, end) as i:
            self.it, self.step = i - (first + 1), step
            body(i)
            self.it = None
        assert all(self.n[k] - mid.get(k, 0) == step.get(k, 0) for k in self.n)
        for k in self.n:
            self.n[k] = before.get(k, 0) + step.get(k, 0) * (end - first)
        for name, (sem, what, n) in self.marks.items():
            if old.get(name) != (sem, what, n):
                self.marks[name] = (sem, what, n + step.get(what, 0) * (end - first - 2))


def after(eng, sem, count):
    if isinstance(count, int) and count <= 0:
        return
    eng.wait_ge(sem, count)


def build_program(nc, a, out):
    ctx = ExitStack()
    with ctx:
        def sb(name, shape, dt=F32):
            return ctx.enter_context(nc.sbuf_tensor(name, shape, dt))

        def sem(name):
            return ctx.enter_context(nc.semaphore(name))

        hT = sb("residual_T", [P, KT, T])
        uT = sb("normed_T", [P, KT, T])
        A = sb("arena", [P, 36, T])
        W = sb("work", [P, 10, T])
        ring = sb("weight_ring", [P, SLOTS, SLAB])
        cst = sb("constants", [P, CONST_W])
        vec = sb("vectors", [P, VEC_W])
        mod = sb("modulation", [P, 2, 72])
        gs = sb("norm_scales", [P, 6, KT])
        gate = sb("residual_gates", [P, 6, KT])
        cond = sb("cond", [P, KT])
        stat = sb("row_stats", [P, 4, 8])
        carrier = sb("wait_carrier", [P, 3])
        top8 = sb("top8", [P, 3, 8])
        small = sb("small", [P, 12, 64])
        table = sb("bias_table", [P, 18])

        lin = [ctx.enter_context(nc.psum_tensor(f"lin{i}", [P, T], F32)) for i in range(2)]
        score = [ctx.enter_context(nc.psum_tensor(f"score{i}", [P, T], F32)) for i in range(2)]
        turn = [ctx.enter_context(nc.psum_tensor(f"turn{i}", [P, T], F32)) for i in range(2)]
        outp = [ctx.enter_context(nc.psum_tensor(f"out{i}", [P, T], F32)) for i in range(2)]

        skew = nc.dram_tensor("skew_scratch", [DIL_HEADS, P * BIAS_W], F32, kind="Internal").ap()

        slot_full = [sem(f"slot_full{s}") for s in range(SLOTS)]
        ada_full = [sem(f"ada_full{s}") for s in range(SLOTS)]
        ada_folded = sem("ada_folded")
        lin_full = [sem(f"lin_full{b}") for b in range(2)]
        lin_taken = [sem(f"lin_taken{b}") for b in range(2)]
        const_loaded = sem("const_loaded")
        vec_loaded = sem("vec_loaded")
        x_loaded = sem("x_loaded")
        dve_step = sem("dve_step")
        act_step = sem("act_step")
        cond_ready = sem("cond_ready")
        angle_ready = sem("angle_ready")
        sel_loaded = sem("sel_loaded")
        squares = sem("squares_added")
        sumsq_summed = sem("sumsq_summed")
        inverse_ready = sem("inverse_ready")
        inverse_wide = sem("inverse_wide")
        mean_ready = sem("mean_ready")
        root_ready = sem("root_ready")
        scaled = sem("scaled")
        u_ready = sem("u_ready")
        tap_done = sem("tap_done")
        silu_done = sem("silu_done")
        gated = sem("gated")
        roped = sem("roped")
        score_ready = sem("score_ready")
        logits_ready = sem("logits_ready")
        negmax_ready = sem("negmax_ready")
        probs_ready = sem("probs_ready")
        probs_normed = sem("probs_normed")
        turned = sem("turned")
        pT_ready = sem("pT_ready")
        pv_done = sem("pv_done")
        head_taken = sem("head_taken")
        relu_used = sem("relu_used")
        forget_ready = sem("forget_ready")
        foxrow_ready = sem("foxrow_ready")
        softplus_ready = sem("softplus_ready")
        zeros_ready = sem("zeros_ready")
        merged_ready = sem("merged_ready")
        table_ready = sem("table_ready")
        bias_stored = [sem(f"bias_stored{i}") for i in range(4)]
        bias_loaded = [sem(f"bias_loaded{i}") for i in range(2)]
        perm_ready = sem("perm_ready")
        dt_ready = sem("dt_ready")
        ssd_ready = sem("ssd_ready")
        ssd_exp = sem("ssd_exp")
        ssd_pe = sem("ssd_pe")
        ssd_dve = sem("ssd_dve")
        result_ready = sem("result_ready")
        result_stored = sem("result_stored")

        def C(name, rows=P, lo=0, width=None):
            at, w = CONST[name]
            return cst[0:rows, at + lo:at + lo + (width or w)]

        def V(name, lo=0, width=None):
            at, w = VEC[name]
            return vec[:, at + lo:at + lo + (w if width is None else width)]

        def Vr(name, i):
            return vec[:, ds(i + VEC[name][0], 1)]

        def job_done(c, slot=None, note=None):
            b = c.n["job"] % 2
            c.add(f"bank{b}")
            c.add("job")
            if slot is not None:
                c.mark(f"slot{slot}", lin_full[b], f"bank{b}")
            if note:
                c.mark(note, lin_taken[b], f"bank{b}")

        def load(sp, c, s, src, width, full=slot_full):
            c.wait_mark(sp, f"slot{s}")
            sp.dma_start(ring[:, s, 0:width], src).then_inc(full[s], 16)

        def load_ada(sp, c, s, layer, sub, m):
            load(sp, c, s, a["ada"][layer, sub, ds(m, 1)].squeeze(0), SLAB, ada_full)
            c.add("folded")
            c.mark(f"slot{s}", ada_folded, "folded")

        def slab_there(pe, c, s):
            c.add(f"load{s}")
            pe.wait_ge(slot_full[s], c[f"load{s}"] * 16)

        def bank_open(pe, c):
            b = c.n["job"] % 2
            after(pe, lin_taken[b], c[f"bank{b}"])
            return lin[b]

        def bank_close(c, ins, **kw):
            ins.then_inc(lin_full[c.n["job"] % 2], 1)
            job_done(c, **kw)

        def bank_wait(eng, c):
            b = c.n["job"] % 2
            eng.wait_ge(lin_full[b], c[f"bank{b}"] + 1)
            return lin[b]

        def bank_take(c, ins, **kw):
            ins.then_inc(lin_taken[c.n["job"] % 2], 1)
            job_done(c, **kw)

        def skip_jobs(c, n=1):
            for _ in range(n):
                job_done(c)

        def all_taken(eng, c):
            for b in range(2):
                after(eng, lin_taken[b], c[f"bank{b}"])

        def vlink(v, c, ins):
            ins.then_inc(dve_step, 1)
            c.add("dve")
            v.wait_ge(dve_step, c["dve"])

        def carry_waits(v, place):
            v.memset(carrier[:, place:place + 1], 0.0)

        def alink(s, c, ins):
            ins.then_inc(act_step, 1)
            c.add("act")
            s.wait_ge(act_step, c["act"])

        def mm(pe, o, l, r, k, last):
            return pe.matmul(o, l, r, start=(k == 0), stop=(k == last))

        def copy_job(s, c, dst, w=T, rows=P, **kw):
            o = bank_wait(s, c)
            bank_take(c, s.activation(dst, o[0:rows, 0:w], ACT.Copy), **kw)

        sums = W[:, 0:2, :]
        scaled_sums = W[:, 7:9, :]
        rinv = score[0][:, :]
        folded = [W[:, 5 + n, :] for n in range(2)]

        def add_squares(v, c, tile, sums=sums):
            vlink(v, c, v.tensor_tensor(sums[:, 1:2, :], tile, tile, ALU.mult))
            v.tensor_tensor(sums[:, 0:1, :], sums[:, 0:1, :], sums[:, 1:2, :], ALU.add).then_inc(squares, 1)
            c.add("sq")
            v.wait_ge(squares, c["sq"])

        def sum_squares(pe, c, bank, sums):
            for q in range(QT):
                last = pe.matmul(bank[:, q:q + 1], sums[:, 0, q * P:(q + 1) * P], C("ones", width=1), start=True,
                                 stop=True)
            last.then_inc(sumsq_summed, 1)

        def spread_inverse(pe, c, bank, at=32):
            pe.wait_ge(inverse_ready, c["norm"])
            for q in range(QT):
                last = pe.matmul(bank[:, q * P:(q + 1) * P], small[:, 4, at + q:at + q + 1].to_broadcast([P, P]),
                                 C("ident"), start=True, stop=True)
            last.then_inc(inverse_wide, 1)

        def norm_pe(pe, c, tiles=KT, sums=sums):
            c.add("sq", tiles)
            c.add("norm")
            counted_norm_pe(pe, c, sums)

        def counted_norm_pe(pe, c, sums):
            pe.wait_ge(squares, c["sq"])
            sum_squares(pe, c, score[0], sums)
            spread_inverse(pe, c, score[0])

        def norm_act(s, c, n=D):
            c.add("norm")
            s.wait_ge(sumsq_summed, c["norm"])
            s.activation(small[:, 4, 16:16 + QT], score[0][:, 0:QT], ACT.Sqrt, bias=V("eps"), scale=1.0 / n)\
             .then_inc(root_ready, 1)

        def norm_root(v, c):
            c.add("norm")
            v.wait_ge(root_ready, c["norm"])
            v.reciprocal(small[:, 4, 32:32 + QT], small[:, 4, 16:16 + QT]).then_inc(inverse_ready, 1)
            v.wait_ge(inverse_wide, c["norm"])

        def ada_norm_dve(v, c, inst):
            norm_root(v, c)
            for k in range(KT):
                v.scalar_tensor_tensor(out=uT[:, k, :], in0=hT[:, k, :], scalar=gs[:, inst, k:k + 1], in1=rinv,
                                       op0=ALU.mult, op1=ALU.mult).then_inc(scaled, 1)

        def ada_norm_act(s, c, inst):
            layer, sub = inst // 3, inst % 3
            norm_act(s, c)
            for k in range(KT):
                c.add("scaled")
                s.wait_ge(scaled, c["scaled"])
                s.activation(uT[:, k, :], uT[:, k, :], ACT.Identity,
                             bias=mod[:, layer, 24 * sub + k:24 * sub + k + 1]).then_inc(u_ready, 1)

        def plain_norm_dve(v, c, g):
            norm_root(v, c)
            for k in range(KT):
                v.scalar_tensor_tensor(out=uT[:, k, :], in0=hT[:, k, :], scalar=V(g, k, 1), in1=rinv,
                                       op0=ALU.mult, op1=ALU.mult).then_inc(u_ready, 1)

        def clear_sumsq(v, c, sums=sums):
            vlink(v, c, v.memset(sums[:, 0, :], 0.0))

        def fold_dve(v, c, s, n):
            c.add(f"ada{s}")
            v.wait_ge(ada_full[s], c[f"ada{s}"] * 16)
            w = ring[:, s, :].rearrange("p (k n) -> p k n", k=KT)
            acc = folded[n][:, 0:SLAB // KT]
            vlink(v, c, v.tensor_scalar(acc, w[:, 0, :], cond[:, 0:1], None, ALU.mult))
            for k in range(1, KT):
                ins = v.scalar_tensor_tensor(out=acc, in0=w[:, k, :], scalar=cond[:, k:k + 1], in1=acc,
                                             op0=ALU.mult, op1=ALU.add)
                if k < KT - 1:
                    vlink(v, c, ins)
            ins.then_inc(ada_folded, 1)

        def ada_pe(pe, c, buffers):
            c.add("folded", len(buffers))
            pe.wait_ge(ada_folded, c["folded"])
            o = bank_open(pe, c)
            for at, n in enumerate(buffers):
                for m in range(3):
                    last = pe.matmul(o[:, 3 * at + m:3 * at + m + 1], folded[n][:, m * P:(m + 1) * P],
                                     C("ones", width=1), start=True, stop=True)
            bank_close(c, last)

        def ada_dve(v, c, sublayers, group):
            o = bank_wait(v, c)
            for n, (layer, sub) in enumerate(sublayers):
                at = VEC["ada_b"][0] + 72 * layer + 24 * sub
                ins = v.tensor_tensor(mod[:, layer, ds(group * 3 + 24 * sub, 3)], o[:, 3 * n:3 * n + 3],
                                      vec[:, ds(group * 3 + at, 3)], ALU.add)
                if n < len(sublayers) - 1:
                    vlink(v, c, ins)
            bank_take(c, ins)

        def mod_dve(v, c, layer, sub):
            i = 3 * layer + sub
            all_taken(v, c)
            vlink(v, c, v.scalar_tensor_tensor(out=gs[:, i, :], in0=mod[:, layer, 24 * sub + 8:24 * sub + 16],
                                               scalar=1.0, in1=V("norm_g", 8 * i, 8), op0=ALU.add, op1=ALU.mult))
            vlink(v, c, v.tensor_scalar(gate[:, i, :], mod[:, layer, 24 * sub + 16:24 * sub + 24],
                                        1.0 if sub == 1 else 0.5, None, ALU.mult))

        onehot = A[:, 0:5, :].rearrange("p a b -> p (a b)")[:, 0:BIAS_W]
        relx = A[:, 5:10, :].rearrange("p a b -> p (a b)")[:, 0:18 * P].rearrange("p (h n) -> p h n", h=18)
        biasrow = [A[:, n:n + 5, :].rearrange("p a b -> p (a b)")[:, 0:BIAS_W] for n in (26, 31, 16, 11)]
        sel_at = CONST["sel"][0]
        CHUNKS = [(0, 512, 0), (512, 512, 0), (1024, 512, 0), (1536, 256, 0), (1792, 256, 1), (2048, 256, 2)]
        cos16, sin16, cos64, sin64 = (A[:, 22 + i, :] for i in range(4))
        positions = W[:, 7, :]

        def prologue_sp(sp, c):
            sp.dma_start(positions.bitcast(I32), a["positions"].to_broadcast([P, T])).then_inc(vec_loaded, 16)
            sp.dma_start(vec[:, :], a["vectors"]).then_inc(vec_loaded, 16)
            sp.dma_start(cst[:, 0:sel_at], a["constants"][:, 0:sel_at]).then_inc(const_loaded, 16)
            sp.dma_start(onehot[0:33, :], a["onehot"]).then_inc(const_loaded, 16)
            for j in range(4):
                load_ada(sp, c, j, 0, 0, j)
                if j == 1:
                    sp.dma_start(hT[:, :, :], a["xT"]).then_inc(x_loaded, 16)
            for j in range(KT):
                if j < 4:
                    load_ada(sp, c, j, 0, 0, j + 4)
                if j < DIL_HEADS:
                    for _ in CHUNKS:
                        job_done(c, note=f"row{j}")
                job_done(c)
                for row in {1: (0,), 2: (1,), 5: (2, 3, 4, 5)}.get(j, ()):
                    c.wait_mark(sp, f"row{row}")
                    sp.dma_start(skew[row].rearrange("(p w) -> p w", p=P), biasrow[row % 4])\
                      .then_inc(bias_stored[row % 4], 16)
            sp.dma_start(cst[0:16, sel_at:], a["constants"][0:16, sel_at:]).then_inc(sel_loaded, 16)

        def all_stored(sp):
            for n in range(4):
                sp.wait_ge(bias_stored[n], 16 * len(range(n, DIL_HEADS, 4)))

        def prologue_pe(pe, c):
            pe.wait_ge(const_loaded, 32)
            pe.wait_ge(table_ready, 1)
            for j in range(KT):
                if j < DIL_HEADS:
                    for lo, w, g in CHUNKS:
                        o = bank_open(pe, c)
                        bank_close(c, pe.matmul(o[:, 0:w], relx[0:33, g * DIL_HEADS + j, :],
                                                onehot[0:33, lo:lo + w], start=True, stop=True))
                ada_pe(pe, c, (j % 2,))

        def prologue_act(s, c):
            s.wait_ge(vec_loaded, 32)
            s.activation(cond[:, :], V("c"), ACT.Silu).then_inc(cond_ready, 1)
            for j in range(KT):
                if j < DIL_HEADS:
                    after(s, bias_stored[j % 4], 16 * (j // 4))
                    for lo, w, _ in CHUNKS:
                        copy_job(s, c, biasrow[j % 4][:, lo:lo + w], w)
                skip_jobs(c)
            for i in range(2):
                s.wait_ge(angle_ready, 2 * i + 2)
                for n in (23, 22):
                    s.activation(A[:, n + 2 * i, :], A[:, n + 2 * i, :], ACT.Sin)

        def prologue_dve(v, c):
            vlink(v, c, v.memset(stat[:, :, :], 0.0))
            vlink(v, c, v.memset(table[:, :], NEG))
            v.wait_ge(vec_loaded, 32)
            vlink(v, c, v.tensor_scalar(table[0:32, :], V("rel")[0:32, :], 8.0, None, ALU.mult))
            v.tensor_copy(relx[0:33, :, :], table[0:33, :].unsqueeze(2).to_broadcast([33, 18, P]))\
             .then_inc(table_ready, 1)
            two_pi = 2 * math.pi
            c1 = 6.28125
            c2 = float(np.float32(math.floor((two_pi - c1) * 2 ** 21) / 2 ** 21))
            c3 = float(np.float32(two_pi - c1 - c2))
            magic = 1.5 * 2 ** 23
            vlink(v, c, v.tensor_copy(positions, positions.bitcast(I32)))
            for i, inv in enumerate(("invf16", "invf64")):
                ang, k, r, q = (A[:, n, :] for n in (10, 21, 23 + 2 * i, 22 + 2 * i))
                vlink(v, c, v.tensor_scalar(ang, positions, V(inv), None, ALU.mult))
                vlink(v, c, v.tensor_scalar(k, ang, 1.0 / two_pi, magic, ALU.mult, ALU.add))
                vlink(v, c, v.tensor_scalar(k, k, -magic, None, ALU.add))
                for part in (c1, c2, c3):
                    vlink(v, c, v.scalar_tensor_tensor(out=ang, in0=k, scalar=-part, in1=ang, op0=ALU.mult,
                                                       op1=ALU.add))
                v.tensor_scalar(r, ang, 3.1415925, -3.1415925, ALU.min, ALU.max).then_inc(angle_ready, 1)
                v.wait_ge(angle_ready, 2 * i + 1)
                vlink(v, c, v.tensor_scalar(q, r, -1.0, None, ALU.mult))
                vlink(v, c, v.tensor_tensor(q, q, r, ALU.min))
                v.tensor_scalar(q, q, math.pi / 2, None, ALU.add).then_inc(angle_ready, 1)
            v.wait_ge(cond_ready, 1)
            clear_sumsq(v, c)
            for j in range(KT):
                fold_dve(v, c, j % 4, j % 2)
                if j == 2:
                    v.wait_ge(x_loaded, 16)
                for k in {2: (0, 1), 3: (2, 3), 4: (4,), 5: (5,), 6: (6,), 7: (7,)}.get(j, ()):
                    add_squares(v, c, hT[:, k:k + 1, :])
                if j < DIL_HEADS:
                    skip_jobs(c, len(CHUNKS))
                ada_dve(v, c, ((0, 0),), j)
            mod_dve(v, c, 0, 0)

        def down_sp(sp, c, src, width, adas=()):
            def body(i):
                for j in range(2):
                    load(sp, c, 2 + j, src[ds(i * 2 + j, 1)].squeeze(0), width)
                    job_done(c, slot=2 + j)
                    for n, (l, s) in enumerate(adas):
                        load_ada(sp, c, n, l, s, i * 2 + j)
                    if adas:
                        job_done(c)
            c.loop(sp, 0, KT // 2, body)

        def down_pe(pe, c, rhs, there, adas=()):
            n_k = len(rhs)

            def body(i):
                for j in range(2):
                    slab_there(pe, c, 2 + j)
                    o = bank_open(pe, c)
                    for k in range(n_k):
                        if isinstance(i, int) and j == 0:
                            there(k)
                        last = mm(pe, o[:, :], ring[:, 2 + j, k * P:(k + 1) * P], rhs[k], k, n_k - 1)
                    bank_close(c, last)
                    if adas:
                        ada_pe(pe, c, range(len(adas)))
            c.loop(pe, 0, KT // 2, body)

        def down_act(s, c, adas=()):
            skip_jobs(c, KT * (2 if adas else 1))

        def down_dve(v, c, inst, adas=(), also=lambda m, tile: None):
            clear_sumsq(v, c)

            def body(i):
                for j in range(2):
                    m = i * 2 + j
                    for n in range(len(adas)):
                        fold_dve(v, c, n, n)
                    o = bank_wait(v, c)
                    tile = hT[:, ds(m, 1), :]
                    if inst is None:
                        ins = v.tensor_tensor(tile, o[:, :].unsqueeze(1), tile, ALU.add)
                    else:
                        ins = v.scalar_tensor_tensor(out=tile, in0=o[:, :].unsqueeze(1),
                                                     scalar=gate[:, inst, ds(m, 1)], in1=tile,
                                                     op0=ALU.mult, op1=ALU.add)
                    bank_take(c, ins, note="updated")
                    c.wait_mark(v, "updated")
                    add_squares(v, c, tile)
                    also(m, tile)
                    if adas:
                        ada_dve(v, c, adas, m)
            c.loop(v, 0, KT // 2, body)
            for l, s in adas:
                mod_dve(v, c, l, s)

        def up_sp(sp, c, src, before_rest=lambda sp: None):
            def body(i):
                for j in range(2):
                    load(sp, c, j, src[ds(i * 2 + j, 1)].squeeze(0), 2 * D)
                    job_done(c)
                    job_done(c, slot=j)
                if isinstance(i, int):
                    before_rest(sp)
            c.loop(sp, 0, FT // 2, body)

        def up_pe(pe, c):
            u0 = c.n["u"]

            def body(i):
                for j in range(2):
                    slab_there(pe, c, j)
                    w = ring[:, j, 0:2 * D].rearrange("p (g k n) -> p g k n", g=2, k=KT)
                    for g in range(2):
                        o = bank_open(pe, c)
                        for k in range(KT):
                            if isinstance(i, int) and j == 0 and g == 0:
                                pe.wait_ge(u_ready, u0 + k + 1)
                            last = mm(pe, o[:, :], w[:, g, k, :], uT[:, k, :], k, KT - 1)
                        bank_close(c, last)
            c.loop(pe, 0, FT // 2, body)
            c.add("u", KT)

        hidden = [A[:, k, :] for k in range(FT)]

        def swiglu_act(s, c):
            def body(i):
                for j in range(2):
                    o = bank_wait(s, c)
                    c.wait_mark(s, f"silu{j}")
                    bank_take(c, s.activation(W[:, 3 + j, :], o[:, :], ACT.Silu))
                    job_done(c, note=f"silu{j}")
            c.marks.pop("silu0", None)
            c.marks.pop("silu1", None)
            c.loop(s, 0, FT // 2, body)

        def swiglu_dve(v, c):
            def body(i):
                for j in range(2):
                    job_done(c, note="gate")
                    c.wait_mark(v, "gate")
                    o = bank_wait(v, c)
                    bank_take(c, v.tensor_tensor(A[:, ds(i * 2 + j, 1), :], o[:, :].unsqueeze(1),
                                                 W[:, 3 + j:4 + j, :], ALU.mult))
            c.loop(v, 0, FT // 2, body)

        def ffn(inst, index, adas):
            def sp(e, c):
                up_sp(e, c, a["up"][index], *((all_stored,) if index == 0 else ()))
                down_sp(e, c, a["down"][index], FF, adas)

            def pe(e, c):
                norm_pe(e, c)
                up_pe(e, c)
                b = (c.n["job"] - 1) % 2
                taken = c.n[f"bank{b}"]

                def there(k):
                    if k == 0:
                        e.wait_ge(lin_taken[b], taken - 1)
                    elif k == FT - 1:
                        e.wait_ge(lin_taken[b], taken)
                down_pe(e, c, hidden, there, adas)

            def act(e, c):
                ada_norm_act(e, c, inst)
                swiglu_act(e, c)
                down_act(e, c, adas)

            def dve(e, c):
                ada_norm_dve(e, c, inst)
                swiglu_dve(e, c)
                if inst != 5:
                    down_dve(e, c, inst, adas)
                else:
                    def scaled_squares(m, tile):
                        scaled_tile = W[:, 9:10, :]
                        vlink(e, c, e.tensor_scalar(scaled_tile, tile, Vr("final_g", m), None, ALU.mult))
                        add_squares(e, c, scaled_tile, scaled_sums)
                    clear_sumsq(e, c, scaled_sums)
                    down_dve(e, c, inst, adas, scaled_squares)
            return sp, pe, act, dve

        logits = [W[:, 2 + n, :] for n in range(4)]
        probsT = [W[:, 6 + n, :] for n in range(2)]

        STEPS = 8 + 3

        def at_step(t, jobs):
            at = 0
            for name, n in jobs:
                for k in range(n):
                    if at * STEPS // sum(m for _, m in jobs) == t:
                        yield name, k, k == n - 1
                    at += 1

        def attend_pe(pe, c, units, fill, values):
            part0, unit0 = c.n["part"], c.n["unit"]
            first_part = [sum(len(u["parts"]) for u in units[:n]) for n in range(len(units) + 1)]
            for t in range(len(units) + 3):
                if t < len(units):
                    for q, part in enumerate(units[t]["parts"]):
                        n = first_part[t] + q
                        after(pe, logits_ready, c.value("part", part0 + n - 1))
                        k = len(part["products"])
                        for m, (l, r, lo, hi) in enumerate(part["products"]):
                            opens = m == 0 or part["products"][m - 1][2] != lo
                            closes = m == k - 1 or part["products"][m + 1][2] != lo
                            last = pe.matmul(score[(part0 + n) % 2][:, lo:hi], l, r, start=opens, stop=closes)
                        last.then_inc(score_ready, 1)
                fill(t)
                if 0 <= t - 2 < len(units):
                    u = t - 2
                    for q, part in enumerate(units[u]["parts"]):
                        n = first_part[u] + q
                        pe.wait_ge(probs_normed, c.value("part", part0 + n + 1))
                        after(pe, pT_ready, c.value("part", part0 + n - 1))
                        for b in range(part["n"] // P):
                            last = pe.transpose(turn[(part0 + n) % 2][:, b * P:(b + 1) * P],
                                                logits[(part0 + n) % 4][:, b * P:(b + 1) * P], C("ident"))
                        last.then_inc(turned, 1)
                if t - 3 >= 0:
                    u = t - 3
                    blocks = sum(len(part["values"]) for part in units[u]["parts"])
                    at = 0
                    for q, part in enumerate(units[u]["parts"]):
                        n = first_part[u] + q
                        pe.wait_ge(pT_ready, c.value("part", part0 + n + 1))
                        if u == 0 and q == 0:
                            after(pe, head_taken, c["head"])
                            c.wait_mark(pe, values)
                        for b, val in enumerate(part["values"]):
                            last = mm(pe, units[u]["out"], val, probsT[(part0 + n) % 2][:, b * P:(b + 1) * P],
                                      at, blocks - 1)
                            at += 1
                        last.then_inc(pv_done, 1)
            count_units(c, units)

        def count_units(c, units):
            c.add("part", sum(len(u["parts"]) for u in units))
            c.add("unit", len(units))

        def attend_dve(v, c, units, scale, fill, arrived=lambda t: None):
            part0, unit0 = c.n["part"], c.n["unit"]
            p = 0
            for t in range(len(units) + 3):
                if t < len(units):
                    st = stat[:, (unit0 + t) % 4, :]
                    parts = units[t]["parts"]
                    arrived(t)
                    for q, part in enumerate(parts):
                        n = part0 + p
                        p += 1
                        v.wait_ge(score_ready, c.value("part", n + 1))
                        after(v, turned, c.value("part", n - 3))
                        carry_waits(v, q)
                        v.tensor_tensor_reduce(logits[n % 4][:, 0:part["n"]], score[n % 2][:, 0:part["n"]],
                                               part["bias"], scale, NEG, ALU.add, ALU.max,
                                               st[:, q:q + 1]).then_inc(logits_ready, 1)
                    v.wait_ge(logits_ready, c.value("part", part0 + p))
                    if len(parts) == 2:
                        vlink(v, c, v.tensor_tensor(st[:, 0:1], st[:, 0:1], st[:, 1:2], ALU.max))
                    v.tensor_scalar(st[:, 2:3], st[:, 0:1], -1.0, None, ALU.mult).then_inc(negmax_ready, 1)
                if 0 < t <= len(units):
                    u = t - 1
                    st = stat[:, (unit0 + u) % 4, :]
                    two = len(units[u]["parts"]) == 2
                    done = sum(len(x["parts"]) for x in units[:u + 1])
                    v.wait_ge(probs_ready, c.value("part", part0 + done))
                    if two:
                        vlink(v, c, v.tensor_tensor(st[:, 3:4], st[:, 3:4], st[:, 4:5], ALU.add))
                    vlink(v, c, v.reciprocal(st[:, 5:6], st[:, 3:4]))
                    for q, part in enumerate(units[u]["parts"]):
                        n = part0 + done - len(units[u]["parts"]) + q
                        probs = logits[n % 4][:, 0:part["n"]]
                        v.tensor_scalar(probs, probs, st[:, 5:6], None, ALU.mult).then_inc(probs_normed, 1)
                fill(t)
            count_units(c, units)

        def attend_act(s, c, units, outs, fill):
            part0, unit0 = c.n["part"], c.n["unit"]
            first_part = [sum(len(u["parts"]) for u in units[:n]) for n in range(len(units) + 1)]
            for t in range(len(units) + 3):
                if t < len(units):
                    st = stat[:, (unit0 + t) % 4, :]
                    s.wait_ge(negmax_ready, c.value("unit", unit0 + t + 1))
                    for q, part in enumerate(units[t]["parts"]):
                        n = part0 + first_part[t] + q
                        lg = logits[n % 4][:, 0:part["n"]]
                        s.activation(lg, lg, ACT.Exp, bias=st[:, 2:3], accum_out=st[:, 3 + q:4 + q])\
                         .then_inc(probs_ready, 1)
                if 0 <= t - 2 < len(units):
                    for q, part in enumerate(units[t - 2]["parts"]):
                        n = part0 + first_part[t - 2] + q
                        s.wait_ge(turned, c.value("part", n + 1))
                        after(s, pv_done, c.value("part", n - 1))
                        s.activation(probsT[n % 2][:, 0:part["n"]], turn[n % 2][:, 0:part["n"]], ACT.Copy)\
                         .then_inc(pT_ready, 1)
                if t - 3 >= 0:
                    for src, dst in outs.get(t - 3, ()):
                        s.wait_ge(pv_done, c.value("part", part0 + first_part[t - 2]))
                        s.activation(dst, src, ACT.Copy).then_inc(head_taken, 1)
                        c.add("head")
                fill(t)
            count_units(c, units)

        def rope_raw_act(s, c, raw, name):
            o = bank_wait(s, c)
            c.wait_mark(s, name)
            bank_take(c, s.activation(raw, o[:, :], ACT.Copy))

        def rope_note(c, name):
            c.add("rope")
            c.mark(name, roped, "rope")

        def rotate_pe(pe, c, raw, rot, note):
            c.wait_mark(pe, note)
            o = bank_open(pe, c)
            bank_close(c, pe.matmul(o[:, :], C(rot), raw, start=True, stop=True))

        def rope_dve(v, c, raw, cos, sin, dst, note):
            c.wait_mark(v, note)
            after(v, roped, c["rope"])
            v.tensor_tensor(W[:, 8, :], raw, cos, ALU.mult)
            o = bank_wait(v, c)
            bank_take(c, v.tensor_tensor(W[:, 9, :], o[:, :], sin, ALU.mult), note="rope_terms")
            c.wait_mark(v, "rope_terms")
            v.tensor_tensor(dst, W[:, 8, :], W[:, 9, :], ALU.add).then_inc(roped, 1)
            c.add("rope")

        def project_part(pe, c, w, rhs, k, **kw):
            o = bank_open(pe, c) if k == 0 else lin[c.n["job"] % 2]
            last = mm(pe, o[:, :], w(k), rhs[k], k, len(rhs) - 1)
            if k == len(rhs) - 1:
                bank_close(c, last, **kw)

        def project(pe, c, w, rhs, arriving=None, **kw):
            for k in range(len(rhs)):
                if arriving is not None:
                    pe.wait_ge(u_ready, arriving + k + 1)
                project_part(pe, c, w, rhs, k, **kw)

        def project_rows_part(pe, c, w, lhs, tiles, width, k, **kw):
            o = bank_open(pe, c) if k == 0 else lin[c.n["job"] % 2]
            per = len(tiles)
            for at in range(k * per, (k + 1) * per):
                n, kk = divmod(at, len(lhs))
                tt = tiles[n]
                last = mm(pe, o[:, n * width:(n + 1) * width], lhs[kk][:, tt * P:(tt + 1) * P], w(kk), kk,
                          len(lhs) - 1)
            if k == len(lhs) - 1:
                bank_close(c, last, **kw)

        def project_rows(pe, c, w, lhs, tiles, width, **kw):
            for k in range(len(lhs)):
                project_rows_part(pe, c, w, lhs, tiles, width, k, **kw)

        u_tiles = [uT[:, k, :] for k in range(KT)]

        def part(products, n, bias, values):
            return dict(products=products, n=n, bias=bias, values=values)

        qT, kT = [A[:, 16, :], A[:, 27, :]], [A[:, 17, :], A[:, 28, :]]
        vN = [A[:, n, :].rearrange("p (t n) -> p t n", t=QT) for n in (18, 29)]
        foxK, foxC = A[0:16, 19, :], A[0:16, 20, :]
        foxQ = [[A[0:16, 21, :], A[0:16, 26, :]], [A[0:16, 30, :], A[0:16, 31, :]]]
        iq, ik = [A[:, 0, :], A[:, 1, :]], A[:, 2, :]
        sel_mask = [None] + [A[:, 4 + n, :] for n in range(1, QT)]
        raw = [W[:, 0, :], W[:, 1, :]]
        mixed = [A[:, 8 + n, :] for n in range(8)]

        FOX_JOBS = (("q", 8), ("k", 8), ("v0", 8), ("v1", 8))
        DSA_JOBS = (("q", 8), ("k", 8), ("v0", 8), ("q_rot", 1), ("k_rot", 1), ("v1", 8))

        def pair_jobs(p):
            return FOX_JOBS if p < 4 else DSA_JOBS

        def pair_step_pe(e, c, p, t):
            if t == 0:
                slab_there(e, c, 2 + p % 2)
            w = ring[:, 2 + p % 2, :].rearrange("p (g k n) -> p g k n", g=3, k=KT)
            for name, k, _ in at_step(t, pair_jobs(p)):
                if name in ("q", "k"):
                    project_part(e, c, lambda k: w[:, "qk".index(name), k, :], u_tiles, k, note=name)
                elif name in ("v0", "v1"):
                    project_rows_part(e, c, lambda k: w[:, 2, k, :], u_tiles, (0, 1) if name == "v0" else (2, 3), P,
                                      k, note=name)
                else:
                    rotate_pe(e, c, raw["qk".index(name[0])], "rot16", name[0])

        def pair_step_act(e, c, p, t):
            s = p % 2
            for name, _, last in at_step(t, pair_jobs(p)):
                if not last:
                    continue
                if name in ("q", "k"):
                    if p < 4:
                        copy_job(e, c, (qT if name == "q" else kT)[s])
                    else:
                        n = "qk".index(name)
                        rope_raw_act(e, c, raw[n], f"raw{n}")
                        rope_note(c, f"raw{n}")
                elif name in ("v0", "v1"):
                    v2 = int(name[1])
                    copy_job(e, c, vN[s][:, 2 * v2:2 * v2 + 2, :].rearrange("p t n -> p (t n)"), 2 * P)
                else:
                    skip_jobs(c)

        def pair_step_dve(e, c, p, t):
            s = p % 2
            if p < 4 and t == 0:
                if p >= 2:
                    e.wait_ge(score_ready, c["part"] + 1)
                for hh in range(2):
                    ins = e.tensor_scalar(foxQ[s][hh], foxC, C("foxrow", 16, 2 * p + hh, 1),
                                          C("foxone", 16, 2 * p + hh, 1), ALU.mult, ALU.add)
                    if hh == 0:
                        vlink(e, c, ins)
                    else:
                        ins.then_inc(foxrow_ready, 1)
            for name, _, last in at_step(t, pair_jobs(p)):
                if not last:
                    continue
                if name == "q_rot":
                    rope_dve(e, c, raw[0], cos16, sin16, qT[s], "q")
                elif name == "k_rot":
                    rope_dve(e, c, raw[1], cos16, sin16, kT[s], "k")
                else:
                    job_done(c, note=name)

        def pair_units(p):
            s = p % 2
            units = []
            for hh in range(2):
                r = slice(64 * hh, 64 * hh + 64)
                for qt in range(QT):
                    n = (qt + 1) * P
                    q = slice(qt * P, n)
                    products = [(qT[s][r, q], kT[s][r, 0:n], 0, n)]
                    if p < 4:
                        products.append((foxQ[s][hh][:, q], foxK[:, 0:n], 0, n))
                        bias = C("causal", lo=T - n, width=n)
                    else:
                        bias = sel_mask[qt][:, 0:n] if qt else C("chunked", lo=T - n, width=n)
                    values = [vN[s][:, b, r] for b in range(qt + 1)]
                    units.append(dict(parts=[part(products, n, bias, values)], out=outp[0][r, q]))
            return units

        def softplus_act(s, c):
            c.add("softplus_in")
            s.wait_ge(forget_ready, c["softplus_in"])
            alink(s, c, s.activation(small[:, 2, :], small[:, 1, :], ACT.Exp))
            s.activation(small[:, 2, :], small[:, 2, :], ACT.Ln, bias=1.0).then_inc(softplus_ready, 1)

        def softplus_dve_in(v, c):
            vlink(v, c, v.tensor_scalar(small[:, 1, :], small[:, 0, :], -1.0, None, ALU.mult))
            v.tensor_tensor(small[:, 1, :], small[:, 1, :], small[:, 0, :], ALU.min).then_inc(forget_ready, 1)
            c.add("softplus")
            v.wait_ge(softplus_ready, c["softplus"])

        def hybrid():
            def sp(e, c):
                load(e, c, 0, a["idx"], SLAB)
                load(e, c, 1, a["idx_small"], KT * 20)
                job_done(c), job_done(c), job_done(c)
                job_done(c, slot=0)
                job_done(c), job_done(c)
                job_done(c, slot=1)
                skip_jobs(c, 1 + 12)

                for p in range(8):
                    load(e, c, 2 + p % 2, a["fox" if p < 4 else "dsa"][p % 4], SLAB)
                    for n, (name, _) in enumerate(pair_jobs(p)):
                        job_done(c, slot=2 + p % 2 if name == "v1" else None)
                c.add("part", 8 * 2 * QT)
                down_sp(e, c, a["hyb_out"], D)

            def pe(e, c):
                norm_pe(e, c)
                slab_there(e, c, 0)
                w = ring[:, 0, :].rearrange("p (k n) -> p k n", k=KT)
                project(e, c, lambda k: w[:, k, 0:128], u_tiles, arriving=c.n["u"], note="iq0")
                c.add("u", KT)
                project(e, c, lambda k: w[:, k, 128:256], u_tiles, note="iq1")
                rotate_pe(e, c, raw[0], "rot16", "iq0")
                project(e, c, lambda k: w[:, k, 256:384], u_tiles, note="ik")
                rotate_pe(e, c, raw[1], "rot16", "iq1")
                rotate_pe(e, c, raw[0], "rot16", "ik")
                slab_there(e, c, 1)
                ws = ring[:, 1, 0:KT * 20].rearrange("p (k n) -> p k n", k=KT)
                project_rows(e, c, lambda k: ws[:, k, :], u_tiles, range(QT), 20)
                c.add("forget", 2)
                e.wait_ge(forget_ready, c["forget"])
                o = bank_open(e, c)
                for b in range(QT):
                    for b2 in range(b + 1):
                        last = mm(e, o[0:16, b * P:(b + 1) * P], small[:, 3, b2 * 16:b2 * 16 + 16],
                                  C("triu") if b2 == b else C("ones"), b2, b)
                bank_close(c, last)
                c.add("rope", 3)
                e.wait_ge(roped, c["rope"])
                for qt in range(1, QT):
                    n = (qt + 1) * P
                    for hh in range(4):
                        r = slice(64 * (hh % 2), 64 * (hh % 2) + 64)
                        o = bank_open(e, c)
                        bank_close(c, e.matmul(o[:, 0:n], iq[hh // 2][r, qt * P:n], ik[r, 0:n], start=True, stop=True))

                for t in range(STEPS):
                    pair_step_pe(e, c, 0, t)
                for p in range(8):
                    c.wait_mark(e, "q")
                    c.wait_mark(e, "k")
                    if p < 4:
                        c.add("foxrow")
                        e.wait_ge(foxrow_ready, c["foxrow"])
                    else:
                        c.add("rope", 2)
                        e.wait_ge(roped, c["rope"])
                    attend_pe(e, c, pair_units(p), lambda t: p < 7 and pair_step_pe(e, c, p + 1, t), "v1")
                    c.add("head")
                down_pe(e, c, mixed, lambda k: k in (0, 7) and e.wait_ge(head_taken, c["head"] - (k < 7)))

            def act(e, c):
                ada_norm_act(e, c, 1)
                rope_raw_act(e, c, raw[0], "raw0")
                rope_note(c, "raw0")
                rope_raw_act(e, c, raw[1], "raw1")
                rope_note(c, "raw1")
                skip_jobs(c)
                rope_raw_act(e, c, raw[0], "raw0")
                rope_note(c, "raw0")
                skip_jobs(c, 3)
                softplus_act(e, c)
                c.add("softplus_in")
                skip_jobs(c)
                for n in range(12):
                    o = bank_wait(e, c)
                    width = (n // 4 + 2) * P
                    after(e, relu_used, n - 1)
                    bank_take(c, e.activation(W[:, 2 + n % 2, 0:width], o[:, 0:width], ACT.Relu, scale=IDX_SCALE))
                c.add("relu", 12)

                for t in range(STEPS):
                    pair_step_act(e, c, 0, t)
                for p in range(8):
                    attend_act(e, c, pair_units(p), {7: [(outp[0][:, :], A[:, 8 + p, :])]},
                               lambda t: p < 7 and pair_step_act(e, c, p + 1, t))
                down_act(e, c)

            def dve(e, c):
                ada_norm_dve(e, c, 1)
                job_done(c, note="iq0")
                job_done(c, note="iq1")
                rope_dve(e, c, raw[0], cos16, sin16, iq[0], "iq0")
                job_done(c, note="ik")
                rope_dve(e, c, raw[1], cos16, sin16, iq[1], "iq1")
                rope_dve(e, c, raw[0], cos16, sin16, ik, "ik")
                o = bank_wait(e, c)
                rows = o[:, 0:80].rearrange("p (t n) -> p t n", t=QT)
                x = small[:, 0, :].rearrange("p (t n) -> p t n", t=QT)
                vlink(e, c, e.tensor_tensor(x, rows[:, :, 0:16], V("b_f").unsqueeze(1).to_broadcast([P, QT, 16]),
                                            ALU.add))
                iw = small[:, 4, 0:16]
                bank_take(c, e.tensor_scalar(iw.rearrange("p (t n) -> p t n", t=QT), rows[:, :, 16:20], 0.5, None,
                                             ALU.mult), note="iw")
                c.wait_mark(e, "iw")
                softplus_dve_in(e, c)
                e.scalar_tensor_tensor(out=small[:, 3, :], in0=small[:, 0, :], scalar=0.0, in1=small[:, 2, :],
                                       op0=ALU.min, op1=ALU.subtract).then_inc(forget_ready, 1)
                o = bank_wait(e, c)
                vlink(e, c, e.tensor_copy(foxC, o[0:16, :]))
                bank_take(c, e.tensor_scalar(foxK, o[0:16, :], C("foxkey", 16, 0, 1), C("foxkey", 16, 1, 1), ALU.mult,
                                             ALU.add))
                for n in range(12):
                    qt, hh = n // 4 + 1, n % 4
                    width = (qt + 1) * P
                    job_done(c, note="relu")
                    c.wait_mark(e, "relu")
                    acc, r, w = sel_mask[qt][:, 0:width], W[:, 2 + n % 2, 0:width], iw[:, 4 * qt + hh:4 * qt + hh + 1]
                    if hh == 0:
                        e.tensor_scalar(acc, r, w, None, ALU.mult).then_inc(relu_used, 1)
                    else:
                        e.scalar_tensor_tensor(out=acc, in0=r, scalar=w, in1=acc, op0=ALU.mult, op1=ALU.add)\
                         .then_inc(relu_used, 1)
                    e.wait_ge(relu_used, n + 1)
                    if hh == 3:
                        last = acc[:, width - P:width]
                        vlink(e, c, e.tensor_tensor(last, last, C("chunked", lo=T - P, width=P), ALU.add))

                def search(qt):
                    tile = sel_mask[qt][:, 0:(qt + 1) * P]
                    carry_waits(e, 2)
                    vlink(e, c, e.max(top8[:, qt - 1, :], tile))
                    carry_waits(e, 2)
                    vlink(e, c, e.match_replace(tile, top8[:, qt - 1, :], tile, GONE))

                todo = [qt for _ in range(TOPK // 8) for qt in range(1, QT)]

                def beside(p, t):
                    if p < 7:
                        pair_step_dve(e, c, p + 1, t)
                    if p < 4 and t < 8:
                        for _ in range(2 if t % 2 == 0 else 1):
                            search(todo.pop())

                for t in range(STEPS):
                    pair_step_dve(e, c, 0, t)
                for p in range(8):
                    attend_dve(e, c, pair_units(p), 0.125, lambda t: beside(p, t))
                    if p == 3:
                        assert not todo
                        for qt in range(1, QT):
                            tile = sel_mask[qt][:, 0:(qt + 1) * P]
                            vlink(e, c, e.tensor_scalar(tile, tile, -2.0e38, NEG, ALU.is_gt, ALU.mult))
                down_dve(e, c, 1)
            return sp, pe, act, dve

        latent = [A[:, n, :] for n in range(5)]
        kr = A[:, 5, :]
        qn = [[A[:, 16, :], A[:, 17, :]], [A[:, 28, :], A[:, 29, :]]]
        kn = [[A[:, 19, :], A[:, 20, :]], [A[:, 30, :], A[:, 31, :]]]
        qr = [A[:, 18, :], A[:, 32, :]]
        vM = [A[:, n:n + 2, :].rearrange("p a b -> p (a b)").rearrange("p (t n) -> p t n", t=QT) for n in (26, 33)]
        MLA_JOBS = (("qr", 3), ("q0", 3), ("q1", 3), ("q_rot", 1), ("k0", 2), ("k1", 2), ("v0", 2), ("v1", 2))

        def mla_step_pe(e, c, p, t):
            if t == 0:
                slab_there(e, c, 2 + p % 2)
            wq = ring[:, 2 + p % 2, 0:1152].rearrange("p (k n) -> p k n", k=3)
            wk = ring[:, 2 + p % 2, 1152:2176].rearrange("p (k n) -> p k n", k=2)
            for name, k, _ in at_step(t, MLA_JOBS):
                if name == "q_rot":
                    rotate_pe(e, c, raw[0], "rot64", "qr")
                elif name[0] == "q":
                    at = {"q0": 0, "q1": P, "qr": 2 * P}[name]
                    project_part(e, c, lambda k: wq[:, k, at:at + P], latent[0:3], k, note=name)
                elif name[0] == "k":
                    at = P * int(name[1])
                    project_part(e, c, lambda k: wk[:, k, at:at + P], latent[3:5], k, note=name)
                else:
                    project_rows_part(e, c, lambda k: wk[:, k, 256:512], latent[3:5], (0, 1) if name == "v0" else (2, 3),
                                      2 * P, k, note=name)

        def mla_step_act(e, c, p, t):
            s = p % 2
            for name, _, last in at_step(t, MLA_JOBS):
                if not last:
                    continue
                if name == "q_rot":
                    skip_jobs(c)
                elif name == "qr":
                    rope_raw_act(e, c, raw[0], "raw0")
                    rope_note(c, "raw0")
                elif name[0] == "v":
                    v2 = int(name[1])
                    copy_job(e, c, vM[s][:, 2 * v2:2 * v2 + 2, :].rearrange("p t n -> p (t n)"))
                else:
                    copy_job(e, c, (qn if name[0] == "q" else kn)[s][int(name[1])])

        def mla_step_dve(e, c, p, t):
            for name, _, last in at_step(t, MLA_JOBS):
                if last and name == "q_rot":
                    rope_dve(e, c, raw[0], cos64, sin64, qr[p % 2], "qr")
                elif last:
                    job_done(c, note=name)
        kr_raw = W[:, 3, :]

        def mla_units(p):
            s = p % 2
            units = []
            for hh in range(2):
                r = slice(64 * hh, 64 * hh + 64)
                for qt in range(QT):
                    n = (qt + 1) * P
                    q = slice(qt * P, n)
                    products = [(qn[s][hh][:, q], kn[s][hh][:, 0:n], 0, n), (qr[s][r, q], kr[r, 0:n], 0, n)]
                    values = [vM[s][:, b, hh * P:(hh + 1) * P] for b in range(qt + 1)]
                    units.append(dict(parts=[part(products, n, C("chunked", lo=T - n, width=n), values)],
                                      out=outp[hh][:, q]))
            return units

        def mla():
            def sp(e, c):
                for n in range(2):
                    load(e, c, n, a["mla_down"][n], SLAB)
                    skip_jobs(c, 2)
                    job_done(c, slot=n)
                skip_jobs(c)

                for p in range(4):
                    load(e, c, 2 + p % 2, a["mla_up"][p], 2176)
                    for name, _ in MLA_JOBS:
                        job_done(c, slot=2 + p % 2 if name == "v1" else None)
                c.add("part", 4 * 2 * QT)
                down_sp(e, c, a["mla_out"], D)

            def pe(e, c):
                norm_pe(e, c)
                u0 = c.n["u"]
                c.add("u", KT)
                for n in range(2):
                    slab_there(e, c, n)
                    w = ring[:, n, :].rearrange("p (k n) -> p k n", k=KT)
                    for m in range(3):
                        project(e, c, lambda k: w[:, k, m * P:(m + 1) * P], u_tiles,
                                arriving=u0 if (n, m) == (0, 0) else None,
                                note="kr" if (n, m) == (1, 2) else None)
                        if (n, m) == (1, 0):
                            norm_pe(e, c, 3)
                rotate_pe(e, c, kr_raw, "rot64", "kr")
                norm_pe(e, c, 2)
                c.add("u", 5)
                e.wait_ge(u_ready, c["u"])

                c.add("rope")
                for t in range(STEPS):
                    mla_step_pe(e, c, 0, t)
                for p in range(4):
                    for name in ("q0", "q1", "k0", "k1"):
                        c.wait_mark(e, name)
                    c.add("rope")
                    e.wait_ge(roped, c["rope"])
                    attend_pe(e, c, mla_units(p), lambda t: p < 3 and mla_step_pe(e, c, p + 1, t), "v1")
                    c.add("head", 2)
                down_pe(e, c, mixed, lambda k: k in (0, 6, 7) and e.wait_ge(head_taken, c["head"] - min(7 - k, 2)))

            def act(e, c):
                ada_norm_act(e, c, 4)
                for n in range(4):
                    copy_job(e, c, latent[n])
                norm_act(e, c, 384)
                copy_job(e, c, latent[4])
                copy_job(e, c, kr_raw)
                norm_act(e, c, 256)
                skip_jobs(c)
                c.add("rope")

                for t in range(STEPS):
                    mla_step_act(e, c, 0, t)
                for p in range(4):
                    attend_act(e, c, mla_units(p), {3: [(outp[0][:, :], A[:, 8 + 2 * p, :])],
                                                    7: [(outp[1][:, :], A[:, 9 + 2 * p, :])]},
                               lambda t: p < 3 and mla_step_act(e, c, p + 1, t))
                down_act(e, c)

            def dve(e, c):
                ada_norm_dve(e, c, 4)
                for name, tiles in (("q_norm", latent[0:3]), ("kv_norm", latent[3:5])):
                    clear_sumsq(e, c)
                    for t in tiles:
                        job_done(c, note="latent")
                        c.wait_mark(e, "latent")
                        add_squares(e, c, t.unsqueeze(1))
                    norm_root(e, c)
                    for k, t in enumerate(tiles):
                        e.scalar_tensor_tensor(out=t, in0=t, scalar=V(name, k, 1), in1=rinv, op0=ALU.mult,
                                               op1=ALU.mult).then_inc(u_ready, 1)
                job_done(c, note="kr")
                rope_dve(e, c, kr_raw, cos64, sin64, kr, "kr")

                for t in range(STEPS):
                    mla_step_dve(e, c, 0, t)
                for p in range(4):
                    attend_dve(e, c, mla_units(p), (128 + 64) ** -0.5, lambda t: p < 3 and mla_step_dve(e, c, p + 1, t))
                down_dve(e, c, 4)
            return sp, pe, act, dve

        def renorm():
            def pe(e, c):
                c.add("sq", 2 * KT)
                e.wait_ge(squares, c["sq"])
                sum_squares(e, c, score[0], sums)
                sum_squares(e, c, score[1], scaled_sums)
                c.add("norm")
                spread_inverse(e, c, score[0])
                c.add("norm")
                spread_inverse(e, c, score[1], 48)

            def act(e, c):
                norm_act(e, c)
                c.add("norm")
                e.wait_ge(mean_ready, 1)
                e.activation(small[:, 4, 20:20 + QT], small[:, 4, 40:40 + QT], ACT.Sqrt, bias=V("eps"), scale=1.0 / D)\
                 .then_inc(root_ready, 1)

            def dve(e, c):
                inverse, square, mean, second = (small[:, 4, at:at + QT] for at in (32, 36, 40, 48))
                c.add("norm")
                e.wait_ge(root_ready, c["norm"])
                e.reciprocal(inverse, small[:, 4, 16:16 + QT]).then_inc(inverse_ready, 1)
                e.wait_ge(inverse_ready, c["norm"])
                vlink(e, c, e.tensor_tensor(square, inverse, inverse, ALU.mult))
                c.add("norm")
                e.wait_ge(sumsq_summed, c["norm"])
                e.tensor_tensor(mean, score[1][:, 0:QT], square, ALU.mult).then_inc(mean_ready, 1)
                e.wait_ge(root_ready, c["norm"])
                e.reciprocal(second, small[:, 4, 20:20 + QT]).then_inc(inverse_ready, 1)
                e.wait_ge(inverse_wide, c["norm"])
                for k in range(KT):
                    vlink(e, c, e.scalar_tensor_tensor(out=hT[:, k, :], in0=hT[:, k, :], scalar=V("final_g", k, 1),
                                                       in1=rinv, op0=ALU.mult, op1=ALU.mult))
                    e.scalar_tensor_tensor(out=uT[:, k, :], in0=hT[:, k, :], scalar=V("ln1", k, 1), in1=score[1][:, :],
                                           op0=ALU.mult, op1=ALU.mult).then_inc(u_ready, 1)
            return (lambda e, c: None), pe, act, dve

        uP = [A[:, n, :] for n in range(KT)]
        dq = [[A[:, at + n, :] for n in range(3)] for at in (8, 26)]
        dk = [[A[:, at + n, :] for n in range(3)] for at in (11, 29)]
        dv = [A[:, at:at + 3, :].rearrange("p a b -> p (a b)").rearrange("p (t n) -> p t n", t=RES) for at in (23, 32)]
        DIL_PLACE = [[(0, 0), (0, 64), (2, 64)], [(1, 64), (1, 0), (2, 0)]]
        DIL_JOBS = tuple((name, KT) for name in ("q0", "q1", "q2", "k0", "k1", "k2", "v0", "v1", "v2", "v3"))
        dbias = [A[:, 14 + 3 * n:17 + 3 * n, :].rearrange("p a b -> p (a b)")[:, 0:GN * P] for n in range(2)]
        dil_out = [A[:, 20 + n, :] for n in range(3)]
        merged = [A[:, 28 + n, :] for n in range(KT)]

        def by_residue(ap):
            return ap.rearrange("p (n r) -> p r n", r=RES)

        def dil_step_pe(e, c, p, t):
            for name, k, _ in at_step(t, DIL_JOBS):
                slot, n = "qkv".index(name[0]), int(name[1])
                if n == 0 and k == 0:
                    slab_there(e, c, slot)
                w = ring[:, slot, :].rearrange("p (k n) -> p k n", k=KT)
                if name[0] != "v":
                    if p == 0 and name == "q0":
                        e.wait_ge(u_ready, u_before_dilated + k + 1)
                    project_part(e, c, lambda k: w[:, k, n * P:(n + 1) * P], u_tiles, k, note=name)
                else:
                    if p == 0 and n == 0 and k == 0:
                        e.wait_ge(perm_ready, KT)
                    project_rows_part(e, c, lambda k: w[:, k, :], uP, (n,), 384, k, note=name)

        def dil_step_act(e, c, p, t):
            s = p % 2
            for name, _, last in at_step(t, DIL_JOBS):
                if not last:
                    continue
                n = int(name[1])
                if name[0] == "v":
                    copy_job(e, c, dv[s][:, n, :], 384)
                else:
                    o = bank_wait(e, c)
                    dst = (dq if name[0] == "q" else dk)[s][n]
                    bank_take(c, e.activation(dst.rearrange("p (r n) -> p r n", r=RES), by_residue(o[:, :]), ACT.Copy))

        def dil_step_dve(e, c, p, t):
            for _, _, last in at_step(t, DIL_JOBS):
                if last:
                    job_done(c)

        def dil_units(p):
            s = p % 2
            units = []
            for jj in range(2):
                o = slice(64 * jj, 64 * jj + 64)
                place = [(n, slice(row, row + 64)) for n, row in DIL_PLACE[jj]]
                for r in range(RES):
                    q = slice(r * P, (r + 1) * P)
                    at = 192 * jj
                    n, rows = place[0]
                    first = part([(dq[s][n][rows, q], dk[s][n][rows, :], 0, T)], T, dbias[jj][:, (3 - r) * P:(7 - r) * P],
                                 [dv[s][:, b, at:at + 64] for b in range(RES)])
                    second = part([(dq[s][n][rows, q], dk[s][n][rows, q], g * P, (g + 1) * P)
                                   for g, (n, rows) in enumerate(place[1:])],
                                  2 * P, dbias[jj][:, 7 * P:9 * P],
                                  [dv[s][:, r, at + 64:at + 128], dv[s][:, r, at + 128:at + 192]])
                    units.append(dict(parts=[first, second], out=outp[jj][o, q]))
            return units

        def dilated():
            pairs = DIL_HEADS // 2

            def sp(e, c):
                before_pairs = [c.n[f"bank{b}"] for b in range(2)]
                for p in range(pairs):
                    for n, name in enumerate(("dil_q", "dil_k", "dil_v")):
                        load(e, c, n, a[name][p], SLAB)
                    if p == 0:
                        for b in range(2):
                            e.wait_ge(lin_full[b], before_pairs[b])
                    for jj in range(2):
                        src = skew[2 * p + jj, 127:127 + P * (BIAS_W - 1)].rearrange("(p w) -> p w", w=BIAS_W - 1)
                        c.wait_mark(e, f"bias{jj}")
                        e.dma_start(dbias[jj][:, 0:8 * P].rearrange("p (t n) -> p t n", n=P),
                                    src[:, 0:8 * GW].rearrange("p (t w) -> p t w", w=GW)[:, :, 0:P])\
                         .then_inc(bias_loaded[jj], 16)
                        e.dma_start(dbias[jj][:, 8 * P:9 * P], src[:, 8 * GW:8 * GW + P]).then_inc(bias_loaded[jj], 16)
                        c.add("part", 2 * RES)
                        c.mark(f"bias{jj}", logits_ready, "part")
                    for name, _ in DIL_JOBS:
                        job_done(c, slot={"q2": 0, "k2": 1, "v3": 2}.get(name))
                branch_sp(e, c, a["branch_a"], D + 384)

            def pe(e, c):
                c.add("u", KT)
                for t in range(STEPS):
                    dil_step_pe(e, c, 0, t)
                for p in range(pairs):
                    for name in ("q1", "q2", "k1", "k2"):
                        c.wait_mark(e, name)
                    attend_pe(e, c, dil_units(p), lambda t: p < pairs - 1 and dil_step_pe(e, c, p + 1, t), "v3")
                    c.add("head", 2)
                branch_pe(e, c, dil_out, lambda: e.wait_ge(head_taken, c["head"]))

            def act(e, c):
                for t in range(STEPS):
                    dil_step_act(e, c, 0, t)
                for p in range(pairs):
                    outs = {3 + 4 * jj: [(outp[jj][64 * jj:64 * jj + 64, :].rearrange("p (r n) -> p r n", r=RES),
                                          A[64 * jj:64 * jj + 64, 20 + p, :].rearrange("p (n r) -> p r n", r=RES))]
                            for jj in range(2)}
                    attend_act(e, c, dil_units(p), outs, lambda t: p < pairs - 1 and dil_step_act(e, c, p + 1, t))
                branch_act(e, c, 0)

            def dve(e, c):
                def bias_there(t):
                    if t % RES == 0:
                        jj = t // RES
                        c.add(f"bias{jj}", 32)
                        e.wait_ge(bias_loaded[jj], c[f"bias{jj}"])

                for t in range(STEPS):
                    dil_step_dve(e, c, 0, t)
                for p in range(pairs):
                    attend_dve(e, c, dil_units(p), 0.125, lambda t: p < pairs - 1 and dil_step_dve(e, c, p + 1, t),
                               bias_there)
                branch_dve(e, c, 0)
            return sp, pe, act, dve

        def permute_pool(e):
            for k in range(KT):
                e.wait_ge(u_ready, u_before_dilated + k + 1)
                e.tensor_copy(uP[k].rearrange("p (r n) -> p r n", r=RES), by_residue(uT[:, k, :])).then_inc(perm_ready, 1)

        def branch_sp(e, c, src, width):
            def body(i):
                for j in range(2):
                    load(e, c, j, src[ds(i * 2 + j, 1)].squeeze(0), width)
                    job_done(c)
                    job_done(c, slot=j)
            c.loop(e, 0, KT // 2, body)

        def branch_pe(e, c, rhs, branch_there):
            def body(i):
                for j in range(2):
                    slab_there(e, c, j)
                    project(e, c, lambda k: ring[:, j, k * P:(k + 1) * P], u_tiles)
                    if isinstance(i, int) and j == 0:
                        branch_there()
                    project(e, c, lambda k: ring[:, j, D + k * P:D + (k + 1) * P], rhs)
            c.loop(e, 0, KT // 2, body)

        def branch_act(e, c, n):
            def body(i):
                for j in range(2):
                    o = bank_wait(e, c)
                    c.wait_mark(e, f"gate{j}")
                    bank_take(c, e.activation(W[:, 3 + j, :], o[:, :], ACT.Sigmoid, bias=Vr("b_gate", i * 2 + (j + 8 * n))))
                    job_done(c, note=f"gate{j}")
            c.marks.pop("gate0", None)
            c.marks.pop("gate1", None)
            c.loop(e, 0, KT // 2, body)

        def branch_dve(e, c, n):
            def body(i):
                for j in range(2):
                    job_done(c, note="gate")
                    c.wait_mark(e, "gate")
                    o = bank_wait(e, c)
                    dst = A[:, ds(i * 2 + (28 + j), 1), :]
                    if n == 0:
                        bank_take(c, e.tensor_tensor(dst, o[:, :].unsqueeze(1), W[:, 3 + j:4 + j, :], ALU.mult))
                    else:
                        bank_take(c, e.tensor_tensor(W[:, 5 + j, :], o[:, :], W[:, 3 + j, :], ALU.mult), note="y")
                        c.wait_mark(e, "y")
                        e.tensor_tensor(dst, dst, W[:, 5 + j:6 + j, :], ALU.add).then_inc(merged_ready, 1)
            c.loop(e, 0, KT // 2, body)

        flatW = W[:, :, :].rearrange("p a b -> p (a b)")
        padded = [flatW[:, 1024 * n:1024 * n + 16 + T] for n in range(4)]
        pooled = [A[:, n, :] for n in range(KT)]
        pool_y = [A[:, 8 + n, :] for n in range(KT)]

        def pooling():
            def sp(e, c):
                for n in range(3):
                    load(e, c, n, a["pool_in"][n], SLAB)
                load(e, c, 3, a["pool_w"], 2048)
                for n in range(8):
                    job_done(c, slot=n // 3)
                for n in range(8):
                    job_done(c, slot=3)
                branch_sp(e, c, a["branch_b"], 2 * D)

            def pe(e, c):
                for n in range(8):
                    if n % 3 == 0:
                        slab_there(e, c, n // 3)
                    w = ring[:, n // 3, :].rearrange("p (k n) -> p k n", k=KT)
                    project(e, c, lambda k: w[:, k, (n % 3) * P:(n % 3 + 1) * P], u_tiles)
                slab_there(e, c, 3)
                w = ring[:, 3, 0:2048].rearrange("p (g k n) -> p g k n", g=4, k=2)
                for n in range(8):
                    if n % 2 == 0:
                        e.wait_ge(gated, c["gated"] + n + 2)
                    g = n // 2
                    project(e, c, lambda k: w[:, g, k, (n % 2) * P:(n % 2 + 1) * P], pooled[2 * g:2 * g + 2])
                c.add("gated", 8)
                taken = [(lin_taken[b], c.n[f"bank{b}"]) for b in range(2)]
                branch_pe(e, c, pool_y, lambda: [e.wait_ge(*t) for t in taken])

            def act(e, c):
                for n in range(8):
                    o = bank_wait(e, c)
                    if n < 2:
                        e.wait_ge(zeros_ready, 1)
                    after(e, gated, c["gated"] + n - 1 if n >= 2 else 0)
                    bank_take(c, e.activation(padded[n % 2][:, 16:16 + T], o[:, :], ACT.Copy))
                c.add("gated", 8)
                for n in range(8):
                    o = bank_wait(e, c)
                    bank_take(c, e.activation(pool_y[n], o[:, :], ACT.Copy, scale=V("pool_scale", n, 1)))
                branch_act(e, c, 1)

            def dve(e, c):
                for n in range(3):
                    vlink(e, c, e.memset(padded[n][:, 0:16], 0.0))
                e.memset(padded[3][:, 0:16], 0.0).then_inc(zeros_ready, 1)
                e.wait_ge(zeros_ready, 1)
                for n in range(8):
                    job_done(c, note="x")
                    c.wait_mark(e, "x")
                    x = cur = padded[n % 2]
                    step = 1
                    for k in range(n // 2 + 1):
                        nxt = padded[2 + k % 2]
                        vlink(e, c, e.tensor_tensor(nxt[:, 16:16 + T], cur[:, 16:16 + T],
                                                    cur[:, 16 - step:16 - step + T], ALU.add))
                        cur, step = nxt, 2 * step
                    vlink(e, c, e.scalar_tensor_tensor(out=pooled[n], in0=cur[:, 16:16 + T], scalar=1.0 / step,
                                                       in1=x[:, 16:16 + T], op0=ALU.mult, op1=ALU.subtract))
                    vlink(e, c, e.tensor_tensor(stat16, cur[:, 16:32], C("poolfix", P, 16 * (n // 2), 16), ALU.mult))
                    e.tensor_tensor(pooled[n][:, 0:16], stat16, x[:, 16:32], ALU.subtract).then_inc(gated, 1)
                    c.add("gated")
                skip_jobs(c, 8)
                branch_dve(e, c, 1)
            return sp, pe, act, dve

        stat16 = small[:, 11, 0:16]

        xs = [A[:, n, :] for n in range(KT)]
        bT, cT = [A[:, 8, :], A[:, 9, :]], [A[:, 10, :], A[:, 11, :]]
        bN = [A[:, 12 + g, :] for g in range(2)]
        z_silu = [W[:, 9, :], A[:, 12, :]]
        group_sums = [A[:, 8:10, :], A[:, 10:14:3, :]]
        xdt = [A[:, 14 + 2 * n:16 + 2 * n, :].rearrange("p a b -> p (a b)") for n in range(QT)]
        state = [[A[:, 22 + 2 * n + g, :] for g in range(2)] for n in range(3)]
        acsT = W[0:16, 0, :]
        cb = [W[:, 1 + g, :] for g in range(2)]
        xdec = [W[:, 3 + 2 * n:5 + 2 * n, :].rearrange("p a b -> p (a b)") for n in range(2)]
        m_dt, m_nacs, m_dec, m_tot = small[:, 5, :], small[:, 6, :], small[:, 7, :], small[:, 8, :]
        m_a, m_expA = small[:, 9, :], small[:, 10, 0:16]

        def by_chunk(ap):
            return ap.rearrange("p (t n) -> p t n", t=QT)

        def head_wide(col, first, n):
            return col[:, first:first + n].unsqueeze(2).to_broadcast([P, n, 64])

        def ssd():
            def sp(e, c):
                for n in range(4):
                    load(e, c, n, a["xbc"][n], SLAB)
                for n in range(12):
                    job_done(c, slot=n // 3)
                load(e, c, 0, a["dt"], KT * 16)
                job_done(c, slot=0)
                skip_jobs(c, 2 + 8 + 2 + 2 + 6)
                for n in range(3):
                    load(e, c, 1 + n, a["z"][n], SLAB)
                for j in range(8):
                    skip_jobs(c, 3)
                    job_done(c, slot=1 + j // 3)
                branch_sp(e, c, a["branch_c"], 2 * D)

            def y_pe(e, c, j):
                g = j // 4
                c.add("ssdM", 2)
                e.wait_ge(ssd_dve, c["ssdM"])
                after(e, ssd_ready, j)
                for hh in range(2):
                    h = 2 * j + hh
                    M = W[:, 3 + 2 * (j % 2) + hh, :]
                    for k in range(QT):
                        e.matmul(outp[0][64 * hh:64 * hh + 64, k * P:(k + 1) * P], xdt[k][:, h * 64:(h + 1) * 64],
                                 M[:, k * P:(k + 1) * P], start=True, stop=True)
                for k in range(1, QT):
                    last = e.matmul(outp[1][:, k * P:(k + 1) * P], state[k - 1][g][:, (j % 4) * P:(j % 4 + 1) * P],
                                    cT[g][:, k * P:(k + 1) * P], start=True, stop=True)
                last.then_inc(ssd_pe, 1)

            def pe(e, c):
                for n in range(12):
                    if n % 3 == 0:
                        slab_there(e, c, n // 3)
                    w = ring[:, n // 3, :].rearrange("p (k n) -> p k n", k=KT)
                    project(e, c, lambda k: w[:, k, (n % 3) * P:(n % 3 + 1) * P], u_tiles)
                slab_there(e, c, 0)
                w = ring[:, 0, 0:KT * 16].rearrange("p (k n) -> p k n", k=KT)
                project_rows(e, c, lambda k: w[:, k, :], u_tiles, range(QT), 16)
                e.wait_ge(dt_ready, 1)
                o = bank_open(e, c)
                e.matmul(o[:, 0:64], C("triu"), m_a, start=True, stop=True)
                bank_close(c, e.matmul(o[:, 64:128], C("ones"), m_a, start=True, stop=True))
                o = bank_open(e, c)
                for k in range(QT):
                    last = e.matmul(o[0:16, k * P:(k + 1) * P], by_chunk(m_a)[:, k, :], C("triu"), start=True, stop=True)
                bank_close(c, last)
                c.add("silu", 12)
                e.wait_ge(silu_done, c["silu"])
                for k in range(QT):
                    for half in range(2):
                        o = bank_open(e, c)
                        for n in range(4):
                            last = e.matmul(o[:, n * P:(n + 1) * P], xs[4 * half + n][:, k * P:(k + 1) * P], C("ident"),
                                            start=True, stop=True)
                        bank_close(c, last)
                for g in range(2):
                    o = bank_open(e, c)
                    for k in range(QT):
                        last = e.matmul(o[:, k * P:(k + 1) * P], bT[g][:, k * P:(k + 1) * P], C("ident"),
                                        start=True, stop=True)
                    bank_close(c, last)
                for g in range(2):
                    o = bank_open(e, c)
                    for k in range(QT):
                        last = e.matmul(o[:, k * P:(k + 1) * P], bT[g][:, k * P:(k + 1) * P],
                                        cT[g][:, k * P:(k + 1) * P], start=True, stop=True)
                    bank_close(c, last)
                for k in range(3):
                    e.wait_ge(ssd_dve, k + 1)
                    for g in range(2):
                        o = bank_open(e, c)
                        bank_close(c, e.matmul(o[:, :], bN[g][:, k * P:(k + 1) * P], xdec[k % 2][:, g * T:(g + 1) * T],
                                               start=True, stop=True))
                c.add("ssdM", 3)
                e.wait_ge(sel_loaded, 16)
                for j in range(8):
                    for hh in range(2):
                        o = bank_open(e, c)
                        bank_close(c, e.matmul(o[:, :], C("sel", 16, (2 * j + hh) * P, P), acsT, start=True, stop=True))
                    if j > 0:
                        y_pe(e, c, j - 1)
                    o = bank_open(e, c)
                    bank_close(c, e.matmul(o[:, :], C("selpair", 16, j * P, P), acsT, start=True, stop=True))
                    if j % 3 == 0:
                        slab_there(e, c, 1 + j // 3)
                    w = ring[:, 1 + j // 3, :].rearrange("p (k n) -> p k n", k=KT)
                    project(e, c, lambda k: w[:, k, (j % 3) * P:(j % 3 + 1) * P], u_tiles)
                    if j == 5:
                        norm_pe(e, c, 4, group_sums[0])
                y_pe(e, c, 7)
                c.add("sq", 4)
                c.add("norm")
                c.add("u", 8)

                def normed():
                    counted_norm_pe(e, c, group_sums[1])
                    e.wait_ge(u_ready, c["u"])
                branch_pe(e, c, xs, normed)

            def act(e, c):
                for n in range(12):
                    o = bank_wait(e, c)
                    e.activation(W[:, 3 + n % 2, :], o[:, :], ACT.Identity, bias=V("conv_b", n, 1),
                                 scale=V("conv_w", 36 + n, 1)).then_inc(tap_done, 1)
                    job_done(c, note="conv")
                    c.wait_mark(e, "conv")
                    e.activation(A[:, n, :], W[:, 3 + n % 2, :], ACT.Silu).then_inc(silu_done, 1)
                c.add("tap", 12)
                c.add("silu", 12)
                job_done(c)
                softplus_act(e, c)
                e.activation(m_expA, V("a_log"), ACT.Exp).then_inc(ssd_exp, 1)
                skip_jobs(c)
                copy_job(e, c, acsT, T, 16)
                e.wait_ge(forget_ready, 4)
                e.activation(m_dec, m_dec, ACT.Exp).then_inc(ssd_exp, 1)
                e.activation(m_tot, m_tot, ACT.Exp).then_inc(ssd_exp, 1)
                skip_jobs(c, 8)
                for g in range(2):
                    copy_job(e, c, bN[g])
                for g in range(2):
                    copy_job(e, c, cb[g])
                skip_jobs(c, 6)
                for j in range(8):
                    for hh in range(2):
                        h = 2 * j + hh
                        R = W[:, 3 + 2 * (j % 2) + hh, :]
                        job_done(c, note="decay")
                        c.wait_mark(e, "decay")
                        for k in range(QT):
                            ins = e.activation(R[:, k * P:(k + 1) * P], R[:, k * P:(k + 1) * P], ACT.Exp,
                                               bias=by_chunk(m_nacs)[:, k, h:h + 1])
                        ins.then_inc(ssd_exp, 1)
                    o = bank_wait(e, c)
                    after(e, ssd_ready, j - 1)
                    bank_take(c, e.activation(W[:, 7 + j % 2, :], o[:, :], ACT.Exp))
                    o = bank_wait(e, c)
                    after(e, ssd_ready, j - 1)
                    bank_take(c, e.activation(z_silu[j % 2], o[:, :], ACT.Silu))
                    if j == 5:
                        norm_act(e, c, 512)
                norm_act(e, c, 512)
                branch_act(e, c, 2)

            def dve(e, c):
                for n in range(12):
                    o = bank_wait(e, c)
                    e.wait_ge(tap_done, n + 1)
                    buf = W[:, 3 + n % 2, :]
                    for d in (1, 2, 3):
                        ins = e.scalar_tensor_tensor(out=buf[:, d:T], in0=o[:, 0:T - d],
                                                     scalar=V("conv_w", 12 * (3 - d) + n, 1), in1=buf[:, d:T],
                                                     op0=ALU.mult, op1=ALU.add)
                        if d < 3:
                            vlink(e, c, ins)
                    bank_take(c, ins)
                o = bank_wait(e, c)
                bank_take(c, e.tensor_tensor(by_chunk(small[:, 0, :]), by_chunk(o[:, 0:64]),
                                             V("dt_bias").unsqueeze(1).to_broadcast([P, QT, 16]), ALU.add), note="dt")
                c.wait_mark(e, "dt")
                softplus_dve_in(e, c)
                vlink(e, c, e.scalar_tensor_tensor(out=m_dt, in0=small[:, 0, :], scalar=0.0, in1=small[:, 2, :],
                                                   op0=ALU.max, op1=ALU.add))
                e.wait_ge(ssd_exp, 1)
                e.scalar_tensor_tensor(out=by_chunk(m_a), in0=by_chunk(m_dt), scalar=-1.0,
                                       in1=m_expA.unsqueeze(1).to_broadcast([P, QT, 16]), op0=ALU.mult,
                                       op1=ALU.mult).then_inc(dt_ready, 1)
                o = bank_wait(e, c)
                vlink(e, c, e.tensor_scalar(m_nacs, o[:, 0:64], -1.0, None, ALU.mult))
                vlink(e, c, e.tensor_copy(m_tot, o[:, 64:128]))
                bank_take(c, e.tensor_tensor(m_dec, m_nacs, o[:, 64:128], ALU.add), note="dec")
                c.wait_mark(e, "dec")
                e.tensor_copy(small[:, 11, 16:17], m_dec[:, 0:1]).then_inc(forget_ready, 1)
                skip_jobs(c)
                for k in range(QT):
                    for half in range(2):
                        o = bank_wait(e, c)
                        bank_take(c, e.tensor_tensor(
                            xdt[k][:, half * T:(half + 1) * T].rearrange("p (h d) -> p h d", d=64),
                            o[:, :].rearrange("p (h d) -> p h d", d=64),
                            head_wide(by_chunk(m_dt)[:, k, :], 8 * half, 8), ALU.mult))
                all_x = {b: c.n[f"bank{b}"] for b in range(2)}
                skip_jobs(c, 4)
                e.wait_ge(ssd_exp, 3)
                for b in range(2):
                    e.wait_ge(lin_taken[b], all_x[b])

                def decayed(k):
                    e.tensor_tensor(xdec[k % 2].rearrange("p (h d) -> p h d", d=64),
                                    xdt[k].rearrange("p (h d) -> p h d", d=64),
                                    head_wide(by_chunk(m_dec)[:, k, :], 0, 16), ALU.mult).then_inc(ssd_dve, 1)
                decayed(0)
                decayed(1)
                for k in range(3):
                    for g in range(2):
                        dst = state[k][g]
                        if k:
                            vlink(e, c, e.tensor_tensor(dst.rearrange("p (h d) -> p h d", d=64),
                                                        state[k - 1][g].rearrange("p (h d) -> p h d", d=64),
                                                        head_wide(by_chunk(m_tot)[:, k, :], 8 * g, 8), ALU.mult))
                        o = bank_wait(e, c)
                        if k:
                            bank_take(c, e.tensor_tensor(dst, dst, o[:, :], ALU.add), note="state")
                        else:
                            bank_take(c, e.tensor_copy(dst, o[:, :]), note="state")
                        c.wait_mark(e, "state")
                    if k == 0:
                        decayed(2)
                for j in range(8):
                    g = j // 4
                    for hh in range(2):
                        o = bank_wait(e, c)
                        R = W[:, 3 + 2 * (j % 2) + hh, :]
                        after(e, ssd_pe, j - 1)
                        bank_take(c, e.tensor_tensor(by_chunk(R), by_chunk(o[:, :]),
                                                     C("below").unsqueeze(1).to_broadcast([P, QT, P]), ALU.add))
                    skip_jobs(c, 2)
                    if j > 0:
                        y_dve(e, c, j - 1)
                    for hh in range(2):
                        R = W[:, 3 + 2 * (j % 2) + hh, :]
                        e.wait_ge(ssd_exp, 3 + 2 * j + hh + 1)
                        e.tensor_tensor(R, R, cb[g], ALU.mult).then_inc(ssd_dve, 1)
                    if j == 5:
                        group_norm_dve(e, c, 0)
                y_dve(e, c, 7)
                group_norm_dve(e, c, 1)
                branch_dve(e, c, 2)

            def group_norm_dve(e, c, g):
                norm_root(e, c)
                for n in range(4 * g, 4 * g + 4):
                    e.scalar_tensor_tensor(out=xs[n], in0=xs[n], scalar=V("ssd_norm", n, 1), in1=rinv,
                                           op0=ALU.mult, op1=ALU.mult).then_inc(u_ready, 1)

            def y_dve(e, c, j):
                g = j // 4
                e.wait_ge(ssd_pe, j + 1)
                E = W[:, 7 + j % 2, :]
                vlink(e, c, e.scalar_tensor_tensor(out=xs[j], in0=xs[j], scalar=V("ssd_d", j, 1), in1=outp[0][:, :],
                                                   op0=ALU.mult, op1=ALU.add))
                for b in range(2):
                    e.wait_ge(lin_taken[b], c.n[f"bank{b}"] - (2 if j < 7 else 0))
                vlink(e, c, e.tensor_tensor(E[:, P:T], outp[1][:, P:T], E[:, P:T], ALU.mult))
                vlink(e, c, e.tensor_tensor(xs[j][:, P:T], xs[j][:, P:T], E[:, P:T], ALU.add))
                e.tensor_tensor(xs[j], xs[j], z_silu[j % 2], ALU.mult).then_inc(ssd_ready, 1)
                e.wait_ge(ssd_ready, j + 1)
                if j % 4 == 0:
                    clear_sumsq(e, c, group_sums[g])
                add_squares(e, c, A[:, j:j + 1, :], group_sums[g])
            return sp, pe, act, dve

        def output_projection():
            def pe(e, c):
                down_pe(e, c, merged, lambda k: e.wait_ge(merged_ready, KT + k + 1))
            return (lambda e, c: down_sp(e, c, a["w_o"], D), pe, lambda e, c: down_act(e, c),
                    lambda e, c: down_dve(e, c, None))

        def conv_ffn():
            def sp(e, c):
                up_sp(e, c, a["up2"])
                down_sp(e, c, a["down2"], FF)

            def pe(e, c):
                norm_pe(e, c)
                up_pe(e, c)
                c.add("gated", FT)
                down_pe(e, c, hidden, lambda k: e.wait_ge(gated, c["gated"] - FT + k + 1))

            def act(e, c):
                def body(i):
                    for j in range(2):
                        for g in range(2):
                            o = bank_wait(e, c)
                            after(e, gated, c["gated"] - 1)
                            e.activation(W[:, 3 + 2 * j + g, :], o[:, :], ACT.Identity,
                                         bias=Vr("ffn_cb", i * 2 + (j + FT * g)),
                                         scale=Vr("ffn_cw", i * 2 + (j + FT * g + 4 * FT))).then_inc(tap_done, 1)
                            job_done(c, note=f"conv{g}")
                        c.wait_mark(e, "conv0")
                        e.activation(W[:, 7 + j, :], W[:, 3 + 2 * j, :], ACT.Silu).then_inc(silu_done, 1)
                        c.add("gated")
                norm_act(e, c)
                c.loop(e, 0, FT // 2, body)
                down_act(e, c)

            def dve(e, c):
                plain_norm_dve(e, c, "ln2")
                c.add("tap", 12)
                c.add("silu", 12)

                def body(i):
                    for j in range(2):
                        for g in range(2):
                            o = bank_wait(e, c)
                            c.add("tap")
                            e.wait_ge(tap_done, c["tap"])
                            buf = W[:, 3 + 2 * j + g, :]
                            for d in (1, 2):
                                ins = e.scalar_tensor_tensor(out=buf[:, d:T], in0=o[:, 0:T - d],
                                                             scalar=Vr("ffn_cw", i * 2 + (j + FT * g + 2 * FT * (2 - d))),
                                                             in1=buf[:, d:T], op0=ALU.mult, op1=ALU.add)
                                if d == 1:
                                    vlink(e, c, ins)
                            bank_take(c, ins, note="conv")
                        c.wait_mark(e, "conv")
                        c.add("silu")
                        e.wait_ge(silu_done, c["silu"])
                        e.tensor_tensor(A[:, ds(i * 2 + j, 1), :], W[:, 4 + 2 * j:5 + 2 * j, :], W[:, 7 + j:8 + j, :],
                                        ALU.mult).then_inc(gated, 1)
                        c.add("gated")
                c.loop(e, 0, FT // 2, body)
                down_dve(e, c, None)
            return sp, pe, act, dve

        def last_norm():
            def sp(e, c):
                for k in range(KT):
                    e.wait_ge(result_ready, k + 1)
                    e.dma_start(out[k], A[:, k, :]).then_inc(result_stored, 16)
                e.wait_ge(result_stored, 16 * KT)

            def dve(e, c):
                norm_root(e, c)
                for k in range(KT):
                    e.scalar_tensor_tensor(out=A[:, k, :], in0=hT[:, k, :], scalar=V("final2", k, 1), in1=rinv,
                                           op0=ALU.mult, op1=ALU.mult).then_inc(result_ready, 1)
            return sp, norm_pe, norm_act, dve

        stages = [
            (prologue_sp, prologue_pe, prologue_act, prologue_dve),
            ffn(0, 0, ((0, 1), (0, 2))), hybrid(), ffn(2, 1, ((1, 0),)),
            ffn(3, 2, ((1, 1), (1, 2))), mla(), ffn(5, 3, ()),
            renorm(), dilated(), pooling(), ssd(), output_projection(), conv_ffn(), last_norm(),
        ]
        u_before_dilated = 6 * KT + 5

        block = ctx.enter_context(nc.Block())

        @block.sync
        def _(sp):
            c = Counts()
            for run, _, _, _ in stages:
                run(sp, c)

        @block.tensor
        def _(pe):
            c = Counts()
            for _, run, _, _ in stages:
                run(pe, c)

        @block.scalar
        def _(act):
            c = Counts()
            for _, _, run, _ in stages:
                run(act, c)

        @block.vector
        def _(dve):
            c = Counts()
            for _, _, _, run in stages:
                run(dve, c)

        @block.gpsimd
        def _(pool):
            permute_pool(pool)


def _bucket(dist):
    dist = np.asarray(dist)
    f = np.float32
    nf = np.maximum(dist, 1).astype(f)
    large = 16 + (np.log(nf / f(16)) / f(math.log(2048 / 16)) * f(16)).astype(np.int32)
    return np.where(dist < 16, dist, np.minimum(large, 31))


def _inv_freq(rot, theta):
    x = np.float32(-math.log(theta) * 2.0) * np.arange(rot // 2, dtype=np.float32) / np.float32(rot)
    return np.exp(x.astype(np.float64)).astype(np.float32)


def _rotation(rot, period=64):
    m = np.zeros((P, P), np.float32)
    for base in range(0, P, period):
        for j in range(rot // 2):
            m[base + j + rot // 2, base + j] = -1.0
            m[base + j, base + j + rot // 2] = 1.0
    return m


def _inv_freq_column(rot, theta):
    col = np.zeros((P, 1), np.float32)
    for base in (0, 64):
        col[base:base + rot // 2, 0] = _inv_freq(rot, theta)
        col[base + rot // 2:base + rot, 0] = _inv_freq(rot, theta)
    return col


def shape_constants():
    c = np.zeros((P, CONST_W), np.float32)

    def put(name, value):
        at, w = CONST[name]
        value = np.asarray(value, np.float32)
        c[:value.shape[0], at:at + w] = value
    i, j = np.arange(P)[:, None], np.arange(P)[None, :]
    put("ident", np.eye(P))
    put("ones", np.ones((P, P)))
    put("triu", i <= j)
    put("causal", np.concatenate([np.zeros((P, T - P)), np.where(j > i, NEG, 0)], 1))
    put("chunked", np.concatenate([np.zeros((P, T - P)), np.where(j // 64 > i // 64, NEG, 0)], 1))
    put("below", np.where(j < i, NEG, 0))
    put("rot16", _rotation(16))
    put("rot64", _rotation(64))
    fix = np.concatenate([1.0 / np.minimum(np.arange(16) + 1, w) for w in (2, 4, 8, 16)])
    put("poolfix", np.tile(fix, (P, 1)))
    sel = np.zeros((16, SSD_HEADS, P))
    pair = np.zeros((16, SSD_HEADS // 2, P))
    for h in range(SSD_HEADS):
        sel[h, h] = 1
        pair[h, h // 2, 64 * (h % 2):64 * (h % 2) + 64] = 1
    put("sel", sel.reshape(16, -1))
    put("selpair", pair.reshape(16, -1))
    put("foxrow", np.concatenate([8 * np.eye(8, 16), np.zeros((8, 16))], 0))
    put("foxone", np.concatenate([np.zeros((8, 16)), -np.eye(8, 16)], 0))
    key = np.zeros((16, 2))
    key[8:, 0] = 8
    key[:8, 1] = 1
    put("foxkey", key)
    return c


def distance_onehots():
    m = np.arange(GW) - (P - 1)
    out = np.zeros((33, GN, GW), np.float32)
    for t in range(GN):
        if t < 7:
            dist = -RES * m + (3 - t)
            ok = (dist >= 0) & (dist <= 128)
        else:
            dist = -RES * m
            ok = (dist >= 0) & ((m % 4 == 0) | (t == 7))
        b = np.where(ok, _bucket(np.maximum(dist, 0)), 32)
        out[b, t, np.arange(GW)] = 1
    return out.reshape(33, BIAS_W)


def tiles(w):
    k, m = w.shape
    return w.reshape(k // P, P, m // P, P).transpose(2, 1, 0, 3).reshape(m // P, P, k)


def slab(w):
    k, m = w.shape
    return w.reshape(k // P, P, m).transpose(1, 0, 2).reshape(P, k // P * m)


def slabs3(w):
    out = []
    for at in range(0, w.shape[1], 384):
        piece = w[:, at:at + 384]
        if piece.shape[1] < 384:
            piece = np.concatenate([piece, w[:, :384 - piece.shape[1]]], 1)
        out.append(slab(piece))
    return np.stack(out)


def columns(v):
    return v.reshape(-1, P).T


def layout(x):
    w_in, w2 = x["hyb_w_in"][0], x["w_in_2"][0]
    fq, fk, fv, ff, dq, dk, dv, iq, iw, ik = np.split(w_in, np.cumsum([512, 512, 512, 8, 512, 512, 512, 256, 4]), 1)
    q2, k2, v2, pool_in, z, xbc, dt, gates = np.split(w2, np.cumsum([1152, 1152, 1152, 1024, 1024, 1536, 16]), 1)

    def pairs(q, k, v):
        return np.concatenate([tiles(q), tiles(k), tiles(v)], 2)

    def up_gate(g, u):
        return np.concatenate([tiles(g), tiles(u)], 2)

    uq = x["mla_w_uq"][0].reshape(384, 8, 192)
    ukv = x["mla_w_ukv"][0].reshape(256, 8, 256)
    mla_up = []
    for i in range(4):
        h = (2 * i, 2 * i + 1)
        wq = np.concatenate([uq[:, h[0], :128], uq[:, h[1], :128], uq[:, h[0], 128:], uq[:, h[1], 128:]], 1)
        wk = np.concatenate([ukv[:, h[0], :128], ukv[:, h[1], :128], ukv[:, h[0], 128:], ukv[:, h[1], 128:]], 1)
        mla_up.append(np.concatenate([slab(wq), slab(wk)], 1))
    md = x["mla_w_down"][0]
    q3, k3, v3 = (w.reshape(D, 3, DIL_HEADS, HD) for w in (q2, k2, v2))

    def dil_tiles(w):
        order = [(0, 0), (1, 0), (1, 1), (0, 1), (2, 1), (2, 0)]
        return np.stack([slab(np.concatenate([w[:, g, 2 * p + jj] for g, jj in order], 1)) for p in range(3)])
    g3 = [gates[:, n * D:(n + 1) * D] for n in range(3)]
    rel = np.zeros((P, 18), np.float32)
    rel[:32] = x["rel_bias_2"]
    vec = [columns(x["c"]), columns(x["ada_b"]), columns(x["norm_g"]), columns(x["final_g"]), columns(x["ln1_g_2"]),
           columns(x["ln2_g_2"]), columns(x["final_g_2"]), columns(x["mla_q_norm"]), columns(x["mla_kv_norm"]),
           columns(x["b_gate_2"]), columns(x["pool_scale_2"]), columns(x["ssd_conv_w_2"]),
           columns(x["ssd_conv_b_2"]), columns(x["ssd_norm_w_2"]), columns(np.repeat(x["ssd_d_2"][0], HD)),
           columns(x["ffn_conv_w_2"]), columns(x["ffn_conv_b_2"]), np.tile(x["ssd_dt_bias_2"], (P, 1)),
           np.tile(x["ssd_a_log_2"], (P, 1)), np.tile(x["fox_b_f"], (P, 2)), rel, _inv_freq_column(16, 500000.0),
           _inv_freq_column(64, 10000.0), np.full((P, 1), EPS, np.float32)]
    gate_w, up_w, down_w = (x[f"ffn_w_{n}"].reshape(4, *x[f"ffn_w_{n}"].shape[2:]) for n in ("gate", "up", "down"))
    return {
        "constants": shape_constants(),
        "onehot": distance_onehots(),
        "vectors": np.concatenate(vec, 1),
        "positions": x["positions"],
        "xT": x["x"][0].T.reshape(KT, P, T).transpose(1, 0, 2),
        "ada": x["ada_w"].reshape(2, KT, P, 3, 8, 384).transpose(0, 3, 4, 2, 1, 5).reshape(2, 3, 8, P, SLAB),
        "up": np.stack([up_gate(gate_w[n], up_w[n]) for n in range(4)]),
        "down": np.stack([tiles(down_w[n]) for n in range(4)]),
        "idx": slab(np.concatenate([iq, ik, ik], 1)),
        "idx_small": slab(np.concatenate([ff, ff, iw], 1)),
        "fox": pairs(fq, fk, fv),
        "dsa": pairs(dq, dk, dv),
        "hyb_out": tiles(x["hyb_w_out"][0]),
        "mla_down": np.stack([slab(md[:, :384]), slab(np.concatenate([md[:, 384:704], md[:, 640:704]], 1))]),
        "mla_up": np.stack(mla_up),
        "mla_out": tiles(x["mla_w_out"][0]),
        "dil_q": dil_tiles(q3),
        "dil_k": dil_tiles(k3),
        "dil_v": np.stack([slab(v3[:, :, 2 * p:2 * p + 2].transpose(0, 2, 1, 3).reshape(D, 384)) for p in range(3)]),
        "branch_a": up_gate(g3[0], x["w_a_2"][0]),
        "branch_b": up_gate(g3[1], x["w_b_2"][0]),
        "branch_c": up_gate(g3[2], x["w_c_2"][0]),
        "pool_in": slabs3(pool_in),
        "pool_w": np.concatenate([slab(x["pool_w_2"][0, g]) for g in range(4)], 1),
        "xbc": slabs3(xbc),
        "dt": slab(dt),
        "z": slabs3(z),
        "w_o": tiles(x["w_o_2"][0]),
        "up2": up_gate(x["ffn_w_up_2"][0][:, :FF], x["ffn_w_up_2"][0][:, FF:]),
        "down2": tiles(x["ffn_w_down_2"][0]),
    }


def kernel(**inputs):
    import concourse.bacc as _bacc
    from concourse.bass_utils import run_bass_kernel_spmd as _run

    nc = _bacc.Bacc("TRN2", target_bir_lowering=False, num_devices=1)
    arrays, aps = {}, {}
    for name, value in layout({k: np.asarray(v) for k, v in inputs.items()}).items():
        value = np.ascontiguousarray(value)
        arrays[f"in_{name}"] = value
        aps[name] = nc.dram_tensor(f"in_{name}", value.shape, mybir.dt.from_np(value.dtype), kind="ExternalInput").ap()
    out = nc.dram_tensor("out_T", [KT, P, T], F32, kind="ExternalOutput").ap()
    build_program(nc, aps, out)
    r = _run(nc, [arrays], core_ids=[0])
    return np.ascontiguousarray(r.results[0]["out_T"].reshape(D, T).T).reshape(1, T, D)
```
